# Optimizing a Trainium2 kernel written in Bass

```python
import jax, jax.numpy as jnp
from jax import lax
import numpy as np

D_MODEL = 1024
BATCH = 1
SEQ = 512
DEPTH = 2
DEC_BATCH = 8
DEC_SEQ = 1
PAST_LEN = 4096
PAGE_SIZE = 128

GLA_HEADS = 4
GLA_DK = 64
GLA_DV = 128
GLA_GATE_RANK = 16
GLA_TAU = 16.0
GLA_CHUNK = 64
SB_HEADS = 8
SB_HEAD_DIM = 64
SB_QBLOCK = 128
SB_BIAS_INIT = -8.0
N_MEM = 256
MEM_HEADS = 4
MEM_HEAD_DIM = 128
D_FF = 2816
FFN_CONV = 3
EPS = 1e-6

GLA_QK = GLA_HEADS * GLA_DK
GLA_VW = GLA_HEADS * GLA_DV
SB_W = SB_HEADS * SB_HEAD_DIM
MEM_WIDTH = MEM_HEADS * MEM_HEAD_DIM
TOKEN_WIDTH = 512
MIX_WIDTH = TOKEN_WIDTH + MEM_WIDTH
GLA_IN = 2 * GLA_QK + 2 * GLA_VW + GLA_GATE_RANK + MEM_WIDTH
SB_IN = 3 * SB_W + MEM_WIDTH
N_GLA_LAYERS = (DEPTH + 1) // 2
N_SB_LAYERS = DEPTH // 2

kernel_name = 'hybrid_gla_stickbreak_memxattn_convffn_step'

def rmsnorm(x, g):
    xf = x.astype(jnp.float32)
    y = xf * lax.rsqrt(jnp.mean(xf * xf, axis=-1, keepdims=True) + EPS)
    return (y * g.astype(jnp.float32)).astype(x.dtype)

def gla_chunked(q, k, v, log_a):
    B, L, H, DK = q.shape
    DV = v.shape[-1]
    C = GLA_CHUNK
    N = L // C
    def blk(t):
        return t.astype(jnp.float32).reshape(B, N, C, H, t.shape[-1]).transpose(1, 0, 3, 2, 4)
    qc, kc, vc, ac = blk(q), blk(k), blk(v), blk(log_a)
    b = jnp.cumsum(ac, axis=3)
    b_last = b[:, :, :, -1, :]
    q_dec = qc * jnp.exp(b)
    k_dec = kc * jnp.exp(-b)
    k_to_end = kc * jnp.exp(b_last[:, :, :, None, :] - b)
    causal = jnp.tril(jnp.ones((C, C), dtype=bool))
    att = jnp.where(causal, jnp.einsum('nbhck,nbhsk->nbhcs', q_dec, k_dec), 0.0)
    o_intra = jnp.einsum('nbhcs,nbhsv->nbhcv', att, vc)
    def step(S, inp):
        qd, kt, vv, bl = inp
        o_inter = jnp.einsum('bhck,bhkv->bhcv', qd, S)
        S = jnp.exp(bl)[..., None] * S + jnp.einsum('bhck,bhcv->bhkv', kt, vv)
        return S, o_inter
    S0 = jnp.zeros((B, H, DK, DV), jnp.float32)
    S_fin, o_inter = lax.scan(step, S0, (q_dec, k_to_end, vc, b_last))
    o = (o_intra + o_inter).transpose(1, 0, 3, 2, 4).reshape(B, L, H, DV)
    return o, S_fin

def gla_recurrent(q, k, v, log_a, S0):
    def step(S, inp):
        qt, kt, vt, at = inp
        S = jnp.exp(at)[..., None] * S + kt[..., :, None] * vt[..., None, :]
        return S, jnp.einsum('bhk,bhkv->bhv', qt, S)
    xs = tuple(t.astype(jnp.float32).transpose(1, 0, 2, 3) for t in (q, k, v, log_a))
    S, o = lax.scan(step, S0.astype(jnp.float32), xs)
    return o.transpose(1, 0, 2, 3), S

def gla_mixer(z, w_gate_up, b_gate, out_norm, S0):
    B, L, _ = z.shape
    o1 = 2 * GLA_QK
    o2 = o1 + GLA_VW
    o3 = o2 + GLA_VW
    o4 = o3 + GLA_GATE_RANK
    q = z[..., :GLA_QK].reshape(B, L, GLA_HEADS, GLA_DK) * (GLA_DK ** -0.5)
    k = z[..., GLA_QK:o1].reshape(B, L, GLA_HEADS, GLA_DK)
    v = z[..., o1:o2].reshape(B, L, GLA_HEADS, GLA_DV)
    g = z[..., o2:o3]
    gd = z[..., o3:o4]
    mq = z[..., o4:]
    log_a = (jax.nn.log_sigmoid((gd @ w_gate_up + b_gate).astype(jnp.float32)) / GLA_TAU).reshape(B, L, GLA_HEADS, GLA_DK)
    if S0 is None:
        o, S = gla_chunked(q, k, v, log_a)
    else:
        o, S = gla_recurrent(q, k, v, log_a, S0)
    o = rmsnorm(o.astype(z.dtype), out_norm).reshape(B, L, GLA_VW)
    return o * jax.nn.silu(g), mq, S

def stick_breaking(q, k, v, bias, q_pos0):
    B, Lq, H, D = q.shape
    Lk = k.shape[1]
    blk = min(SB_QBLOCK, Lq)
    nb = -(-Lq // blk)
    q = jnp.pad(q, ((0, 0), (0, nb * blk - Lq), (0, 0), (0, 0)))
    scale = D ** -0.5
    bias_f = bias.astype(jnp.float32)[None, :, None, None]
    outs = []
    for bi in range(nb):
        i0 = bi * blk
        end = min(Lk, q_pos0 + i0 + blk)
        kb, vb = k[:, :end], v[:, :end]
        z = jnp.einsum('bqhd,bkhd->bhqk', q[:, i0:i0 + blk], kb, preferred_element_type=jnp.float32) * scale + bias_f
        qpos = q_pos0 + i0 + jnp.arange(blk)
        mask = jnp.arange(end)[None, :] < qpos[:, None]
        log_fail = jnp.where(mask, jax.nn.log_sigmoid(-z), 0.0)
        after = lax.cumsum(log_fail, axis=3, reverse=True) - log_fail
        w = jnp.where(mask, jnp.exp(jax.nn.log_sigmoid(z) + after), 0.0)
        outs.append(jnp.einsum('bhqk,bkhd->bqhd', w.astype(v.dtype), vb))
    return jnp.concatenate(outs, axis=1)[:, :Lq]

def sb_mixer(z, bias, past_k, past_v):
    B, L, _ = z.shape
    q = z[..., :SB_W].reshape(B, L, SB_HEADS, SB_HEAD_DIM)
    k = z[..., SB_W:2 * SB_W].reshape(B, L, SB_HEADS, SB_HEAD_DIM)
    v = z[..., 2 * SB_W:3 * SB_W].reshape(B, L, SB_HEADS, SB_HEAD_DIM)
    mq = z[..., 3 * SB_W:]
    if past_k is None:
        o = stick_breaking(q, k, v, bias, 0)
    else:
        keys = jnp.concatenate([past_k.astype(k.dtype), k], axis=1)
        vals = jnp.concatenate([past_v.astype(v.dtype), v], axis=1)
        o = stick_breaking(q, keys, vals, bias, past_k.shape[1])
    return o.reshape(B, L, SB_W), mq, k, v

def mem_kv(mem, g_norm, w_kv, k_norm):
    B, N, _ = mem.shape
    kv = rmsnorm(mem, g_norm) @ w_kv
    mk = rmsnorm(kv[..., :MEM_WIDTH].reshape(B, N, MEM_HEADS, MEM_HEAD_DIM), k_norm)
    mv = kv[..., MEM_WIDTH:].reshape(B, N, MEM_HEADS, MEM_HEAD_DIM)
    return mk, mv

def mem_attend(mq, mk, mv):
    s = jnp.einsum('blhd,bmhd->bhlm', mq, mk.astype(mq.dtype), preferred_element_type=jnp.float32) * (MEM_HEAD_DIM ** -0.5)
    p = jax.nn.softmax(s, axis=-1)
    return jnp.einsum('bhlm,bmhd->blhd', p.astype(mq.dtype), mv.astype(mq.dtype))

def conv_ffn(h, conv_prev, w_up, conv_w, conv_b, w_down):
    L = h.shape[1]
    up = h @ w_up
    gate, val = up[..., :D_FF], up[..., D_FF:]
    ext = jnp.concatenate([conv_prev.astype(gate.dtype), gate], axis=1)
    acc = conv_b
    for t in range(FFN_CONV):
        acc = acc + ext[:, t:t + L] * conv_w[t]
    y = (jax.nn.silu(acc) * val) @ w_down
    return y, ext[:, ext.shape[1] - (FFN_CONV - 1):]

def layer_tail(x, tok, mq, mk, mv, q_norm, w_o, g_ffn, conv_prev, w_up, conv_w, conv_b, w_down):
    B, L, _ = x.shape
    mqn = rmsnorm(mq.reshape(B, L, MEM_HEADS, MEM_HEAD_DIM), q_norm)
    m_out = mem_attend(mqn, mk, mv).reshape(B, L, MEM_WIDTH)
    x = x + jnp.concatenate([tok, m_out], axis=-1) @ w_o
    y, conv_new = conv_ffn(rmsnorm(x, g_ffn), conv_prev, w_up, conv_w, conv_b, w_down)
    return x + y, conv_new

def setup_inputs(seed: int = 0) -> dict:
    key = jax.random.key(seed)
    ks = jax.random.split(key, 32)
    f32 = jnp.float32
    n_pages = PAST_LEN // PAGE_SIZE
    n_phys = (DEC_BATCH * n_pages * 5) // 4
    def nrm(k, shape, scale):
        return jax.random.normal(k, shape, f32) * scale
    def gain(k, shape):
        return 1.0 + 0.02 * jax.random.normal(k, shape, f32)
    page_table = jax.random.permutation(ks[0], n_phys)[:DEC_BATCH * n_pages].reshape(DEC_BATCH, n_pages).astype(jnp.int32)
    return {
        'x_prompt': nrm(ks[1], (BATCH, SEQ, D_MODEL), 1.0),
        'x_sample': nrm(ks[2], (DEC_BATCH, DEC_SEQ, D_MODEL), 1.0),
        'state_gla': nrm(ks[3], (N_GLA_LAYERS, DEC_BATCH, GLA_HEADS, GLA_DK, GLA_DV), 1.0),
        'cache_sb_k': nrm(ks[4], (N_SB_LAYERS, n_phys, PAGE_SIZE, SB_HEADS, SB_HEAD_DIM), 1.0),
        'cache_sb_v': nrm(ks[5], (N_SB_LAYERS, n_phys, PAGE_SIZE, SB_HEADS, SB_HEAD_DIM), 1.0),
        'cache_mem_k': nrm(ks[6], (DEPTH, DEC_BATCH, N_MEM, MEM_HEADS, MEM_HEAD_DIM), 1.0),
        'cache_mem_v': nrm(ks[7], (DEPTH, DEC_BATCH, N_MEM, MEM_HEADS, MEM_HEAD_DIM), 1.0),
        'state_ffn_conv': nrm(ks[8], (DEPTH, DEC_BATCH, FFN_CONV - 1, D_FF), 1.0),
        'page_table': page_table,
        'mem_prompt': nrm(ks[9], (BATCH, N_MEM, D_MODEL), 1.0),
        'norm_mix': gain(ks[10], (DEPTH, D_MODEL)),
        'w_in_gla': nrm(ks[11], (N_GLA_LAYERS, D_MODEL, GLA_IN), D_MODEL ** -0.5),
        'w_gate_up': nrm(ks[12], (N_GLA_LAYERS, GLA_GATE_RANK, GLA_QK), GLA_GATE_RANK ** -0.5),
        'b_gate': nrm(ks[13], (N_GLA_LAYERS, GLA_QK), 0.01),
        'gla_out_norm': gain(ks[14], (N_GLA_LAYERS, GLA_DV)),
        'w_in_sb': nrm(ks[15], (N_SB_LAYERS, D_MODEL, SB_IN), D_MODEL ** -0.5),
        'sb_bias': SB_BIAS_INIT + 0.1 * jax.random.normal(ks[26], (N_SB_LAYERS, SB_HEADS), f32),
        'mem_norm': gain(ks[16], (DEPTH, D_MODEL)),
        'w_mem_kv': nrm(ks[17], (DEPTH, D_MODEL, 2 * MEM_WIDTH), D_MODEL ** -0.5),
        'mem_q_norm': gain(ks[18], (DEPTH, MEM_HEAD_DIM)),
        'mem_k_norm': gain(ks[19], (DEPTH, MEM_HEAD_DIM)),
        'w_out': nrm(ks[20], (DEPTH, MIX_WIDTH, D_MODEL), MIX_WIDTH ** -0.5),
        'norm_ffn': gain(ks[21], (DEPTH, D_MODEL)),
        'w_ffn_up': nrm(ks[22], (DEPTH, D_MODEL, 2 * D_FF), D_MODEL ** -0.5),
        'ffn_conv_w': nrm(ks[23], (DEPTH, FFN_CONV, D_FF), FFN_CONV ** -0.5),
        'ffn_conv_b': nrm(ks[24], (DEPTH, D_FF), 0.01),
        'w_ffn_down': nrm(ks[25], (DEPTH, D_FF, D_MODEL), D_FF ** -0.5),
    }

def reference(x_prompt, x_sample, state_gla, cache_sb_k, cache_sb_v, cache_mem_k, cache_mem_v, state_ffn_conv, page_table, mem_prompt, norm_mix, w_in_gla, w_gate_up, b_gate, gla_out_norm, w_in_sb, sb_bias, mem_norm, w_mem_kv, mem_q_norm, mem_k_norm, w_out, norm_ffn, w_ffn_up, ffn_conv_w, ffn_conv_b, w_ffn_down):
    x = x_prompt
    p_gla, p_sbk, p_sbv, p_mk, p_mv, p_conv = [], [], [], [], [], []
    conv0 = jnp.zeros((x.shape[0], FFN_CONV - 1, D_FF), x.dtype)
    for i in range(DEPTH):
        j = i // 2
        h = rmsnorm(x, norm_mix[i])
        if i % 2 == 0:
            tok, mq, S = gla_mixer(h @ w_in_gla[j], w_gate_up[j], b_gate[j], gla_out_norm[j], None)
            p_gla.append(S.astype(x.dtype))
        else:
            tok, mq, k, v = sb_mixer(h @ w_in_sb[j], sb_bias[j], None, None)
            p_sbk.append(k)
            p_sbv.append(v)
        mk, mv = mem_kv(mem_prompt, mem_norm[i], w_mem_kv[i], mem_k_norm[i])
        p_mk.append(mk)
        p_mv.append(mv)
        x, c = layer_tail(x, tok, mq, mk, mv, mem_q_norm[i], w_out[i], norm_ffn[i], conv0, w_ffn_up[i], ffn_conv_w[i], ffn_conv_b[i], w_ffn_down[i])
        p_conv.append(c)
    y_prompt = x

    x = x_sample
    db = x.shape[0]
    n_pages = page_table.shape[1]
    s_gla, s_sbk, s_sbv, s_conv = [], [], [], []
    for i in range(DEPTH):
        j = i // 2
        h = rmsnorm(x, norm_mix[i])
        if i % 2 == 0:
            tok, mq, S = gla_mixer(h @ w_in_gla[j], w_gate_up[j], b_gate[j], gla_out_norm[j], state_gla[j])
            s_gla.append(S.astype(state_gla.dtype))
        else:
            past_k = cache_sb_k[j][page_table].reshape(db, n_pages * cache_sb_k.shape[2], SB_HEADS, SB_HEAD_DIM)
            past_v = cache_sb_v[j][page_table].reshape(db, n_pages * cache_sb_v.shape[2], SB_HEADS, SB_HEAD_DIM)
            tok, mq, k, v = sb_mixer(h @ w_in_sb[j], sb_bias[j], past_k, past_v)
            s_sbk.append(k)
            s_sbv.append(v)
        x, c = layer_tail(x, tok, mq, cache_mem_k[i], cache_mem_v[i], mem_q_norm[i], w_out[i], norm_ffn[i], state_ffn_conv[i], w_ffn_up[i], ffn_conv_w[i], ffn_conv_b[i], w_ffn_down[i])
        s_conv.append(c)
    y_sample = x

    return (y_prompt, y_sample,
            jnp.stack(p_gla), jnp.stack(s_gla),
            jnp.stack(p_sbk), jnp.stack(p_sbv), jnp.stack(s_sbk), jnp.stack(s_sbv),
            jnp.stack(p_mk), jnp.stack(p_mv),
            jnp.stack(p_conv), jnp.stack(s_conv))


_drawn_inputs = setup_inputs


def setup_inputs(seed=0):
    import zlib

    import numpy as np

    out = dict(_drawn_inputs(seed))
    spreads = {}
    factors = {'cache_sb_k': 4.305,
     'cache_sb_v': 3.463,
     'b_gate': 8.0,
     'gla_out_norm': 5.961,
     'sb_bias': 8.0,
     'mem_norm': 2.89,
     'mem_q_norm': 8.0,
     'mem_k_norm': 2.885,
     'ffn_conv_b': 8.0,
     'norm_ffn': 2.673}
    for name, (base, spread) in spreads.items():
        noise = np.random.default_rng([zlib.crc32(name.encode()), seed]).standard_normal(out[name].shape)
        drawn = base * np.exp(spread * noise) if base else spread * noise
        out[name] = __import__('jax').numpy.asarray(drawn.astype(out[name].dtype))
    for name, factor in factors.items():
        out[name] = (out[name] * factor).astype(out[name].dtype)
    return out
```

```python
import numpy as np
import concourse.bass as bass
from concourse import mybir
from contextlib import ExitStack

F32 = mybir.dt.float32
I32 = mybir.dt.int32
ACT = mybir.ActivationFunctionType
ALU = mybir.AluOpType
AX = mybir.AxisListType

P = 128
D = 1024
KD = D // P
SEQ, NB = 512, 8
TOK = SEQ + NB
HALF = TOK // 2
TT = SEQ // P
GR = 16
CH = 64
NCH = SEQ // CH
GDK, GDV = 64, 128
NMEM, MT = 256, 2
MW = 512
SBH, SBD = 8, 64
PAGES, PAGE = 32, 128
DFF = 2816
NF = DFF // P
PCOL = 256
EPS = 1e-6
TR_BANK, NORM_BANK = 4, 6
KGROUPS = PAGES // 4


class Steps:

    def __init__(self, eng, sem):
        self.eng, self.sem, self.n, self.extra = eng, sem, 0, 0

    def mark(self, ins):
        self.n += 1
        ins.then_inc(self.sem, 1)
        return self.n

    def wait(self, n):
        self.eng.wait_ge(self.sem, n + self.extra)

    def link(self, ins):
        self.wait(self.mark(ins))

    def enter(self, i, per):
        self.start, self.per, self.extra = self.n, per, i * per

    def leave(self, count):
        assert self.n - self.start == self.per, (self.n - self.start, self.per)
        self.n = self.start + self.per * count
        self.extra = 0


class Place:

    def __init__(self):
        self.panel = self.group = self.tr = self.norm = self.sq = 0


def build(nc, I, O):
    ctx = ExitStack()
    with ctx:
        def sb(name, shape, dt=F32):
            return ctx.enter_context(nc.sbuf_tensor(name, shape, dt))

        def sem(name):
            return ctx.enter_context(nc.semaphore(name))

        xT = sb("xT", [P, KD, TOK])
        hT = sb("hT", [P, KD, TOK])
        big = sb("big", [P, NF, TOK])
        zT = big[:, 0:12, :]
        mix = big[:, 12:20, :]
        vS = big[0:NB, 20, 0:512]
        vT = sb("vT", [P, TT, 512])
        wring = sb("wring", [P, 2, 8, PCOL])
        kring = sb("kring", [P, 2, 4, 512])
        vring = sb("vring", [P, 2, 4, 512])
        memR = sb("memR", [P, KD, NMEM])
        prod = sb("prod", [P, 4, 512])
        memH = prod[:, :, :].rearrange("p a (b c) -> p (a b) c", b=2)
        memK = sb("memK", [P, MT, 512])
        memKT = sb("memKT", [P, 4, NMEM])
        memV = sb("memV", [P, MT, 512])
        scr = sb("scr", [P, 5200])
        rstd = sb("rstd", [P, 2, TOK])
        sq = sb("sq", [P, 2, TOK])
        ident = sb("ident", [P, P])
        ones = sb("ones", [P, P])
        tri = sb("tri", [P, P])
        keep = sb("keep", [P, SEQ])
        keepp = sb("keepp", [P, SBH, PAGES])
        cv = sb("cv", [P, 232])
        prev = sb("prev", [P, 2, NF, 2 * NB])
        pre = sb("pre", [P, NF, NB])
        tails = sb("tails", [P, NF, 2 + NB])
        eps = sb("eps", [P, 1])
        sbb = sb("sbb", [P, SBH])
        knorm = sb("knorm", [P, 2, P])
        wgd = sb("wgd", [P, KD, GR])
        wgu = sb("wgu", [GR, 256])
        gdT = sb("gdT", [GR, TOK])
        pt = sb("pt", [1, NB * PAGES], I32)
        st = sb("st", [P, 160])
        s32 = sb("s32", [32, NMEM])
        ps = sb("ps", [P, MT, 32])
        om = sq[0:SBH, 0, 0:512]
        qcol = sb("qcol", [P, 2, 4])
        PS = ctx.enter_context(nc.psum_tensor("PS", [P, 8, 512], F32))

        c_mix = lambda l, k: cv[:, 8 * l + k:8 * l + k + 1]
        c_ffn = lambda l, k: cv[:, 16 + 8 * l + k:17 + 8 * l + k]
        c_mem = lambda l, k: cv[:, 32 + 8 * l + k:33 + 8 * l + k]
        c_bg = lambda j: cv[:, 48 + j:49 + j]
        c_on = cv[:, 50:51]
        c_qn = lambda l: cv[:, 51 + l:52 + l]
        NC1 = 53
        NCC = 4 * NF

        def c_conv(l, t, f):
            o = NC1 + l * NCC + t * NF
            return cv[:, bass.ds(f + o, 1)]

        memtok = scr[:, 0:2048].rearrange("p (t n) -> p t n", t=2)
        xs = scr[0:NB, 2048:3072]
        rows1 = scr[0:NC1, 3072:3200]
        rows2 = [scr[0:NCC, 3200 + 128 * l:3328 + 128 * l] for l in range(2)]
        xtok = hT[:, :, :].rearrange("p a b -> p (a b)")[:, 0:4096].rearrange("p (t n) -> p t n", t=4)
        bigf = big[:, :, :].rearrange("p a b -> p (a b)")
        prows = [bigf[0:2 * NB, DFF * l:DFF * (l + 1)] for l in range(2)]
        la = scr[:, 0:1040].rearrange("p (j n) -> p j n", j=2)
        lb = scr[:, 1040:2080].rearrange("p (j n) -> p j n", j=2)
        eb = scr[:, 2080:3120].rearrange("p (j n) -> p j n", j=2)
        ke = scr[:, 3120:4160].rearrange("p (j n) -> p j n", j=2)
        hTf = hT[:, :, :].rearrange("p a b -> p (a b)")
        keT = hTf[:, 0:1024].rearrange("p (j t n) -> p j t n", j=2, t=4)
        att = hTf[:, 1024:3072].rearrange("p (h t n) -> p h t n", h=4, t=4)
        ksT = hTf[0:NB, 3072:3328]
        krf = kring[:, :, :, :].rearrange("p a b c -> p (a b c)")
        S = krf[:, 0:2048].rearrange("p (n j v) -> p n j v", n=8, j=2)
        SS = krf[:, 2048:4096].rearrange("p (b j v) -> p b j v", b=8, j=2)
        kdiag = vring[0:NB, 0, :, :].rearrange("p a b -> p (a b)").rearrange("p (b n) -> p b n", b=8)
        ktok = hTf[:, 0:2048].rearrange("p (t n) -> p t n", t=4)
        kstok = hTf[0:NB, 2048:2560]
        tailr = hTf[0:2 + NB, 0:DFF]
        ytok = bigf[:, 0:4096].rearrange("p (t n) -> p t n", t=4)
        ystok = bigf[0:NB, 4096:5120]
        SBO = {0: 0, 1: 512, 3: 896, 2: 1024}
        SBW = 1280
        sbt = [scr[:, 2560 * p:2560 * p + SBW] for p in range(2)]
        sbz = [scr[:, 2560 * p + SBW:2560 * p + 2 * SBW] for p in range(2)]
        def s5(p, k):
            o = 1280 * p + 256 * k
            return scr[:, o:o + 256].rearrange("p (h g) -> p h g", h=SBH)
        zs, zb, lg, cs, wsb = ([s5(p, k) for p in range(2)] for k in range(5))
        pb = [scr[:, 1024 * p:1024 * p + 1024].rearrange("p (t m) -> p t m", t=4) for p in range(2)]
        pT = [scr[:, 2048 + 1024 * p:3072 + 1024 * p].rearrange("p (m n) -> p m n", m=2) for p in range(2)]
        sm = scr[:, 4096:4160].rearrange("p (m b h) -> p m b h", m=2, b=NB)
        ext = [scr[:, 522 * p:522 * p + 522] for p in range(2)]
        acc = [scr[:, 1044 + 520 * p:1564 + 520 * p] for p in range(2)]
        sg = [scr[:, 2084 + 520 * p:2604 + 520 * p] for p in range(2)]

        x_in, mem_in, row_in, bc_in = sem("x_in"), sem("mem_in"), sem("row_in"), sem("bc_in")
        gd_in, pt_in, ss_in = sem("gd_in"), sem("pt_in"), sem("ss_in")
        w_in = [sem("w_in0"), sem("w_in1")]
        part_done = sem("part_done")
        k_in = [sem("k_in0"), sem("k_in1")]
        v_in = [sem("v_in0"), sem("v_in1")]
        k_used, v_used = sem("k_used"), sem("v_used")
        const_ok = sem("const_ok")
        dense_done = sem("dense_done")
        dense_free = [sem("dense_free0"), sem("dense_free1")]
        tr_done = sem("tr_done")
        tr_out = [sem("tr_out_act"), sem("tr_out_dve")]
        sq_ok, sq_used, rstd_ok, applied = (sem(n) for n in ("sq_ok", "sq_used", "rstd_ok", "norm_applied"))
        act_step, dve_step, pool_step = sem("act_step"), sem("dve_step"), sem("pool_step")
        memh_ok = sem("memh_ok")
        kss_ok, kr_ok, mk_ok = sem("kss_ok"), sem("kr_ok"), sem("mk_ok")
        gd_done, gd_ok, gu_done, gu_read = (sem(n) for n in ("gd_done", "gd_ok", "gu_done", "gu_read"))
        ln_ok, lb_ok, eb_ok, ked_ok, kee_ok, qk_ok, ke_ok = (sem(n) for n in ("ln_ok", "lb_ok", "eb_ok", "ked_ok", "kee_ok", "qk_ok", "ke_ok"))
        att_done, att_out, att_ok = sem("att_done"), sem("att_out"), sem("att_ok")
        kv_done, s_ok, kdiag_ok, outer_done, ss_ok = (sem(n) for n in ("kv_done", "s_ok", "kdiag_ok", "outer_done", "ss_ok"))
        o_done, os_done, o_ok = sem("o_done"), sem("os_done"), sem("o_ok")
        eg_ok, gla_ok = sem("eg_ok"), sem("gla_ok")
        sc_done, mx_ok, pe_ok, pn_ok, po_done, po_out = (sem(n) for n in ("sc_done", "mx_ok", "pexp_ok", "pn_ok", "po_done", "po_out"))
        qb_done, qb_read, sm_ok, smx_ok, sme_ok, smn_ok, so_done, so_out = (
            sem(n) for n in ("qb_done", "qb_read", "sm_ok", "smx_ok", "sme_ok", "smn_ok", "so_done", "so_out"))
        z_done, z_read, zl_ok, spr_ok, sp_ok, r_done, zr_ok, wr_ok, w_ok, sbo_done, sbo_out = (
            sem(n) for n in ("z_done", "z_read", "zl_ok", "spr_ok", "sp_ok", "r_done", "zr_ok", "wr_ok", "w_ok", "sbo_done", "sbo_out"))
        bq_done, bk_done, bz_ok, bl_ok, bcs_ok, br_done, bzr_ok, bw_ok, bo_done, bom_ok, bf_done, qcol_ok = (
            sem(n) for n in ("bq_done", "bk_done", "bz_ok", "bl_ok", "bcs_ok", "br_done", "bzr_ok", "bw_ok", "bo_done", "bom_ok", "bf_done", "qcol_ok"))
        bs_out = sem("bs_out")
        ga_ok, ge_ok, gc_ok, act_ok, pre_ok = (sem(n) for n in ("ga_ok", "ge_ok", "gc_ok", "act_ok", "pre_ok"))
        state_st, mem_st, kt_st, tail_st, y_st = (sem(n) for n in ("state_st", "mem_st", "kt_st", "tail_st", "y_st"))

        GIN = {0: [0, 256, 1024, 1280, 1552, 1808], 1: [0, 256, 512, 768, 1536, 1792]}
        GV = {0: [512, 768], 1: [1024, 1280]}
        GROUPS = 90
        w_main = {0: I["w_in_gla"], 1: I["w_in_sb"]}

        def kw(ap2):
            return ap2.rearrange("(k p) n -> p k n", p=P)

        UP0, DOWN0, PANELS = 16, 16 + NF, 16 + NF + 12

        def w_ready(l, n):
            ups = min(max(0, (n - UP0) // 2 + 1), NF // 2)
            return 16 * (l * (PANELS // 2 + NF // 2) + n // 2 + 1 + ups)

        def wait_panel(eng, n):
            l, n = n // PANELS, n % PANELS
            if n < 10:
                c = 2 * n + 2
            elif n < 12:
                c = 20 + 5 * (n - 9)
            elif n < DOWN0:
                c = 30 + 2 * (n - 11)
            elif (n - DOWN0) % 3 < 2:
                u = n - DOWN0
                eng.wait_ge(part_done, 8 * l + 2 * (u // 3) + u % 3 + 1)
                return
            else:
                c = 82 + 2 * ((n - DOWN0) // 3 + 1)
            eng.wait_ge(dense_done, GROUPS * l + c)

        APPLIED = [[16, 24, 32], [40, 44, 52]]
        TRN = {"setup": 16, "ktok": 16 + 22 + 2 + 6, "tail": [16 + 22, 16 + 22 + 24], "y": 16 + 22 + 24 + 10}

        def wait_tr(eng, n):
            eng.wait_ge(tr_out[0], n // 2)
            eng.wait_ge(tr_out[1], n // 2)

        block = ctx.enter_context(nc.Block())

        @block.sync
        def _(sp):
            pl = Place()

            def panel(src):
                n, s = pl.panel, pl.panel % 2
                if n >= 2:
                    wait_panel(sp, n - 2)
                sp.dma_start(wring[:, s, 0:src.shape[1], 0:src.shape[2]], src).then_inc(w_in[s], 16)
                pl.panel += 1

            sp.dma_start(xtok, I["x_prompt"][0].rearrange("(t p) n -> p t n", p=P)).then_inc(x_in, 16)
            sp.dma_start(xs, I["x_sample"].rearrange("b s n -> (b s) n")).then_inc(x_in, 16)
            sp.dma_start(memtok, I["mem_prompt"][0].rearrange("(t p) n -> p t n", p=P)).then_inc(mem_in, 16)
            nr = 0
            for name, o, n in (("norm_mix", 0, 16), ("norm_ffn", 16, 16), ("mem_norm", 32, 16), ("b_gate", 48, 2),
                               ("gla_out_norm", 50, 1), ("mem_q_norm", 51, 2)):
                sp.dma_start(rows1[o:o + n, :], I[name].rearrange("l (k p) -> (l k) p", p=P)).then_inc(row_in, 16)
                nr += 1
            for l in range(2):
                sp.dma_start(rows2[l][0:3 * NF, :], I["ffn_conv_w"][l].rearrange("t (f p) -> (t f) p", p=P)).then_inc(row_in, 16)
                sp.dma_start(rows2[l][3 * NF:4 * NF, :], I["ffn_conv_b"][l].rearrange("(f p) -> f p", p=P)).then_inc(row_in, 16)
                sp.dma_start(prows[l], I["state_ffn_conv"][l].rearrange("b t f -> (b t) f")).then_inc(row_in, 16)
            sp.dma_start(knorm[:, :, :], I["mem_k_norm"].rearrange("(a l) d -> a l d", a=1).to_broadcast((P, 2, P))).then_inc(bc_in, 16)
            sp.dma_start(sbb[:, :], I["sb_bias"].to_broadcast((P, SBH))).then_inc(bc_in, 16)
            sp.dma_start(wgd[:, :, :], kw(I["w_in_gla"][0])[:, :, 1536:1536 + GR]).then_inc(gd_in, 16)
            sp.dma_start(wgu[:, :], I["w_gate_up"][0]).then_inc(gd_in, 16)
            sp.dma_start(pt[:, :], I["page_table"].rearrange("(a b) n -> a (b n)", a=1)).then_inc(pt_in, 16)
            for hh in range(2):
                for j in range(2):
                    sp.dma_start(SS[64 * hh:64 * hh + 64, :, j, :],
                                 I["state_gla"][0, :, 2 * j + hh].rearrange("b k v -> k b v")).then_inc(ss_in, 16)

            def mem_groups(l, n0):
                kk, vv = (kring, k_used, k_in, "cache_mem_k"), (vring, v_used, v_in, "cache_mem_v")
                for g, (ring, used, in_, cache) in ((0, kk), (1, kk), (0, vv), (1, vv), (2, kk), (3, kk), (2, vv), (3, vv)):
                    n = n0 + g
                    if n >= 2:
                        sp.wait_ge(used, n - 1)
                    for bb in range(2):
                        for mt in range(2):
                            sp.dma_start(ring[:, g % 2, 2 * bb + mt, :],
                                         I[cache][l, 2 * g + bb, P * mt:P * mt + P].rearrange("m h d -> m (h d)")).then_inc(in_[g % 2], 16)

            def pages(cache, ring, in_, b, g):
                for jj in range(4):
                    page = sp.value_load(pt[0:1, bass.ds(b * PAGES + (PAGES - 1 - 4 * g - jj), 1)], min_val=0,
                                         max_val=I[cache].shape[1] - 1)
                    sp.dma_start(ring[:, g % 2, jj, :],
                                 I[cache][0, bass.ds(page, 1)].rearrange("a p h d -> (a p) (h d)")).then_inc(in_[g % 2], 16)

            for l in range(2):
                wm = kw(w_main[l][0])
                wkv = kw(I["w_mem_kv"][l])
                for p in range(4):
                    panel(wkv[:, :, PCOL * p:PCOL * p + PCOL])
                for c in GIN[l] + GV[l]:
                    panel(wm[:, :, c:c + PCOL])
                wo = kw(I["w_out"][l])
                for p in range(2):
                    panel(wo[:, :, PCOL * p:PCOL * p + PCOL])
                if l == 0:
                    sp.wait_ge(s_ok, 1)
                    sp.wait_ge(ss_ok, 1)
                    for hh in range(2):
                        for j in range(2):
                            sp.dma_start(O["gla_p"][0, 0, 2 * j + hh], S[64 * hh:64 * hh + 64, 7, j, :]).then_inc(state_st, 16)
                            sp.dma_start(O["gla_s"][0, :, 2 * j + hh].rearrange("b k v -> k b v"),
                                         SS[64 * hh:64 * hh + 64, :, j, :]).then_inc(state_st, 16)
                    sp.wait_ge(state_st, 8 * 16)
                    sp.wait_ge(os_done, 1)
                    mem_groups(0, 0)
                else:
                    sp.wait_ge(pt_in, 16)
                    for g in range(KGROUPS):
                        sp.wait_ge(k_used, 3 + g)
                        pages("cache_sb_k", kring, k_in, 0, g)
                    with sp.Fori(0, NB - 1) as b:
                        for g in range(KGROUPS):
                            sp.wait_ge(k_used, b * KGROUPS + (3 + KGROUPS + g))
                            pages("cache_sb_k", kring, k_in, b + 1, g)
                            sp.wait_ge(v_used, b * KGROUPS + (3 + g))
                            pages("cache_sb_v", vring, v_in, b, g)
                    for g in range(KGROUPS):
                        sp.wait_ge(v_used, 3 + (NB - 1) * KGROUPS + g)
                        pages("cache_sb_v", vring, v_in, NB - 1, g)
                    mem_groups(1, 4 + NB * KGROUPS)
                for p in range(2, 4):
                    panel(wo[:, :, PCOL * p:PCOL * p + PCOL])
                wu = I["w_ffn_up"][l].rearrange("(k p) (c f n) -> p k c f n", p=P, c=2, n=P)
                with sp.Fori(0, NF // 2) as i:
                    for s in range(2):
                        sp.wait_ge(dense_done, i * 4 + (GROUPS * l + 36 + 2 * s))
                        for c in range(2):
                            sp.dma_start(wring[:, s, :, P * c:P * c + P],
                                         wu[:, :, c, bass.ds(2 * i + s, 1), :].rearrange("p k a n -> p k (a n)")).then_inc(w_in[s], 16)
                pl.panel += NF
                wd = I["w_ffn_down"][l].rearrange("(k p) (m n) -> p k m n", p=P, n=PCOL)
                for u in range(12):
                    kc = u % 3
                    nk = 8 if kc < 2 else 6
                    panel(wd[:, 8 * kc:8 * kc + nk, u // 3, :])
            sp.wait_ge(state_st, 8 * 16)

        @block.gpsimd
        def _(pool):
            steps = Steps(pool, pool_step)
            nc.gpsimd.memset(ident[:, :], 0.0).then_inc(pool_step, 1)
            nc.gpsimd.memset(ones[:, :], 1.0).then_inc(pool_step, 1)
            nc.gpsimd.memset(tri[:, :], 1.0).then_inc(pool_step, 1)
            nc.gpsimd.memset(keep[:, :], 1.0).then_inc(pool_step, 1)
            nc.gpsimd.memset(keepp[:, :, :], 1.0).then_inc(pool_step, 1)
            nc.gpsimd.memset(eps[:, :], EPS).then_inc(pool_step, 1)
            steps.n = 6
            pool.wait_ge(pool_step, 6)
            af = nc.gpsimd.affine_select
            af(out=ident[:, :], in_=ident[:, :], compare_op=ALU.not_equal, fill=1.0, base=0, pattern=[[-1, P]], channel_multiplier=1).then_inc(const_ok, 1)
            af(out=tri[:, :], in_=tri[:, :], compare_op=ALU.is_ge, fill=0.0, base=0, pattern=[[-1, P]], channel_multiplier=1).then_inc(const_ok, 1)
            af(out=keep[:, :], in_=keep[:, :], compare_op=ALU.not_equal, fill=0.0, base=0, pattern=[[0, NCH], [1, CH]], channel_multiplier=0).then_inc(const_ok, 1)
            af(out=keepp[:, :, :], in_=keepp[:, :, :], compare_op=ALU.not_equal, fill=0.0, base=0, pattern=[[0, SBH], [1, PAGES]], channel_multiplier=0).then_inc(const_ok, 1)

            for l in range(2):
                pool.wait_ge(mk_ok, l + 1)
                pool.dma_start(O["mem_k"][l, 0].rearrange("(t p) h d -> p t (h d)", p=P), memK[:, :, :]).then_inc(mem_st, 16)
                pool.dma_start(O["mem_v"][l, 0].rearrange("(t p) h d -> p t (h d)", p=P), memV[:, :, :]).then_inc(mem_st, 16)
                if l == 0:
                    for h in range(4):
                        pool.wait_ge(att_out, h + 1)
                        steps.link(af(out=att[:, h], in_=att[:, h], compare_op=ALU.is_ge, fill=0.0, base=0,
                                      pattern=[[0, TT], [1, P]], channel_multiplier=-1))
                        af(out=att[:, h].rearrange("p t (c n) -> p t c n", c=2), in_=att[:, h].rearrange("p t (c n) -> p t c n", c=2),
                           compare_op=ALU.is_ge, fill=0.0, base=0, pattern=[[0, TT], [-CH, 2], [0, CH]], channel_multiplier=1).then_inc(att_ok, 1)
                else:
                    for h in range(SBH):
                        for ready, done in ((spr_ok, sp_ok), (wr_ok, w_ok)):
                            pool.wait_ge(ready, h + 1)
                            for kc in range(TT):
                                blk = sbt[h % 2][:, SBO[kc]:SBO[kc] + P]
                                af(out=blk, in_=blk, compare_op=ALU.is_gt, fill=0.0, base=0, pattern=[[1, P]],
                                   channel_multiplier=-1).then_inc(done, 1)
                    wait_tr(pool, TRN["ktok"])
                    pool.wait_ge(dense_free[0], (GROUPS + 30) // 2)
                    pool.wait_ge(dense_free[1], (GROUPS + 30) // 2)
                    flat = lambda ap: ap.rearrange("t h d -> t (h d)")
                    pool.dma_start(flat(O["sb_kp"][0, 0]).rearrange("(t p) n -> p t n", p=P), ktok).then_inc(kt_st, 16)
                    pool.dma_start(flat(O["sb_vp"][0, 0]).rearrange("(t p) n -> p t n", p=P), vT[:, :, :]).then_inc(kt_st, 16)
                    pool.dma_start(O["sb_ks"][0].rearrange("b s h d -> (b s) (h d)"), kstok).then_inc(kt_st, 16)
                    pool.dma_start(O["sb_vs"][0].rearrange("b s h d -> (b s) (h d)"), vS).then_inc(kt_st, 16)
                wait_tr(pool, TRN["tail"][l])
                pool.dma_start(O["conv_p"][l, 0], tailr[0:2, :]).then_inc(tail_st, 16)
                pool.dma_start(O["conv_s"][l, :, 1, :], tailr[2:2 + NB, :]).then_inc(tail_st, 16)
                pool.dma_start(O["conv_s"][l, :, 0, :], I["state_ffn_conv"][l, :, 1, :]).then_inc(tail_st, 16)
            wait_tr(pool, TRN["y"])
            pool.dma_start(O["y_p"][0].rearrange("(t p) n -> p t n", p=P), ytok).then_inc(y_st, 16)
            pool.dma_start(O["y_s"].rearrange("b s n -> (b s) n"), ystok).then_inc(y_st, 16)
            pool.wait_ge(mem_st, 64)
            pool.wait_ge(kt_st, 64)
            pool.wait_ge(tail_st, 96)
            pool.wait_ge(y_st, 32)

        @block.tensor
        def _(pe):
            pl = Place()
            mm, tp = nc.tensor.matmul, nc.tensor.transpose

            def tr_unit(parts):
                n = pl.tr
                if n >= 2:
                    pe.wait_ge(tr_out[n % 2], n // 2)
                for c, src in parts:
                    k, m = src.shape[0], src.shape[1]
                    last = tp(PS[0:m, TR_BANK + n % 2, c:c + k], src, ident[0:k, 0:k])
                last.then_inc(tr_done, 1)
                pl.tr += 1

            def norm_sums(nk, width=TOK):
                if pl.norm:
                    pe.wait_ge(rstd_ok, pl.norm)
                w = width // 2
                for k in range(nk):
                    pe.wait_ge(sq_ok, pl.sq + 1)
                    for c in range(2):
                        last = mm(PS[:, NORM_BANK + c, 0:w], ones[:, :], sq[:, pl.sq % 2, w * c:w * c + w],
                                  start=(k == 0), stop=(k == nk - 1))
                    last.then_inc(sq_used, 1)
                    pl.sq += 1
                pl.norm += 1

            def dense_group(s, par, cols, nk, src, k0, first, last_, i=None, g=None):
                for k in range(nk):
                    for c in range(2):
                        last = mm(PS[:, 2 * par + c, 0:HALF], wring[:, s, k, cols:cols + P],
                                  src[:, k0 + k, HALF * c:HALF * c + HALF],
                                  start=(first and k == 0), stop=(last_ and k == nk - 1))
                return last

            def free(par):
                if pl.group >= 2:
                    pe.wait_ge(dense_free[par], pl.group // 2)

            def in_panel(l, n):
                pe.wait_ge(w_in[n % 2], w_ready(l, n))

            def fm_panel(l, n, src):
                in_panel(l, n)
                for m in range(2):
                    free(m)
                    last = dense_group(n % 2, m, P * m, 8, src, 0, True, True)
                    last.then_inc(dense_done, 1)
                    pl.group += 1

            def gla():
                pe.wait_ge(gd_ok, 1)
                for j in range(2):
                    if j:
                        pe.wait_ge(gu_read, 1)
                    for c in range(2):
                        last = mm(PS[:, NORM_BANK + c, 0:HALF], wgu[:, P * j:P * j + P], gdT[:, HALF * c:HALF * c + HALF],
                                  start=True, stop=True)
                    last.then_inc(gu_done, 1)
                pe.wait_ge(qk_ok, 1)
                for h in range(4):
                    j, r = h // 2, 64 * (h % 2)
                    for t in range(TT):
                        last = mm(PS[:, h, P * t:P * t + P], zT[r:r + 64, 2 + j, P * t:P * t + P],
                                  zT[r:r + 64, j, P * t:P * t + P], start=True, stop=True)
                    last.then_inc(att_done, 1)
                for j in range(2):
                    tr_unit([(P * t, ke[:, j, P * t:P * t + P]) for t in range(TT)])
                for j in range(2):
                    tr_unit([(0, zT[:, 2 + j, SEQ:TOK])])
                pe.wait_ge(att_out, 4)
                wait_tr(pe, pl.tr)
                for n in range(NCH):
                    t, r = n // 2, 64 * (n % 2)
                    for h in range(4):
                        j, o = h // 2, 64 * (h % 2)
                        c = 256 * (n // 4) + P * j
                        last = mm(PS[o:o + 64, n % 4, c:c + P], keT[r:r + 64, j, t, o:o + 64],
                                  vT[r:r + 64, t, P * h:P * h + P], start=True, stop=True)
                last.then_inc(kv_done, 1)
                pe.wait_ge(s_ok, 1)
                pe.wait_ge(kdiag_ok, 1)
                for b in range(NB):
                    for h in range(4):
                        j, o = h // 2, 64 * (h % 2)
                        c = 256 * (b % 2) + P * j
                        last = mm(PS[o:o + 64, b // 2, c:c + P], kdiag[:, b, 64 * h:64 * h + 64],
                                  vS[:, P * h:P * h + P], start=True, stop=True)
                last.then_inc(outer_done, 1)
                pe.wait_ge(ss_ok, 1)
                for h in range(4):
                    j, r = h // 2, 64 * (h % 2)
                    pe.wait_ge(att_ok, h + 1)
                    for t in range(TT):
                        last = mm(PS[:, h, P * t:P * t + P], vT[:, t, P * h:P * h + P], att[:, h, t, :], start=True, stop=False)
                        for n in (2 * t, 2 * t + 1):
                            if n:
                                last = mm(PS[:, h, CH * n:CH * n + CH], S[r:r + 64, n - 1, j, :],
                                          zT[r:r + 64, j, CH * n:CH * n + CH], start=False, stop=(n == 2 * t + 1))
                    last.then_inc(o_done, 1)
                for h in range(4):
                    j, r = h // 2, 64 * (h % 2)
                    for b in range(NB):
                        last = mm(PS[:, NORM_BANK + h % 2, NB * j + b:NB * j + b + 1], SS[r:r + 64, b, j, :],
                                  zT[r:r + 64, j, SEQ + b:SEQ + b + 1], start=True, stop=True)
                last.then_inc(os_done, 1)

            PSf = PS[:, :, :].rearrange("p a b -> p (a b)")

            def sb_prompt():
                for t in range(TT):
                    tr_unit([(P * j, zT[:, 4 + j, P * t:P * t + P]) for j in range(4)])
                for a in range(2):
                    tr_unit([(P * c, zT[:, 4 + 2 * a + c, SEQ:TOK]) for c in range(2)])

                def scores(h):
                    j, r = h // 2, 64 * (h % 2)
                    if h:
                        pe.wait_ge(z_read, h)
                    for kc in range(TT):
                        w = SEQ - P * kc
                        last = mm(PSf[:, SBO[kc]:SBO[kc] + w], zT[r:r + 64, 4 + j, P * kc:P * kc + P],
                                  zT[r:r + 64, j, P * kc:SEQ], start=True, stop=True)
                    last.then_inc(z_done, 1)

                scores(0)
                wait_tr(pe, pl.tr)
                for h in range(SBH):
                    x = sbt[h % 2]
                    pe.wait_ge(sp_ok, 4 * h + 4)
                    if h:
                        pe.wait_ge(zr_ok, h)
                    for kc in range(TT):
                        w = SEQ - P * kc
                        o = 2048 + SBO[kc]
                        last = mm(PSf[:, o:o + w], tri[:, :], x[:, SBO[kc]:SBO[kc] + w], start=True, stop=(kc == TT - 1))
                        for k2 in range(kc + 1, TT):
                            w2 = SEQ - P * k2
                            last = mm(PSf[:, o + P * (k2 - kc):o + P * (k2 - kc) + w2], ones[:, :],
                                      x[:, SBO[k2]:SBO[k2] + w2], start=False, stop=(k2 == TT - 1))
                    last.then_inc(r_done, 1)
                    if h + 1 < SBH:
                        scores(h + 1)
                    pe.wait_ge(w_ok, 4 * h + 4)
                    if h >= 2 and h % 2 == 0:
                        pe.wait_ge(sbo_out, h // 2)
                    r = 64 * (h % 2)
                    for kc in range(TT):
                        w = SEQ - P * kc
                        last = mm(PS[r:r + 64, 3, P * kc:SEQ], vT[:, kc, SBD * h:SBD * h + SBD],
                                  x[:, SBO[kc]:SBO[kc] + w], start=(kc == 0), stop=(kc == TT - 1))
                    last.then_inc(sbo_done, 1)

            def sb_samples():
                def q_rows(p, n, i=0):
                    pe.wait_ge(qcol_ok, n)
                    for j in range(4):
                        last = mm(PS[:, p, P * j:P * j + P], qcol[:, p, j:j + 1].to_broadcast((P, P)), ident[:, :],
                                  start=True, stop=True)
                    last.then_inc(bq_done, 1)

                def sample(i, p, more):
                    pe.wait_ge(bcs_ok, i * 2 + (p + 1))
                    mm(PS[:, 2 + p, 0:256], tri[:, :], zs[p].rearrange("p h g -> p (h g)"), start=True, stop=False)
                    mm(PS[:, 2 + p, 0:256], ones[:, :], cs[p].rearrange("p h g -> p (h g)"), start=False, stop=True).then_inc(br_done, 1)
                    if more:
                        q_rows(p, i * 2 + (p + 3))
                    pe.wait_ge(bw_ok, i * 2 + (p + 1))
                    for g in range(KGROUPS):
                        pe.wait_ge(v_in[g % 2], i * 512 + (256 * p + 64 * (3 + g // 2)))
                        for jj in range(4):
                            last = mm(PS[0:SBH, 4 + p, :], wsb[p][:, :, 4 * g + jj], vring[:, g % 2, jj, :],
                                      start=(g == 0 and jj == 0), stop=(g == KGROUPS - 1 and jj == 3))
                        last.then_inc(v_used, 1)
                    pe.wait_ge(bom_ok, i * 2 + (p + 1))
                    for j in range(4):
                        last = mm(PS[:, NORM_BANK, bass.ds(i * 4 + (16 * j + 2 * p), 2)], om[:, P * j:P * j + P],
                                  ident[0:SBH, 2 * j:2 * j + 2], start=True, stop=True)
                    last.then_inc(bf_done, 1)

                pe.wait_ge(sbo_out, 4)
                q_rows(0, 1)
                q_rows(1, 2)
                with pe.Fori(0, NB // 2 - 1) as i:
                    for p in range(2):
                        sample(i, p, True)
                for p in range(2):
                    sample(NB // 2 - 1, p, False)

            pe.wait_ge(const_ok, 4)
            pe.wait_ge(row_in, 12 * 16)
            tr_unit([(0, rows1), (NC1, rows2[0]), (NC1 + NCC, rows2[1])])
            for l in range(2):
                tr_unit([(16 * f, prows[l][:, P * f:P * f + P]) for f in range(NF)])
            pe.wait_ge(x_in, 32)
            tr_unit([(NB * k, xs[:, P * k:P * k + P]) for k in range(KD)])
            for k in range(KD):
                tr_unit([(P * t, xtok[:, t, P * k:P * k + P]) for t in range(TT)])
            pe.wait_ge(mem_in, 16)
            for k in range(0, KD, 2):
                tr_unit([(256 * a + P * t, memtok[:, t, P * (k + a):P * (k + a) + P]) for a in range(2) for t in range(2)])
            norm_sums(KD, NMEM)

            for l in range(2):
                norm_sums(KD)
                pe.wait_ge(memh_ok, l + 1)
                for p in range(4):
                    in_panel(l, p)
                    for t in range(MT):
                        free(t)
                        for k in range(KD):
                            last = mm(PS[:, 2 * t, 0:PCOL], memH[:, k, P * t:P * t + P], wring[:, p % 2, k, :],
                                      start=(k == 0), stop=(k == KD - 1))
                        last.then_inc(dense_done, 1)
                        pl.group += 1
                pe.wait_ge(mk_ok, l + 1)
                for a in range(2):
                    tr_unit([(256 * c + P * t, memK[:, t, P * (2 * a + c):P * (2 * a + c) + P]) for c in range(2) for t in range(2)])
                pe.wait_ge(applied, APPLIED[l][0])
                for p in range(6):
                    fm_panel(l, 4 + p, hT)
                if l == 0:
                    pe.wait_ge(gd_in, 32)
                    pe.wait_ge(rstd_ok, pl.norm)
                    for k in range(KD):
                        for c in range(2):
                            last = mm(PS[0:GR, NORM_BANK + c, 0:HALF], wgd[:, k, :], hT[:, k, HALF * c:HALF * c + HALF],
                                      start=(k == 0), stop=(k == KD - 1))
                    last.then_inc(gd_done, 1)
                for p in range(2):
                    in_panel(l, 10 + p)
                    for t in range(TT + 1):
                        n = P if t < TT else NB
                        free(pl.group % 2)
                        for k in range(KD):
                            last = mm(PS[0:n, 2 * (pl.group % 2), 0:PCOL], hT[:, k, P * t:P * t + n], wring[:, p, k, :],
                                      start=(k == 0), stop=(k == KD - 1))
                        last.then_inc(dense_done, 1)
                        pl.group += 1
                for par in range(2):
                    pe.wait_ge(dense_free[par], pl.group // 2)
                if l == 0:
                    gla()
                    for h in range(4):
                        norm_sums(1)
                else:
                    sb_prompt()
                    sb_samples()
                for h in range(4):
                    norm_sums(1)
                for h in range(4 + 1):
                    if h < 4:
                        pe.wait_ge(applied, APPLIED[l][1] - 3 + h)
                        if h == 0:
                            pe.wait_ge(tr_out[0], pl.tr // 2)
                            pe.wait_ge(tr_out[1], pl.tr // 2)
                        if h >= 2:
                            pe.wait_ge(po_out, 4 * l + h - 1)
                        for t in range(TT):
                            last = mm(PS[:, 2 * (h % 2) + t // 2, 256 * (t % 2):256 * (t % 2) + 256],
                                      zT[:, 8 + h, P * t:P * t + P], memKT[:, h, :], start=True, stop=True)
                        last.then_inc(sc_done, 1)
                    if h >= 1:
                        a = h - 1
                        pe.wait_ge(pn_ok, 4 * l + a + 1)
                        for mt in range(MT):
                            tr_unit([(P * t, pb[a % 2][:, t, P * mt:P * mt + P]) for t in range(TT)])
                        for mt in range(MT):
                            pe.wait_ge(tr_out[mt], pl.tr // 2)
                            last = mm(PS[:, 2 * (a % 2), :], memV[:, mt, P * a:P * a + P], pT[a % 2][:, mt, :],
                                      start=(mt == 0), stop=(mt == MT - 1))
                        last.then_inc(po_done, 1)
                pe.wait_ge(rstd_ok, pl.norm)
                for b in range(NB):
                    if b >= 2:
                        pe.wait_ge(qb_read, 8 * l + b - 1)
                    for h in range(4):
                        last = mm(PS[:, NORM_BANK + b % 2, P * h:P * h + P], zT[:, 8 + h, SEQ + b:SEQ + b + 1].to_broadcast((P, P)),
                                  ident[:, :], start=True, stop=True)
                    last.then_inc(qb_done, 1)
                n0 = 4 + NB * KGROUPS if l else 0
                pe.wait_ge(k_used, n0 + 4)
                tr_unit([(P * mt, sm[:, mt].rearrange("p b h -> p (b h)")) for mt in range(MT)])
                pe.wait_ge(smn_ok, l + 1)
                tr_unit([(32 * mt, s32[:, P * mt:P * mt + P]) for mt in range(MT)])
                pe.wait_ge(tr_out[1], pl.tr // 2)
                for g in range(4):
                    n = n0 + g
                    pe.wait_ge(v_in[g % 2], 64 * (n // 2 + 1))
                    for bb in range(2):
                        b = 2 * g + bb
                        for h in range(4):
                            for mt in range(MT):
                                last = mm(PS[:, NORM_BANK, 8 * h + b:8 * h + b + 1], vring[:, g % 2, 2 * bb + mt, P * h:P * h + P],
                                          ps[:, mt, 4 * b + h:4 * b + h + 1], start=(mt == 0), stop=(mt == MT - 1))
                    last.then_inc(v_used, 1)
                pe.wait_ge(so_out, l + 1)
                pe.wait_ge(po_out, 4 * l + 4)
                for p in range(4):
                    fm_panel(l, 12 + p, mix)
                norm_sums(KD)
                pe.wait_ge(applied, APPLIED[l][2])
                g0 = pl.group
                with pe.Fori(0, NF // 2) as i:
                    for s in range(2):
                        pe.wait_ge(w_in[s], i * 32 + w_ready(l, 16 + s))
                        for m in range(2):
                            pe.wait_ge(dense_free[m], i * 2 + (g0 // 2 + s))
                            last = dense_group(s, m, P * m, 8, hT, 0, True, True)
                            last.then_inc(dense_done, 1)
                pl.group += 2 * NF
                pe.wait_ge(dense_free[1], (pl.group) // 2)
                for q in range(6):
                    tr_unit([(P * a, tails[:, 4 * q + a, :]) for a in range(4) if 4 * q + a < NF])
                g0 = pl.group
                with pe.Fori(0, 2) as i:
                    for u in range(6):
                        m, kc, s = u // 3, u % 3, u % 2
                        pe.wait_ge(w_in[s], i * 48 + w_ready(l, 16 + NF + u))
                        for par in range(2):
                            if kc == 0:
                                pe.wait_ge(dense_free[par], i * 2 + (g0 // 2 + m))
                            last = dense_group(s, par, P * par, 8 if kc < 2 else 6, big, 8 * kc, kc == 0, kc == 2)
                            if kc == 2:
                                last.then_inc(dense_done, 1)
                        if kc < 2:
                            last.then_inc(part_done, 1)
                pl.group += 8
            for par in range(2):
                pe.wait_ge(dense_free[par], GROUPS)
            for t in range(TT):
                for q in range(2):
                    tr_unit([(P * a, xT[:, 4 * q + a, P * t:P * t + P]) for a in range(4)])
            for q in range(2):
                tr_unit([(P * a, xT[:, 4 * q + a, SEQ:TOK]) for a in range(4)])

        def bank(n, rows, cols):
            return PS[0:rows, TR_BANK + n % 2, 0:cols]

        def units_setup():
            yield lambda n: (cv[:, 0:NC1 + 2 * NCC], bank(n, P, NC1 + 2 * NCC))
            for l in range(2):
                yield lambda n, l=l: (prev[:, l], bank(n, P, 16 * NF).rearrange("p (f x) -> p f x", x=16))
            yield lambda n: (xT[:, :, SEQ:TOK], bank(n, P, NB * KD).rearrange("p (k b) -> p k b", b=NB))
            for k in range(KD):
                yield lambda n, k=k: (xT[:, k, 0:SEQ], bank(n, P, SEQ))
            for q in range(4):
                yield lambda n, q=q: (memR[:, 2 * q:2 * q + 2, :], bank(n, P, 512).rearrange("p (a m) -> p a m", a=2))

        def units_memk():
            for a in range(2):
                yield lambda n, a=a: (memKT[:, 2 * a:2 * a + 2, :], bank(n, P, 512).rearrange("p (a m) -> p a m", a=2))

        def units_gla():
            for j in range(2):
                yield lambda n, j=j: (keT[:, j], bank(n, P, 512).rearrange("p (t m) -> p t m", t=TT))
            for j in range(2):
                yield lambda n, j=j: (ksT[:, P * j:P * j + P], bank(n, NB, P))

        def units_sb():
            for t in range(TT):
                yield lambda n, t=t: (ktok[:, t, :], bank(n, P, 512))
            for a in range(2):
                yield lambda n, a=a: (kstok[:, 256 * a:256 * a + 256], bank(n, NB, 256))

        def units_probs(h):
            for mt in range(MT):
                yield lambda n, mt=mt: (pT[h % 2][:, mt, :], bank(n, P, SEQ))

        def units_tail():
            for q in range(6):
                w = 512 if q < 5 else 256
                yield lambda n, q=q, w=w: (tailr[:, 512 * q:512 * q + w], bank(n, 2 + NB, w))

        def units_y():
            for t in range(TT):
                for q in range(2):
                    yield lambda n, t=t, q=q: (ytok[:, t, 512 * q:512 * q + 512], bank(n, P, 512))
            for q in range(2):
                yield lambda n, q=q: (ystok[:, 512 * q:512 * q + 512], bank(n, NB, 512))

        s_mx = lambda p: st[:, 8 * p:8 * p + 4]
        s_sum = lambda p: st[:, 16 + 8 * p:20 + 8 * p]
        s_kn = st[:, 32:40]
        s_smx, s_ssum = st[0:32, 48:49], st[0:32, 49:50]
        MSC = float(P) ** -0.5
        one = ones[:, 0:1]

        def norm_sources(l, what):
            if what == "mem":
                return [memR[:, k, :] for k in range(KD)], D, None, None, NMEM
            if what == "mix":
                return [xT[:, k, :] for k in range(KD)], D, [c_mix(l, k) for k in range(KD)], [hT[:, k, :] for k in range(KD)], TOK
            if what == "ffn":
                return [xT[:, k, :] for k in range(KD)], D, [c_ffn(l, k) for k in range(KD)], [hT[:, k, :] for k in range(KD)], TOK
            if what == "gla":
                return [mix[:, l, :]], GDV, [c_on], [mix[:, l, :]], TOK
            return [zT[:, 8 + what, :]], P, [c_qn(l)], [zT[:, 8 + what, :]], TOK

        @block.scalar
        def _(act):
            pl = Place()
            steps = Steps(act, act_step)
            fn = nc.scalar.activation

            def units(which):
                for u in which:
                    if pl.tr % 2 == 0:
                        act.wait_ge(tr_done, pl.tr + 1)
                        dst, src = u(pl.tr)
                        fn(dst, src, ACT.Copy).then_inc(tr_out[0], 1)
                    pl.tr += 1

            def norm(l, what, ready=None):
                srcs, n, _, _, w = norm_sources(l, what)
                for k, src in enumerate(srcs):
                    if ready:
                        ready(k)
                    if pl.sq >= 2:
                        act.wait_ge(sq_used, pl.sq - 1)
                    fn(sq[:, pl.sq % 2, 0:w], src, ACT.Square).then_inc(sq_ok, 1)
                    pl.sq += 1
                act.wait_ge(sq_used, pl.sq)
                if pl.norm >= 2:
                    act.wait_ge(applied, pl.applied[-2])
                r = rstd[:, pl.norm % 2, 0:w]
                steps.link(fn(r.rearrange("p (c n) -> p c n", c=2), PS[:, NORM_BANK:NORM_BANK + 2, 0:w // 2], ACT.Ln,
                              scale=1.0 / n, bias=eps[:, 0:1]))
                fn(r, r, ACT.Exp, scale=-0.5).then_inc(rstd_ok, 1)
                pl.norm += 1
                pl.applied.append(pl.applied[-1] + len(srcs))

            pl.applied = [0]

            def gla():
                act.wait_ge(gd_done, 1)
                fn(gdT[:, :].rearrange("p (c n) -> p c n", c=2), PS[0:GR, NORM_BANK:NORM_BANK + 2, 0:HALF], ACT.Copy).then_inc(gd_ok, 1)
                for j in range(2):
                    act.wait_ge(gu_read, j + 1)
                    steps.link(fn(la[:, j], lb[:, j], ACT.Abs))
                    steps.link(fn(la[:, j], la[:, j], ACT.Exp, scale=-1.0))
                    fn(la[:, j], la[:, j], ACT.Ln, bias=one).then_inc(ln_ok, 1)
                act.wait_ge(lb_ok, 1)
                fn(eb, lb, ACT.Exp, scale=1.0 / 16).then_inc(eb_ok, 1)
                fn(la, lb, ACT.Exp, scale=-1.0 / 16).then_inc(eb_ok, 1)
                act.wait_ge(ked_ok, 1)
                fn(ke[:, :, 0:SEQ], ke[:, :, 0:SEQ], ACT.Exp, scale=1.0 / 16).then_inc(kee_ok, 1)
                for h in range(4):
                    act.wait_ge(att_done, h + 1)
                    fn(att[:, h], PS[:, h, :].rearrange("p (t n) -> p t n", t=TT), ACT.Copy).then_inc(att_out, 1)
                units(units_gla())
                act.wait_ge(qk_ok, 1)
                fn(scr[:, 0:4 * TOK].rearrange("p (h n) -> p h n", h=4), zT[:, 4:8, :], ACT.Exp, scale=-1.0).then_inc(eg_ok, 1)
                for h in range(4):
                    act.wait_ge(o_done, h + 1)
                    steps.link(fn(mix[:, h, 0:SEQ], PS[:, h, :], ACT.Copy))
                act.wait_ge(os_done, 1)
                for a in range(2):
                    steps.link(fn(mix[:, a:4:2, SEQ:TOK], PS[:, NORM_BANK + a, 0:16].rearrange("p (j b) -> p j b", j=2), ACT.Copy))
                for h in range(4):
                    norm(h, "gla")

            def softplus_prompt(h):
                act.wait_ge(z_read, h + 1)
                if h >= 2:
                    act.wait_ge(sbo_done, h - 1)
                x = sbt[h % 2]
                steps.link(fn(x, sbz[h % 2], ACT.Abs))
                steps.link(fn(x, x, ACT.Exp, scale=-1.0))
                fn(x, x, ACT.Ln, bias=one).then_inc(zl_ok, 1)

            def sb_prompt():
                softplus_prompt(0)
                for h in range(SBH):
                    act.wait_ge(zr_ok, h + 1)
                    fn(sbt[h % 2], sbz[h % 2], ACT.Exp).then_inc(wr_ok, 1)
                    if h + 1 < SBH:
                        softplus_prompt(h + 1)
                    if h % 2:
                        act.wait_ge(sbo_done, h + 1)
                        fn(mix[:, h // 2, 0:SEQ], PS[:, 3, :], ACT.Copy).then_inc(sbo_out, 1)

            def q_column(b, p, n):
                if n is not None:
                    act.wait_ge(bq_done, n)
                fn(qcol[:, p, :], zT[:, 0:4, bass.ds(b + SEQ, 1)].rearrange("p j a -> p (j a)"), ACT.Copy).then_inc(qcol_ok, 1)

            def sample(i, p, more):
                act.wait_ge(bz_ok, i * 2 + (p + 1))
                steps.link(fn(lg[p], zb[p], ACT.Abs))
                steps.link(fn(lg[p], lg[p], ACT.Exp, scale=-1.0))
                fn(lg[p], lg[p], ACT.Ln, bias=one).then_inc(bl_ok, 1)
                act.wait_ge(bzr_ok, i * 2 + (p + 1))
                fn(wsb[p], zb[p], ACT.Exp).then_inc(bw_ok, 1)
                if more:
                    q_column(i * 2 + (p + 2), p, i * 2 + (p + 1))
                act.wait_ge(v_used, i * 16 + (4 + KGROUPS * (p + 1)))
                fn(om, PS[0:SBH, 4 + p, :], ACT.Copy).then_inc(bom_ok, 1)

            def sb_samples():
                for b in range(2):
                    q_column(b, b, None)
                count = NB // 2 - 1
                with act.Fori(0, count) as i:
                    steps.enter(i, 4)
                    for p in range(2):
                        sample(i, p, True)
                    steps.leave(count)
                for p in range(2):
                    sample(count, p, False)
                act.wait_ge(bf_done, NB)
                o = PS[:, NORM_BANK, 0:64].rearrange("p (j b c) -> p j b c", j=4, c=2)
                for c in range(2):
                    steps.link(fn(mix[64 * c:64 * c + 64, 0:4, SEQ:TOK], o[64 * c:64 * c + 64, :, :, c], ACT.Copy))

            units(units_setup())
            wait_tr(act, 16)
            norm(0, "mem")
            for l in range(2):
                g0 = GROUPS * l
                half = GROUPS // 2
                def x_from(n):
                    return (lambda k: act.wait_ge(dense_free[k % 2], (n + k) // 2 + 1)) if n is not None else None
                norm(l, "mix", x_from(g0 - 8 if l else None))
                if l:
                    act.wait_ge(mem_st, 32)
                for p in range(4):
                    for t in range(MT):
                        act.wait_ge(dense_done, g0 + 2 * p + t + 1)
                        dst = memK if p < 2 else memV
                        fn(dst[:, t, PCOL * (p % 2):PCOL * (p % 2) + PCOL], PS[:, 2 * t, 0:PCOL], ACT.Copy).then_inc(dense_free[t], 1)
                act.wait_ge(kss_ok, l + 1)
                steps.link(fn(s_kn, s_kn, ACT.Ln, scale=1.0 / P, bias=eps[:, 0:1]))
                fn(s_kn, s_kn, ACT.Exp, scale=-0.5).then_inc(kr_ok, 1)
                units(units_memk())
                for j in range(12):
                    act.wait_ge(dense_done, g0 + 8 + j + 1)
                    fn(zT[:, j, :].rearrange("p (c n) -> p c n", c=2), PS[:, 2 * (j % 2):2 * (j % 2) + 2, 0:HALF], ACT.Copy).then_inc(dense_free[j % 2], 1)
                for par in range(2):
                    act.wait_ge(dense_free[par], (g0 + 20) // 2)
                if l == 0:
                    gla()
                else:
                    units(units_sb())
                    sb_prompt()
                    sb_samples()
                for h in range(4):
                    norm(l, h)
                for h in range(4 + 1):
                    if h < 4:
                        act.wait_ge(mx_ok, 4 * l + h + 1)
                        for t in range(TT):
                            last = fn(pb[h % 2][:, t, :], PS[:, 2 * (h % 2) + t // 2, 256 * (t % 2):256 * (t % 2) + 256], ACT.Exp,
                                      scale=MSC, bias=s_mx(h % 2)[:, t:t + 1], accum_out=s_sum(h % 2)[:, t:t + 1])
                        last.then_inc(pe_ok, 1)
                    if h >= 1:
                        a = h - 1
                        units(units_probs(a))
                        act.wait_ge(po_done, 4 * l + a + 1)
                        fn(mix[:, 4 + a, 0:SEQ], PS[:, 2 * (a % 2), :], ACT.Copy).then_inc(po_out, 1)
                act.wait_ge(tr_done, pl.tr + 1)
                fn(s32[:, :], bank(pl.tr, 32, NMEM), ACT.Copy).then_inc(tr_out[0], 1)
                pl.tr += 2
                act.wait_ge(smx_ok, l + 1)
                fn(s32[:, :], s32[:, :], ACT.Exp, scale=MSC, bias=s_smx, accum_out=s_ssum).then_inc(sme_ok, 1)
                act.wait_ge(v_used, (4 + NB * KGROUPS if l else 0) + 4)
                fn(mix[:, 4:8, SEQ:TOK], PS[:, NORM_BANK, 0:32].rearrange("p (h b) -> p h b", h=4), ACT.Copy).then_inc(so_out, 1)
                norm(l, "ffn", x_from(g0 + 30))
                with act.Fori(0, NF // 2) as i:
                    for p in range(2):
                        f = i * 2 + p
                        act.wait_ge(dense_done, i * 4 + (g0 + 38 + 2 * p + 1))
                        fn(ext[p][:, 2:2 + TOK].rearrange("p (c n) -> p c n", c=2), PS[:, 0:2, 0:HALF], ACT.Copy).then_inc(ga_ok, 1)
                        fn(acc[p].rearrange("p (c n) -> p c n", c=2), PS[:, 0:2, 0:HALF], ACT.Identity,
                           scale=c_conv(l, 2, f), bias=c_conv(l, 3, f)).then_inc(dense_free[0], 1)
                        act.wait_ge(gc_ok, i * 2 + (l * NF + p + 1))
                        fn(sg[p], acc[p], ACT.Exp, scale=-1.0).then_inc(ge_ok, 1)
                units(units_tail())
            units(units_y())

        @block.vector
        def _(dve):
            pl = Place()
            steps = Steps(dve, dve_step)
            link = steps.link
            v = nc.vector
            stt, tt, ts = v.scalar_tensor_tensor, v.tensor_tensor, v.tensor_scalar

            def units(which):
                for u in which:
                    if pl.tr % 2 == 1:
                        dve.wait_ge(tr_done, pl.tr + 1)
                        dst, src = u(pl.tr)
                        v.tensor_copy(dst, src).then_inc(tr_out[1], 1)
                    pl.tr += 1

            def norm(l, what):
                srcs, _, gains, outs, w = norm_sources(l, what)
                dve.wait_ge(rstd_ok, pl.norm + 1)
                r = rstd[:, pl.norm % 2, 0:w]
                for k, src in enumerate(srcs):
                    if gains is None:
                        tt(src, src, r, ALU.mult).then_inc(applied, 1)
                    else:
                        stt(outs[k], src, gains[k], r, ALU.mult, ALU.mult).then_inc(applied, 1)
                pl.norm += 1

            def gla():
                for j in range(2):
                    dve.wait_ge(gu_done, j + 1)
                    ts(lb[:, j].rearrange("p (c n) -> p c n", c=2), PS[:, NORM_BANK:NORM_BANK + 2, 0:HALF], c_bg(j), None,
                       ALU.add).then_inc(gu_read, 1)
                    dve.wait_ge(gu_read, j + 1)
                    dve.wait_ge(ln_ok, j + 1)
                    link(stt(la[:, j], lb[:, j], 0.0, la[:, j], ALU.min, ALU.subtract))
                    v.tensor_tensor_scan(lb[:, j, 0:SEQ], keep[:, :], la[:, j, 0:SEQ], 0.0, ALU.mult, ALU.add)
                    link(v.tensor_copy(lb[:, j, SEQ:TOK], la[:, j, SEQ:TOK]))
                ch = lambda a: a[:, :, 0:SEQ].rearrange("p j (n c) -> p j n c", c=CH)
                v.tensor_copy(st[:, 0:1], lb[:, 0, 0:1]).then_inc(lb_ok, 1)
                tt(ch(ke), ch(lb)[:, :, :, CH - 1:CH].to_broadcast((P, 2, NCH, CH)), ch(lb), ALU.subtract).then_inc(ked_ok, 1)
                dve.wait_ge(kee_ok, 1)
                tt(ke[:, :, 0:SEQ], ke[:, :, 0:SEQ], zT[:, 2:4, 0:SEQ], ALU.mult).then_inc(ke_ok, 1)
                dve.wait_ge(ke_ok, 1)
                dve.wait_ge(eb_ok, 2)
                tt(zT[:, 2:4, 0:SEQ], zT[:, 2:4, 0:SEQ], la[:, :, 0:SEQ], ALU.mult)
                ts(zT[:, 0:2, SEQ:TOK], zT[:, 0:2, SEQ:TOK], GDK ** -0.5, None, ALU.mult)
                stt(zT[:, 0:2, 0:SEQ], zT[:, 0:2, 0:SEQ], GDK ** -0.5, eb[:, :, 0:SEQ], ALU.mult, ALU.mult).then_inc(qk_ok, 1)
                units(units_gla())
                wait_tr(dve, pl.tr)
                for b in range(NB):
                    last = ts(kdiag[:, b, :], ksT, ident[0:NB, b:b + 1], None, ALU.mult)
                last.then_inc(kdiag_ok, 1)
                dve.wait_ge(kv_done, 1)
                dve.wait_ge(ss_in, 64)
                for n in range(NCH):
                    kv = PS[:, n % 4, 256 * (n // 4):256 * (n // 4) + 256].rearrange("p (j v) -> p j v", j=2)
                    if n == 0:
                        link(v.tensor_copy(S[:, 0], kv))
                        continue
                    for j in range(2):
                        last = stt(S[:, n, j, :], S[:, n - 1, j, :], eb[:, j, CH * n + CH - 1:CH * n + CH], kv[:, j, :], ALU.mult, ALU.add)
                        if n < NCH - 1:
                            c = steps.mark(last)
                    if n < NCH - 1:
                        steps.wait(c)
                last.then_inc(s_ok, 1)
                dve.wait_ge(outer_done, 1)
                for b in range(NB):
                    for j in range(2):
                        last = stt(SS[:, b, j, :], SS[:, b, j, :], eb[:, j, SEQ + b:SEQ + b + 1],
                                   PS[:, b // 2, 256 * (b % 2) + P * j:256 * (b % 2) + P * j + P], ALU.mult, ALU.add)
                last.then_inc(ss_ok, 1)
                eg = scr[:, 0:4 * TOK].rearrange("p (h n) -> p h n", h=4)
                dve.wait_ge(eg_ok, 1)
                link(ts(eg, eg, 1.0, None, ALU.add))
                link(v.reciprocal(eg, eg))
                link(tt(eg, eg, zT[:, 4:8, :], ALU.mult))
                for h in range(4):
                    norm(h, "gla")
                    dve.wait_ge(applied, APPLIED[0][0] + h + 1)
                    link(tt(mix[:, h, :], mix[:, h, :], eg[:, h, :], ALU.mult))

            def prompt_z(h):
                dve.wait_ge(z_done, h + 1)
                if h >= 2:
                    dve.wait_ge(wr_ok, h - 1)
                ts(sbz[h % 2], PS[:, 0:3, :].rearrange("p a b -> p (a b)")[:, 0:SBW], SBD ** -0.5, sbb[:, h:h + 1], ALU.mult, ALU.add).then_inc(z_read, 1)
                dve.wait_ge(z_read, h + 1)
                dve.wait_ge(zl_ok, h + 1)
                stt(sbt[h % 2], sbz[h % 2], 0.0, sbt[h % 2], ALU.max, ALU.add).then_inc(spr_ok, 1)

            def sb_prompt():
                prompt_z(0)
                for h in range(SBH):
                    dve.wait_ge(r_done, h + 1)
                    tt(sbz[h % 2], sbz[h % 2], PS[:, 4:7, :].rearrange("p a b -> p (a b)")[:, 0:SBW], ALU.subtract).then_inc(zr_ok, 1)
                    if h + 1 < SBH:
                        prompt_z(h + 1)

            def sample(i, p):
                dve.wait_ge(bq_done, i * 2 + (p + 1))
                for g in range(KGROUPS):
                    dve.wait_ge(k_in[g % 2], i * 512 + (256 * p + 64 * (3 + g // 2)))
                    made = []
                    for c in range(2):
                        if g and c == 0:
                            steps.wait(reduced)
                        if g and c == 1:
                            dve.wait_ge(k_used, i * 16 + (4 + KGROUPS * p + g))
                        made.append(steps.mark(tt(prod[:, 2 * c:2 * c + 2, :], kring[:, g % 2, 2 * c:2 * c + 2, :],
                                                  PS[:, p:p + 1, :].to_broadcast((P, 2, 512)), ALU.mult)))
                    for c in range(2):
                        steps.wait(made[c])
                        o = 4 * g + 2 * c
                        last = v.tensor_reduce(zs[p][:, :, o:o + 2].rearrange("p h g -> p g h"),
                                               prod[:, 2 * c:2 * c + 2, :].rearrange("p a (h d) -> p a h d", h=SBH), AX.X, ALU.add)
                        if c == 0:
                            reduced = steps.mark(last)
                        else:
                            last.then_inc(k_used, 1)
                dve.wait_ge(k_used, i * 16 + (4 + KGROUPS * (p + 1)))
                stt(zb[p], zs[p], SBD ** -0.5, sbb[:, :].rearrange("p (h a) -> p h a", a=1).to_broadcast((P, SBH, PAGES)),
                    ALU.mult, ALU.add).then_inc(bz_ok, 1)
                dve.wait_ge(bz_ok, i * 2 + (p + 1))
                dve.wait_ge(bl_ok, i * 2 + (p + 1))
                link(stt(zs[p], zb[p], 0.0, lg[p], ALU.max, ALU.add))
                flat = lambda a: a.rearrange("p h g -> p (h g)")
                link(v.tensor_tensor_scan(flat(cs[p]), keepp[:, :, :].rearrange("p h g -> p (h g)"), flat(zs[p]), 0.0, ALU.mult, ALU.add))
                tt(cs[p], cs[p], zs[p], ALU.subtract).then_inc(bcs_ok, 1)
                dve.wait_ge(br_done, i * 2 + (p + 1))
                tt(flat(zb[p]), flat(zb[p]), PS[:, 2 + p, 0:256], ALU.subtract).then_inc(bzr_ok, 1)

            units(units_setup())
            wait_tr(dve, 16)
            norm(0, "mem")
            for l in range(2):
                g0 = GROUPS * l
                dve.wait_ge(applied, 8)
                for k in range(KD):
                    last = ts(memH[:, k, :], memR[:, k, :], c_mem(l, k), None, ALU.mult)
                last.then_inc(memh_ok, 1)
                if l:
                    dve.wait_ge(tail_st, 48)
                norm(l, "mix")
                for par in range(2):
                    dve.wait_ge(dense_free[par], g0 // 2 + 4)
                kk = memK[:, :, :].rearrange("p t (h d) -> p (t h) d", d=P)
                dve.wait_ge(bc_in, 32)
                link(tt(prod[:, 0:2, :], memK[:, :, :], memK[:, :, :], ALU.mult))
                v.tensor_reduce(s_kn, prod[:, 0:2, :].rearrange("p t (h d) -> p (t h) d", d=P), AX.X, ALU.add).then_inc(kss_ok, 1)
                dve.wait_ge(kr_ok, l + 1)
                link(tt(kk, kk, s_kn.rearrange("p (a b) -> p a b", b=1).to_broadcast((P, 8, P)), ALU.mult))
                tt(kk, kk, knorm[:, l:l + 1, :].to_broadcast((P, 8, P)), ALU.mult).then_inc(mk_ok, 1)
                units(units_memk())
                for q in range(10):
                    p, t = q // 5, q % 5
                    n = P if t < TT else NB
                    dve.wait_ge(dense_done, g0 + 20 + q + 1)
                    dst = vT[:, t, PCOL * p:PCOL * p + PCOL] if t < TT else vS[:, PCOL * p:PCOL * p + PCOL]
                    v.tensor_copy(dst, PS[0:n, 2 * (q % 2), 0:PCOL]).then_inc(dense_free[q % 2], 1)
                if l == 0:
                    gla()
                else:
                    units(units_sb())
                    sb_prompt()
                    with dve.Fori(0, NB // 2) as i:
                        steps.enter(i, 2 * (3 * KGROUPS + 2))
                        for p in range(2):
                            sample(i, p)
                        steps.leave(NB // 2)
                for h in range(4):
                    norm(l, h)
                for h in range(4 + 1):
                    if h < 4:
                        dve.wait_ge(sc_done, 4 * l + h + 1)
                        m = s_mx(h % 2)
                        link(v.tensor_reduce(m, PS[:, 2 * (h % 2):2 * (h % 2) + 2, :].rearrange("p a (b m) -> p (a b) m", b=2), AX.X, ALU.max))
                        ts(m, m, -MSC, None, ALU.mult).then_inc(mx_ok, 1)
                    if h >= 1:
                        a = h - 1
                        dve.wait_ge(pe_ok, 4 * l + a + 1)
                        link(v.reciprocal(s_sum(a % 2), s_sum(a % 2)))
                        for t in range(TT):
                            last = ts(pb[a % 2][:, t, :], pb[a % 2][:, t, :], s_sum(a % 2)[:, t:t + 1], None, ALU.mult)
                        last.then_inc(pn_ok, 1)
                        units(units_probs(a))
                n0 = 4 + NB * KGROUPS if l else 0
                for b in range(NB):
                    n = n0 + b // 2
                    dve.wait_ge(qb_done, NB * l + b + 1)
                    dve.wait_ge(k_in[n % 2], 64 * (n // 2 + 1))
                    pr = prod[:, 2 * (b % 2):2 * (b % 2) + 2, :]
                    tt(pr, kring[:, n % 2, 2 * (b % 2):2 * (b % 2) + 2, :],
                       PS[:, NORM_BANK + b % 2:NORM_BANK + b % 2 + 1, :].to_broadcast((P, 2, 512)), ALU.mult).then_inc(qb_read, 1)
                    dve.wait_ge(qb_read, NB * l + b + 1)
                    last = v.tensor_reduce(sm[:, :, b, :], pr.rearrange("p m (h d) -> p m h d", h=4), AX.X, ALU.add)
                    if b % 2:
                        last.then_inc(k_used, 1)
                pl.tr += 1
                dve.wait_ge(tr_out[0], pl.tr // 2 + 1)
                link(v.tensor_reduce(s_smx, s32[:, :], AX.X, ALU.max))
                ts(s_smx, s_smx, -MSC, None, ALU.mult).then_inc(smx_ok, 1)
                dve.wait_ge(sme_ok, l + 1)
                link(v.reciprocal(s_ssum, s_ssum))
                ts(s32[:, :], s32[:, :], s_ssum, None, ALU.mult).then_inc(smn_ok, 1)
                dve.wait_ge(tr_done, pl.tr + 1)
                v.tensor_copy(ps[:, :, :], bank(pl.tr, P, 64).rearrange("p (m c) -> p m c", m=MT)).then_inc(tr_out[1], 1)
                pl.tr += 1

                def add_to_residual(g):
                    for k in range(KD):
                        dve.wait_ge(dense_done, g + k + 1)
                        x = xT[:, k, :].rearrange("p (c n) -> p c n", c=2)
                        tt(x, x, PS[:, 2 * (k % 2):2 * (k % 2) + 2, 0:HALF], ALU.add).then_inc(dense_free[k % 2], 1)

                add_to_residual(g0 + 30)
                if l:
                    dve.wait_ge(kt_st, 64)
                norm(l, "ffn")
                for p in range(2):
                    v.memset(ext[p][:, 0:2], 0.0)
                tmp = scr[:, 3200:3200 + NF * NB].rearrange("p (f b) -> p f b", b=NB)
                taps = [cv[:, NC1 + l * NCC + t * NF:NC1 + l * NCC + t * NF + NF].rearrange("p (f a) -> p f a", a=1).to_broadcast((P, NF, NB))
                        for t in range(2)]
                pv = prev[:, l].rearrange("p f (b t) -> p f b t", t=2)
                link(tt(tmp, pv[:, :, :, 0], taps[0], ALU.mult))
                link(tt(pre[:, :, :], pv[:, :, :, 1], taps[1], ALU.mult))
                link(tt(pre[:, :, :], pre[:, :, :], tmp, ALU.add))
                with dve.Fori(0, NF // 2) as i:
                    steps.enter(i, 8)
                    for p in range(2):
                        f = i * 2 + p
                        done = i * 2 + (l * NF + p + 1)
                        dve.wait_ge(ga_ok, done)
                        dve.wait_ge(dense_free[0], i * 2 + (g0 // 2 + 19 + p + 1))
                        link(stt(acc[p][:, 0:SEQ], ext[p][:, 1:1 + SEQ], c_conv(l, 1, f), acc[p][:, 0:SEQ], ALU.mult, ALU.add))
                        tt(acc[p][:, SEQ:TOK], acc[p][:, SEQ:TOK], pre[:, bass.ds(f, 1), :].rearrange("p a b -> p (a b)"), ALU.add)
                        v.tensor_copy(tails[:, bass.ds(f, 1), :].rearrange("p a b -> p (a b)"), ext[p][:, SEQ:2 + TOK])
                        stt(acc[p][:, 0:SEQ], ext[p][:, 0:SEQ], c_conv(l, 0, f), acc[p][:, 0:SEQ], ALU.mult, ALU.add).then_inc(gc_ok, 1)
                        dve.wait_ge(gc_ok, done)
                        dve.wait_ge(ge_ok, done)
                        link(ts(sg[p], sg[p], 1.0, None, ALU.add))
                        link(v.reciprocal(sg[p], sg[p]))
                        link(tt(sg[p], sg[p], acc[p], ALU.mult))
                        dve.wait_ge(dense_done, i * 4 + (g0 + 38 + 2 * p + 2))
                        tt(big[:, bass.ds(f, 1), :].rearrange("p a (c n) -> p (a c) n", c=2), sg[p].rearrange("p (c n) -> p c n", c=2),
                           PS[:, 2:4, 0:HALF], ALU.mult).then_inc(dense_free[1], 1)
                    steps.leave(NF // 2)
                units(units_tail())
                add_to_residual(g0 + 82)
            units(units_y())


INS = ["x_prompt", "x_sample", "state_gla", "cache_sb_k", "cache_sb_v", "cache_mem_k", "cache_mem_v", "state_ffn_conv",
       "page_table", "mem_prompt", "norm_mix", "w_in_gla", "w_gate_up", "b_gate", "gla_out_norm", "w_in_sb", "sb_bias",
       "mem_norm", "w_mem_kv", "mem_q_norm", "mem_k_norm", "w_out", "norm_ffn", "w_ffn_up", "ffn_conv_w", "ffn_conv_b",
       "w_ffn_down"]
OUTS = [("y_p", (1, 512, 1024)), ("y_s", (8, 1, 1024)), ("gla_p", (1, 1, 4, 64, 128)), ("gla_s", (1, 8, 4, 64, 128)),
        ("sb_kp", (1, 1, 512, 8, 64)), ("sb_vp", (1, 1, 512, 8, 64)), ("sb_ks", (1, 8, 1, 8, 64)), ("sb_vs", (1, 8, 1, 8, 64)),
        ("mem_k", (2, 1, 256, 4, 128)), ("mem_v", (2, 1, 256, 4, 128)), ("conv_p", (2, 1, 2, 2816)), ("conv_s", (2, 8, 2, 2816))]


def kernel(**inputs):
    import concourse.bacc as bacc
    from concourse.bass_utils import run_bass_kernel_spmd

    nc = bacc.Bacc("TRN2", target_bir_lowering=False, num_devices=1)
    arrays, I, O = {}, {}, {}
    for name in INS:
        a = np.ascontiguousarray(inputs[name])
        arrays[name] = a
        I[name] = nc.dram_tensor(name, a.shape, mybir.dt.from_np(a.dtype), kind="ExternalInput").ap()
    for name, shape in OUTS:
        O[name] = nc.dram_tensor(name, shape, F32, kind="ExternalOutput").ap()
    build(nc, I, O)
    r = run_bass_kernel_spmd(nc, [arrays], core_ids=[0])
    return tuple(r.results[0][name] for name, _ in OUTS)
```

```python
import numpy as np
import concourse.bass as bass
from concourse import mybir
from contextlib import ExitStack

F32 = mybir.dt.float32
I32 = mybir.dt.int32
ACT = mybir.ActivationFunctionType
ALU = mybir.AluOpType
AX = mybir.AxisListType

P = 128
D = 1024
KD = D // P
SEQ, NB = 512, 8
TOK = SEQ + NB
HALF = TOK // 2
TT = SEQ // P
GR = 16
CH = 64
NCH = SEQ // CH
GDK, GDV = 64, 128
NMEM, MT = 256, 2
MW = 512
SBH, SBD = 8, 64
PAGES, PAGE = 32, 128
DFF = 2816
NF = DFF // P
PCOL = 256
EPS = 1e-6
TR_BANK, NORM_BANK = 4, 6
KGROUPS = PAGES // 4


class Steps:

    def __init__(self, eng, sem):
        self.eng, self.sem, self.n, self.extra = eng, sem, 0, 0

    def mark(self, ins):
        self.n += 1
        ins.then_inc(self.sem, 1)
        return self.n

    def wait(self, n):
        self.eng.wait_ge(self.sem, n + self.extra)

    def link(self, ins):
        self.wait(self.mark(ins))

    def enter(self, i, per):
        self.start, self.per, self.extra = self.n, per, i * per

    def leave(self, count):
        assert self.n - self.start == self.per, (self.n - self.start, self.per)
        self.n = self.start + self.per * count
        self.extra = 0


class Idx:

    def __init__(self, c, i=None, per=0):
        self.c, self.i, self.per = c, i, per

    def at(self, mult=1, add=0):
        n = self.c * mult + add
        return n if self.i is None else self.i * (self.per * mult) + n

    def one(self, add=0):
        return bass.ds(self.at(1, add), 1)


class Place:

    def __init__(self):
        self.panel = self.group = self.tr = self.norm = self.sq = 0


def build(nc, I, O):
    ctx = ExitStack()
    with ctx:
        def sb(name, shape, dt=F32):
            return ctx.enter_context(nc.sbuf_tensor(name, shape, dt))

        def sem(name):
            return ctx.enter_context(nc.semaphore(name))

        xT = sb("xT", [P, KD, TOK])
        hT = sb("hT", [P, KD, TOK])
        big = sb("big", [P, NF, TOK])
        zT = big[:, 0:12, :]
        mix = big[:, 12:20, :]
        vS = big[0:NB, 20, 0:512]
        vT = sb("vT", [P, TT, 512])
        vTf = vT[:, :, :].rearrange("p t n -> p (t n)")
        padded = vTf[:, 0:(2 * KD + NF) * 32]
        mixS, hS, actS = (padded[:, 32 * a:32 * b].rearrange("p (k c) -> p k c", c=32)
                          for a, b in ((0, KD), (KD, 2 * KD), (2 * KD, 2 * KD + NF)))
        accS = vTf[:, 1216:1216 + NF * NB].rearrange("p (f b) -> p f b", b=NB)
        sgS = vTf[:, 1392:1392 + NF * NB].rearrange("p (f b) -> p f b", b=NB)
        wring = sb("wring", [P, 2, 8, PCOL])
        kring = sb("kring", [P, 2, 4, 512])
        vring = sb("vring", [P, 2, 4, 512])
        memR = sb("memR", [P, KD, NMEM])
        prod = sb("prod", [P, 4, 512])
        rowsS = prod[:, 0:2, 0:PCOL]
        memH = prod[:, :, :].rearrange("p a (b c) -> p (a b) c", b=2)
        memK = sb("memK", [P, MT, 512])
        memKT = sb("memKT", [P, 4, NMEM])
        memV = sb("memV", [P, MT, 512])
        scr = sb("scr", [P, 5200])
        rstd = sb("rstd", [P, 2, TOK])
        sq = sb("sq", [P, 2, TOK])
        ident = sb("ident", [P, P])
        ones = sb("ones", [P, P])
        tri = sb("tri", [P, P])
        keep = sb("keep", [P, SEQ])
        sel = sb("sel", [P, SBH])
        selb = sb("selb", [P, NB])
        keepp = sb("keepp", [P, SBH, PAGES])
        cv = sb("cv", [P, 232])
        prev = sb("prev", [P, 2, NF, 2 * NB])
        pre = sb("pre", [P, NF, NB])
        tails = sb("tails", [P, NF, 2 + NB])
        eps = sb("eps", [P, 1])
        sbb = sb("sbb", [P, SBH])
        knorm = sb("knorm", [P, 2, P])
        wgd = sb("wgd", [P, KD, GR])
        wgu = sb("wgu", [GR, 256])
        gdT = sb("gdT", [GR, TOK])
        pt = sb("pt", [1, NB * PAGES], I32)
        st = sb("st", [P, 160])
        s32 = sb("s32", [32, NMEM])
        ps = sb("ps", [P, MT, 32])
        om = sq[:, 0, 0:512]
        qcol = sb("qcol", [P, 4])
        PS = ctx.enter_context(nc.psum_tensor("PS", [P, 8, 512], F32))

        c_mix = lambda l, k: cv[:, 8 * l + k:8 * l + k + 1]
        c_ffn = lambda l, k: cv[:, 16 + 8 * l + k:17 + 8 * l + k]
        c_mem = lambda l, k: cv[:, 32 + 8 * l + k:33 + 8 * l + k]
        c_bg = lambda j: cv[:, 48 + j:49 + j]
        c_on = cv[:, 50:51]
        c_qn = lambda l: cv[:, 51 + l:52 + l]
        NC1 = 53
        NCC = 4 * NF

        def c_conv(l, t, f):
            return cv[:, f.one(NC1 + l * NCC + t * NF)]

        memtok = scr[:, 0:2048].rearrange("p (t n) -> p t n", t=2)
        xs = scr[0:NB, 2048:3072]
        rows1 = scr[0:NC1, 3072:3200]
        rows2 = [scr[0:NCC, 3200 + 128 * l:3328 + 128 * l] for l in range(2)]
        xtok = hT[:, :, :].rearrange("p a b -> p (a b)")[:, 0:4096].rearrange("p (t n) -> p t n", t=4)
        bigf = big[:, :, :].rearrange("p a b -> p (a b)")
        prows = [bigf[0:2 * NB, DFF * l:DFF * (l + 1)] for l in range(2)]
        la = scr[:, 0:1040].rearrange("p (j n) -> p j n", j=2)
        lb = scr[:, 1040:2080].rearrange("p (j n) -> p j n", j=2)
        eb = scr[:, 2080:3120].rearrange("p (j n) -> p j n", j=2)
        ke = scr[:, 3120:4160].rearrange("p (j n) -> p j n", j=2)
        hTf = hT[:, :, :].rearrange("p a b -> p (a b)")
        keT = hTf[:, 0:1024].rearrange("p (j t n) -> p j t n", j=2, t=4)
        att = hTf[:, 1024:3072].rearrange("p (h t n) -> p h t n", h=4, t=4)
        ksT = hTf[0:NB, 3072:3328]
        krf = kring[:, :, :, :].rearrange("p a b c -> p (a b c)")
        S = krf[:, 0:2048].rearrange("p (n j v) -> p n j v", n=8, j=2)
        SS = krf[:, 2048:4096].rearrange("p (b j v) -> p b j v", b=8, j=2)
        kdiag = vring[0:NB, 0, :, :].rearrange("p a b -> p (a b)").rearrange("p (b n) -> p b n", b=8)
        ktok = hTf[:, 0:2048].rearrange("p (t n) -> p t n", t=4)
        kstok = hTf[0:NB, 2048:2560]
        tailr = hTf[0:2 + NB, 0:DFF]
        ytok = bigf[:, 0:4096].rearrange("p (t n) -> p t n", t=4)
        ystok = bigf[0:NB, 4096:5120]
        SBO = {0: 0, 1: 512, 3: 896, 2: 1024}
        SBW = 1280
        sbt = [scr[:, 2560 * p:2560 * p + SBW] for p in range(2)]
        sbz = [scr[:, 2560 * p + SBW:2560 * p + 2 * SBW] for p in range(2)]
        def s5(k):
            return scr[:, 3400 + 256 * k:3656 + 256 * k]
        zs, zb, lg, cs = (s5(k).rearrange("p (h g) -> p h g", h=SBH) for k in range(4))
        sp_s = s5(4).rearrange("p (h g) -> p h g", h=SBH)
        wsb = s5(5).rearrange("p (g c) -> p g c", c=32)
        pb = [scr[:, 1024 * p:1024 * p + 1024].rearrange("p (t m) -> p t m", t=4) for p in range(2)]
        pT = [scr[:, 2048 + 1024 * p:3072 + 1024 * p].rearrange("p (m n) -> p m n", m=2) for p in range(2)]
        sm = scr[:, 5000:5064].rearrange("p (m b h) -> p m b h", m=2, b=NB)
        ext = [scr[:, 522 * p:522 * p + 522] for p in range(2)]
        acc = [scr[:, 1044 + 520 * p:1564 + 520 * p] for p in range(2)]
        sg = [scr[:, 2084 + 520 * p:2604 + 520 * p] for p in range(2)]

        x_in, mem_in, row_in, bc_in = sem("x_in"), sem("mem_in"), sem("row_in"), sem("bc_in")
        gd_in, pt_in, ss_in = sem("gd_in"), sem("pt_in"), sem("ss_in")
        w_in = [sem("w_in0"), sem("w_in1")]
        part_done = sem("part_done")
        s_in = [sem(f"s_in{n}") for n in range(6)]
        k_in = [sem("k_in0"), sem("k_in1")]
        v_in = [sem("v_in0"), sem("v_in1")]
        k_used, v_used = sem("k_used"), sem("v_used")
        const_ok = sem("const_ok")
        dense_done = sem("dense_done")
        dense_free = [sem("dense_free0"), sem("dense_free1")]
        tr_done = sem("tr_done")
        tr_out = [sem("tr_out_act"), sem("tr_out_dve")]
        sq_ok, sq_used, rstd_ok, applied = (sem(n) for n in ("sq_ok", "sq_used", "rstd_ok", "norm_applied"))
        act_step, dve_step, pool_step = sem("act_step"), sem("dve_step"), sem("pool_step")
        memh_ok = sem("memh_ok")
        kss_ok, kr_ok, mk_ok = sem("kss_ok"), sem("kr_ok"), sem("mk_ok")
        gd_done, gd_ok, gu_done, gu_read = (sem(n) for n in ("gd_done", "gd_ok", "gu_done", "gu_read"))
        ln_ok, lb_ok, eb_ok, ked_ok, kee_ok, qk_ok, ke_ok = (sem(n) for n in ("ln_ok", "lb_ok", "eb_ok", "ked_ok", "kee_ok", "qk_ok", "ke_ok"))
        att_done, att_out, att_ok = sem("att_done"), sem("att_out"), sem("att_ok")
        kv_done, s_ok, kdiag_ok, outer_done, ss_ok = (sem(n) for n in ("kv_done", "s_ok", "kdiag_ok", "outer_done", "ss_ok"))
        o_done, os_done, o_ok = sem("o_done"), sem("os_done"), sem("o_ok")
        eg_ok, gla_ok = sem("eg_ok"), sem("gla_ok")
        sc_done, mx_ok, pe_ok, pn_ok, po_done, po_out = (sem(n) for n in ("sc_done", "mx_ok", "pexp_ok", "pn_ok", "po_done", "po_out"))
        qb_done, qb_read, sm_ok, smx_ok, sme_ok, smn_ok, so_done, so_out = (
            sem(n) for n in ("qb_done", "qb_read", "sm_ok", "smx_ok", "sme_ok", "smn_ok", "so_done", "so_out"))
        z_done, z_read, zl_ok, spr_ok, sp_ok, r_done, zr_ok, wr_ok, w_ok, sbo_done, sbo_out = (
            sem(n) for n in ("z_done", "z_read", "zl_ok", "spr_ok", "sp_ok", "r_done", "zr_ok", "wr_ok", "w_ok", "sbo_done", "sbo_out"))
        bq_done, bk_done, bz_ok, bl_ok, bcs_ok, br_done, bzr_ok, bw_ok, bo_done, bom_ok, bf_done, qcol_ok = (
            sem(n) for n in ("bq_done", "bk_done", "bz_ok", "bl_ok", "bcs_ok", "br_done", "bzr_ok", "bw_ok", "bo_done", "bom_ok", "bf_done", "qcol_ok"))
        bs_out = sem("bs_out")
        s_read, s_rows_ok, s_sum_done, s_x_ok, s_tails_ok, s_acc_ok, s_silu_ok, s_act_ok = (
            sem(n) for n in ("s_read", "s_rows_ok", "s_sum_done", "s_x_ok", "s_tails_ok", "s_acc_ok", "s_silu_ok", "s_act_ok"))
        ga_ok, ge_ok, gc_ok, act_ok, pre_ok = (sem(n) for n in ("ga_ok", "ge_ok", "gc_ok", "act_ok", "pre_ok"))
        state_st, mem_st, kt_st, tail_st, y_st = (sem(n) for n in ("state_st", "mem_st", "kt_st", "tail_st", "y_st"))

        GIN = {0: [0, 256, 1024, 1280, 1552, 1808], 1: [0, 256, 512, 768, 1536, 1792]}
        GV = {0: [512, 768], 1: [1024, 1280]}
        GROUPS = 90
        w_main = {0: I["w_in_gla"], 1: I["w_in_sb"]}

        def kw(ap2):
            return ap2.rearrange("(k p) n -> p k n", p=P)

        FULL, PROMPT, SAMPLES = (0, TOK), (0, SEQ), (SEQ, NB)

        def parts(cols):
            c0, w = cols
            return [(0, c0, w)] if w == NB else [(c, c0 + w // 2 * c, w // 2) for c in range(2)]

        def pair(par, cols):
            w = cols[1]
            return PS[:, 2 * par, 0:NB] if w == NB else PS[:, 2 * par:2 * par + 2, 0:w // 2]

        def as_pair(ap, cols):
            return ap if cols[1] == NB else ap.rearrange("p (c n) -> p c n", c=2)

        def tile_cols(t, k, cols):
            return t[:, k, cols[0]:cols[0] + cols[1]]

        def up_count(l, cols):
            return NF * (l + (1 if cols == SAMPLES else 0))

        def up_groups(l, cols):
            return GROUPS * l + 38 + (60 if cols == SAMPLES else 0)

        UP0, DOWN0, PANELS = 16, 16 + NF, 16 + NF + 12

        def w_ready(l, n):
            ups = min(max(0, (n - UP0) // 2 + 1), NF // 2)
            return 16 * (l * (PANELS // 2 + NF // 2) + n // 2 + 1 + ups)

        sring = [wring[:, 0], wring[:, 1]] + [t[:, s].rearrange("p a (b n) -> p (a b) n", b=2) for t in (kring, vring) for s in range(2)]
        SUP, SDOWN, SLOTS = 4, 4 + NF, 6

        def s_ready(n):
            return 16 * sum(2 if SUP <= m < SDOWN else 1 for m in range(n % SLOTS, n + 1, SLOTS))

        S_GROUPS = 4 + NF + 4

        def s_group_panels(g):
            return g + 1 if g < SDOWN else SDOWN + 3 * (g - SDOWN + 1)

        def wait_panel(eng, n):
            l, n = n // PANELS, n % PANELS
            if n < 10:
                c = 2 * n + 2
            elif n < 12:
                c = 20 + 5 * (n - 9)
            elif n < DOWN0:
                c = 30 + 2 * (n - 11)
            elif (n - DOWN0) % 3 < 2:
                u = n - DOWN0
                eng.wait_ge(part_done, 8 * l + 2 * (u // 3) + u % 3 + 1)
                return
            else:
                c = 82 + 2 * ((n - DOWN0) // 3 + 1)
            eng.wait_ge(dense_done, GROUPS * l + c)

        APPLIED = [[16, 24, 32], [40, 44, 52, 60]]
        TRN = {"setup": 16, "ktok": 16 + 22 + 2 + 6, "y_p": 62, "tail": [16 + 22, 70], "y_s": 72}

        def wait_tr(eng, n):
            eng.wait_ge(tr_out[0], n // 2)
            eng.wait_ge(tr_out[1], n // 2)

        block = ctx.enter_context(nc.Block())

        @block.sync
        def _(sp):
            pl = Place()

            def panel(src):
                n, s = pl.panel, pl.panel % 2
                if n >= 2:
                    wait_panel(sp, n - 2)
                sp.dma_start(wring[:, s, 0:src.shape[1], 0:src.shape[2]], src).then_inc(w_in[s], 16)
                pl.panel += 1

            sp.dma_start(xtok, I["x_prompt"][0].rearrange("(t p) n -> p t n", p=P)).then_inc(x_in, 16)
            sp.dma_start(xs, I["x_sample"].rearrange("b s n -> (b s) n")).then_inc(x_in, 16)
            sp.dma_start(memtok, I["mem_prompt"][0].rearrange("(t p) n -> p t n", p=P)).then_inc(mem_in, 16)
            nr = 0
            for name, o, n in (("norm_mix", 0, 16), ("norm_ffn", 16, 16), ("mem_norm", 32, 16), ("b_gate", 48, 2),
                               ("gla_out_norm", 50, 1), ("mem_q_norm", 51, 2)):
                sp.dma_start(rows1[o:o + n, :], I[name].rearrange("l (k p) -> (l k) p", p=P)).then_inc(row_in, 16)
                nr += 1
            for l in range(2):
                sp.dma_start(rows2[l][0:3 * NF, :], I["ffn_conv_w"][l].rearrange("t (f p) -> (t f) p", p=P)).then_inc(row_in, 16)
                sp.dma_start(rows2[l][3 * NF:4 * NF, :], I["ffn_conv_b"][l].rearrange("(f p) -> f p", p=P)).then_inc(row_in, 16)
                sp.dma_start(prows[l], I["state_ffn_conv"][l].rearrange("b t f -> (b t) f")).then_inc(row_in, 16)
            sp.dma_start(knorm[:, :, :], I["mem_k_norm"].rearrange("(a l) d -> a l d", a=1).to_broadcast((P, 2, P))).then_inc(bc_in, 16)
            sp.dma_start(sbb[:, :], I["sb_bias"].to_broadcast((P, SBH))).then_inc(bc_in, 16)
            sp.dma_start(wgd[:, :, :], kw(I["w_in_gla"][0])[:, :, 1536:1536 + GR]).then_inc(gd_in, 16)
            sp.dma_start(wgu[:, :], I["w_gate_up"][0]).then_inc(gd_in, 16)
            sp.dma_start(pt[:, :], I["page_table"].rearrange("(a b) n -> a (b n)", a=1)).then_inc(pt_in, 16)
            for hh in range(2):
                for j in range(2):
                    sp.dma_start(SS[64 * hh:64 * hh + 64, :, j, :],
                                 I["state_gla"][0, :, 2 * j + hh].rearrange("b k v -> k b v")).then_inc(ss_in, 16)

            def mem_groups(l, n0):
                kk, vv = (kring, k_used, k_in, "cache_mem_k"), (vring, v_used, v_in, "cache_mem_v")
                for g, (ring, used, in_, cache) in ((0, kk), (1, kk), (0, vv), (1, vv), (2, kk), (3, kk), (2, vv), (3, vv)):
                    n = n0 + g
                    if n >= 2:
                        sp.wait_ge(used, n - 1)
                    for bb in range(2):
                        for mt in range(2):
                            sp.dma_start(ring[:, g % 2, 2 * bb + mt, :],
                                         I[cache][l, 2 * g + bb, P * mt:P * mt + P].rearrange("m h d -> m (h d)")).then_inc(in_[g % 2], 16)

            def pages(cache, ring, in_, b, g):
                for jj in range(4):
                    page = sp.value_load(pt[0:1, bass.ds(b.at(PAGES, PAGES - 1 - 4 * g - jj), 1)], min_val=0,
                                         max_val=I[cache].shape[1] - 1)
                    sp.dma_start(ring[:, g % 2, jj, :],
                                 I[cache][0, bass.ds(page, 1)].rearrange("a p h d -> (a p) (h d)")).then_inc(in_[g % 2], 16)

            def kv_pages(b, p, k, v, v2):
                if k:
                    for g in (2 * p, 2 * p + 1):
                        sp.wait_ge(k_used, b.at(8, 3 + g))
                        pages("cache_sb_k", kring, k_in, b, g)
                if p and v:
                    s, gs = Idx(b.c - 1, b.i, b.per), (2 * p - 2, 2 * p - 1)
                elif not p and v2:
                    s, gs = Idx(b.c - 2, b.i, b.per), (6, 7)
                else:
                    return
                for g in gs:
                    sp.wait_ge(v_used, s.at(8, 3 + g))
                    pages("cache_sb_v", vring, v_in, s, g)

            for l in range(2):
                wm = kw(w_main[l][0])
                wkv = kw(I["w_mem_kv"][l])
                for p in range(4):
                    panel(wkv[:, :, PCOL * p:PCOL * p + PCOL])
                for c in GIN[l] + GV[l]:
                    panel(wm[:, :, c:c + PCOL])
                wo = kw(I["w_out"][l])
                wu = I["w_ffn_up"][l].rearrange("(k p) (c f n) -> p k c f n", p=P, c=2, n=P)
                wd = I["w_ffn_down"][l].rearrange("(k p) n -> p k n", p=P)

                def out_panel(p):
                    panel(wo[:, :, PCOL * p:PCOL * p + PCOL])

                def up_panel(s, f):
                    for c in range(2):
                        sp.dma_start(wring[:, s, :, P * c:P * c + P], wu[:, :, c, f.one(), :].rearrange("p k a n -> p k (a n)")).then_inc(w_in[s], 16)

                def down_panel(u):
                    kc = u % 3
                    nk = 8 if kc < 2 else 6
                    panel(wd[:, 8 * kc:8 * kc + nk, PCOL * (u // 3):PCOL * (u // 3) + PCOL])

                def samples_panel(n, f=None, place=None):
                    s = n % SLOTS
                    dst = sring[s]
                    if n < SUP:
                        sp.dma_start(dst, wo[:, :, PCOL * n:PCOL * n + PCOL]).then_inc(s_in[s], 16)
                    elif n < SDOWN:
                        for c in range(2):
                            sp.dma_start(dst[:, :, P * c:P * c + P], wu[:, :, c, f.one(), :].rearrange("p k a n -> p k (a n)")).then_inc(s_in[s], 16)
                    else:
                        kc, m = (n - SDOWN) % 3, (n - SDOWN) // 3
                        nk = 8 if kc < 2 else 6
                        sp.dma_start(dst[:, 0:nk, :], wd[:, 8 * kc:8 * kc + nk, PCOL * m:PCOL * m + PCOL]).then_inc(s_in[s], 16)

                out_panel(0)
                if l == 0:
                    out_panel(1)
                    sp.wait_ge(s_ok, 1)
                    sp.wait_ge(ss_ok, 1)
                    for hh in range(2):
                        for j in range(2):
                            sp.dma_start(O["gla_p"][0, 0, 2 * j + hh], S[64 * hh:64 * hh + 64, 7, j, :]).then_inc(state_st, 16)
                            sp.dma_start(O["gla_s"][0, :, 2 * j + hh].rearrange("b k v -> k b v"),
                                         SS[64 * hh:64 * hh + 64, :, j, :]).then_inc(state_st, 16)
                    sp.wait_ge(state_st, 8 * 16)
                    sp.wait_ge(os_done, 1)
                    mem_groups(0, 0)
                    for p in range(2, 4):
                        out_panel(p)
                    with sp.Fori(0, NF // 2) as i:
                        for s in range(2):
                            sp.wait_ge(dense_done, i * 4 + (36 + 2 * s))
                            up_panel(s, Idx(s, i, 2))
                    pl.panel += NF
                    for u in range(12):
                        down_panel(u)
                else:
                    sp.wait_ge(pt_in, 16)
                    for p in range(4):
                        kv_pages(Idx(0), p, True, False, False)
                        if p < 3:
                            out_panel(p + 1)
                        else:
                            sp.wait_ge(dense_done, GROUPS + 36)
                            up_panel(0, Idx(0))
                            pl.panel += 1
                    for b, i in ((1, None), (2, 4)):
                        def up_block(b, f0):
                            for p in range(4):
                                kv_pages(b, p, True, True, b.c > 1)
                                f = Idx(f0.c + p + 1, f0.i, f0.per)
                                sp.wait_ge(dense_done, f.at(2, GROUPS + 38 - 2))
                                up_panel((p + 1) % 2, f)
                        if i is None:
                            up_block(Idx(1), Idx(0))
                        else:
                            with sp.Fori(0, 4) as j:
                                up_block(Idx(2, j, 1), Idx(4, j, 4))
                    sp.wait_ge(dense_done, GROUPS + 38 + 40)
                    up_panel(1, Idx(21))
                    pl.panel += NF - 1
                    down_panel(0)
                    for b in range(6, 9):
                        for p in range(4):
                            kv_pages(Idx(b), p, b < NB, True, True)
                            u = 4 * (b - 6) + p + 1
                            if u < 12:
                                down_panel(u)
                    for g in (6, 7):
                        sp.wait_ge(v_used, 3 + 8 * 7 + g)
                        pages("cache_sb_v", vring, v_in, Idx(7), g)
                    for n in range(2):
                        wait_panel(sp, 2 * PANELS - 2 + n)
                        samples_panel(n)
                    n0 = 4 + NB * KGROUPS
                    mem_groups(1, n0)
                    for n in range(2, 6):
                        sp.wait_ge(k_used if n < 4 else v_used, n0 + 3 + n % 2)
                        samples_panel(n, Idx(n - SUP))
                    with sp.Fori(0, 3) as i:
                        for s in range(SLOTS):
                            sp.wait_ge(s_read, i * SLOTS + (s + 1))
                            samples_panel(SLOTS + s, Idx(2 + s, i, SLOTS))
                    for n in range(24, SDOWN + 12):
                        sp.wait_ge(s_read, n - SLOTS + 1)
                        samples_panel(n, Idx(n - SUP))
            sp.wait_ge(state_st, 8 * 16)

        @block.gpsimd
        def _(pool):
            steps = Steps(pool, pool_step)
            nc.gpsimd.memset(ident[:, :], 0.0).then_inc(pool_step, 1)
            nc.gpsimd.memset(ones[:, :], 1.0).then_inc(pool_step, 1)
            nc.gpsimd.memset(tri[:, :], 1.0).then_inc(pool_step, 1)
            nc.gpsimd.memset(keep[:, :], 1.0).then_inc(pool_step, 1)
            nc.gpsimd.memset(keepp[:, :, :], 1.0).then_inc(pool_step, 1)
            nc.gpsimd.memset(eps[:, :], EPS).then_inc(pool_step, 1)
            nc.gpsimd.memset(sel[:, :], 0.0).then_inc(pool_step, 1)
            nc.gpsimd.memset(selb[:, :], 0.0).then_inc(pool_step, 1)
            steps.n = 8
            pool.wait_ge(pool_step, 8)
            af = nc.gpsimd.affine_select
            af(out=ident[:, :], in_=ident[:, :], compare_op=ALU.not_equal, fill=1.0, base=0, pattern=[[-1, P]], channel_multiplier=1).then_inc(const_ok, 1)
            af(out=tri[:, :], in_=tri[:, :], compare_op=ALU.is_ge, fill=0.0, base=0, pattern=[[-1, P]], channel_multiplier=1).then_inc(const_ok, 1)
            af(out=keep[:, :], in_=keep[:, :], compare_op=ALU.not_equal, fill=0.0, base=0, pattern=[[0, NCH], [1, CH]], channel_multiplier=0).then_inc(const_ok, 1)
            af(out=keepp[:, :, :], in_=keepp[:, :, :], compare_op=ALU.not_equal, fill=0.0, base=0, pattern=[[0, SBH], [1, PAGES]], channel_multiplier=0).then_inc(const_ok, 1)

            for j in range(4):
                steps.link(af(out=sel[:, :], in_=sel[:, :], compare_op=ALU.not_equal, fill=1.0, base=-(32 + 8) * j, pattern=[[-1, SBH]],
                              channel_multiplier=1))
                steps.link(af(out=selb[:, :], in_=selb[:, :], compare_op=ALU.not_equal, fill=1.0, base=-32 * j, pattern=[[-1, NB]],
                              channel_multiplier=1))
            nc.gpsimd.memset(st[:, 100:101], 0.0).then_inc(const_ok, 1)

            for l in range(2):
                pool.wait_ge(mk_ok, l + 1)
                pool.dma_start(O["mem_k"][l, 0].rearrange("(t p) h d -> p t (h d)", p=P), memK[:, :, :]).then_inc(mem_st, 16)
                pool.dma_start(O["mem_v"][l, 0].rearrange("(t p) h d -> p t (h d)", p=P), memV[:, :, :]).then_inc(mem_st, 16)
                if l == 0:
                    for h in range(4):
                        pool.wait_ge(att_out, h + 1)
                        steps.link(af(out=att[:, h], in_=att[:, h], compare_op=ALU.is_ge, fill=0.0, base=0,
                                      pattern=[[0, TT], [1, P]], channel_multiplier=-1))
                        af(out=att[:, h].rearrange("p t (c n) -> p t c n", c=2), in_=att[:, h].rearrange("p t (c n) -> p t c n", c=2),
                           compare_op=ALU.is_ge, fill=0.0, base=0, pattern=[[0, TT], [-CH, 2], [0, CH]], channel_multiplier=1).then_inc(att_ok, 1)
                else:
                    for h in range(SBH):
                        for ready, done in ((spr_ok, sp_ok), (wr_ok, w_ok)):
                            pool.wait_ge(ready, h + 1)
                            for kc in range(TT):
                                blk = sbt[h % 2][:, SBO[kc]:SBO[kc] + P]
                                af(out=blk, in_=blk, compare_op=ALU.is_gt, fill=0.0, base=0, pattern=[[1, P]],
                                   channel_multiplier=-1).then_inc(done, 1)
                    wait_tr(pool, TRN["ktok"])
                    pool.wait_ge(dense_free[0], (GROUPS + 30) // 2)
                    pool.wait_ge(dense_free[1], (GROUPS + 30) // 2)
                    flat = lambda ap: ap.rearrange("t h d -> t (h d)")
                    pool.dma_start(flat(O["sb_kp"][0, 0]).rearrange("(t p) n -> p t n", p=P), ktok).then_inc(kt_st, 16)
                    pool.dma_start(flat(O["sb_vp"][0, 0]).rearrange("(t p) n -> p t n", p=P), vT[:, :, :]).then_inc(kt_st, 16)
                    pool.dma_start(O["sb_ks"][0].rearrange("b s h d -> (b s) (h d)"), kstok).then_inc(kt_st, 16)
                    pool.dma_start(O["sb_vs"][0].rearrange("b s h d -> (b s) (h d)"), vS).then_inc(kt_st, 16)
                    wait_tr(pool, TRN["y_p"])
                    pool.dma_start(O["y_p"][0].rearrange("(t p) n -> p t n", p=P), ytok).then_inc(y_st, 16)
                wait_tr(pool, TRN["tail"][l])
                pool.dma_start(O["conv_p"][l, 0], tailr[0:2, :]).then_inc(tail_st, 16)
                pool.dma_start(O["conv_s"][l, :, 1, :], tailr[2:2 + NB, :]).then_inc(tail_st, 16)
                pool.dma_start(O["conv_s"][l, :, 0, :], I["state_ffn_conv"][l, :, 1, :]).then_inc(tail_st, 16)
            wait_tr(pool, TRN["y_s"])
            pool.dma_start(O["y_s"].rearrange("b s n -> (b s) n"), ystok).then_inc(y_st, 16)
            pool.wait_ge(mem_st, 64)
            pool.wait_ge(kt_st, 64)
            pool.wait_ge(tail_st, 96)
            pool.wait_ge(y_st, 32)

        @block.tensor
        def _(pe):
            pl = Place()
            mm, tp = nc.tensor.matmul, nc.tensor.transpose

            def tr_unit(parts):
                n = pl.tr
                if n >= 2:
                    pe.wait_ge(tr_out[n % 2], n // 2)
                for c, src in parts:
                    k, m = src.shape[0], src.shape[1]
                    last = tp(PS[0:m, TR_BANK + n % 2, c:c + k], src, ident[0:k, 0:k])
                last.then_inc(tr_done, 1)
                pl.tr += 1

            def norm_sums(nk, width=TOK):
                if pl.norm:
                    pe.wait_ge(rstd_ok, pl.norm)
                w = width // 2
                for k in range(nk):
                    pe.wait_ge(sq_ok, pl.sq + 1)
                    for c in range(2):
                        last = mm(PS[:, NORM_BANK + c, 0:w], ones[:, :], sq[:, pl.sq % 2, w * c:w * c + w],
                                  start=(k == 0), stop=(k == nk - 1))
                    last.then_inc(sq_used, 1)
                    pl.sq += 1
                pl.norm += 1

            def dense_group(w, par, nk, src, k0, first, last_, cols):
                for k in range(nk):
                    for c, o, n in parts(cols):
                        last = mm(PS[:, 2 * par + c, 0:n], w[:, k, P * par:P * par + P], src[:, k0 + k, o:o + n],
                                  start=(first and k == 0), stop=(last_ and k == nk - 1))
                return last

            def free(par):
                if pl.group >= 2:
                    pe.wait_ge(dense_free[par], pl.group // 2)

            def in_panel(l, n):
                pe.wait_ge(w_in[n % 2], w_ready(l, n))

            def fm_panel(l, n, src, cols=FULL, between=(None, None)):
                w = wring[:, n % 2]
                in_panel(l, n)
                for m in range(2):
                    free(m)
                    dense_group(w, m, 8, src, 0, True, True, cols).then_inc(dense_done, 1)
                    pl.group += 1
                    if between[m]:
                        between[m]()

            def gla():
                pe.wait_ge(gd_ok, 1)
                for j in range(2):
                    if j:
                        pe.wait_ge(gu_read, 1)
                    for c in range(2):
                        last = mm(PS[:, NORM_BANK + c, 0:HALF], wgu[:, P * j:P * j + P], gdT[:, HALF * c:HALF * c + HALF],
                                  start=True, stop=True)
                    last.then_inc(gu_done, 1)
                pe.wait_ge(qk_ok, 1)
                for h in range(4):
                    j, r = h // 2, 64 * (h % 2)
                    for t in range(TT):
                        last = mm(PS[:, h, P * t:P * t + P], zT[r:r + 64, 2 + j, P * t:P * t + P],
                                  zT[r:r + 64, j, P * t:P * t + P], start=True, stop=True)
                    last.then_inc(att_done, 1)
                for j in range(2):
                    tr_unit([(P * t, ke[:, j, P * t:P * t + P]) for t in range(TT)])
                for j in range(2):
                    tr_unit([(0, zT[:, 2 + j, SEQ:TOK])])
                pe.wait_ge(att_out, 4)
                wait_tr(pe, pl.tr)
                for n in range(NCH):
                    t, r = n // 2, 64 * (n % 2)
                    for h in range(4):
                        j, o = h // 2, 64 * (h % 2)
                        c = 256 * (n // 4) + P * j
                        last = mm(PS[o:o + 64, n % 4, c:c + P], keT[r:r + 64, j, t, o:o + 64],
                                  vT[r:r + 64, t, P * h:P * h + P], start=True, stop=True)
                last.then_inc(kv_done, 1)
                pe.wait_ge(s_ok, 1)
                pe.wait_ge(kdiag_ok, 1)
                for b in range(NB):
                    for h in range(4):
                        j, o = h // 2, 64 * (h % 2)
                        c = 256 * (b % 2) + P * j
                        last = mm(PS[o:o + 64, b // 2, c:c + P], kdiag[:, b, 64 * h:64 * h + 64],
                                  vS[:, P * h:P * h + P], start=True, stop=True)
                last.then_inc(outer_done, 1)
                pe.wait_ge(ss_ok, 1)
                for h in range(4):
                    j, r = h // 2, 64 * (h % 2)
                    pe.wait_ge(att_ok, h + 1)
                    for t in range(TT):
                        last = mm(PS[:, h, P * t:P * t + P], vT[:, t, P * h:P * h + P], att[:, h, t, :], start=True, stop=False)
                        for n in (2 * t, 2 * t + 1):
                            if n:
                                last = mm(PS[:, h, CH * n:CH * n + CH], S[r:r + 64, n - 1, j, :],
                                          zT[r:r + 64, j, CH * n:CH * n + CH], start=False, stop=(n == 2 * t + 1))
                    last.then_inc(o_done, 1)
                for h in range(4):
                    j, r = h // 2, 64 * (h % 2)
                    for b in range(NB):
                        last = mm(PS[:, NORM_BANK + h % 2, NB * j + b:NB * j + b + 1], SS[r:r + 64, b, j, :],
                                  zT[r:r + 64, j, SEQ + b:SEQ + b + 1], start=True, stop=True)
                last.then_inc(os_done, 1)

            PSf = PS[:, :, :].rearrange("p a b -> p (a b)")

            def sb_prompt():
                for t in range(TT):
                    tr_unit([(P * j, zT[:, 4 + j, P * t:P * t + P]) for j in range(4)])
                for a in range(2):
                    tr_unit([(P * c, zT[:, 4 + 2 * a + c, SEQ:TOK]) for c in range(2)])

                def scores(h):
                    j, r = h // 2, 64 * (h % 2)
                    if h:
                        pe.wait_ge(z_read, h)
                    for kc in range(TT):
                        w = SEQ - P * kc
                        last = mm(PSf[:, SBO[kc]:SBO[kc] + w], zT[r:r + 64, 4 + j, P * kc:P * kc + P],
                                  zT[r:r + 64, j, P * kc:SEQ], start=True, stop=True)
                    last.then_inc(z_done, 1)

                scores(0)
                wait_tr(pe, pl.tr)
                for h in range(SBH):
                    x = sbt[h % 2]
                    pe.wait_ge(sp_ok, 4 * h + 4)
                    if h:
                        pe.wait_ge(zr_ok, h)
                    for kc in range(TT):
                        w = SEQ - P * kc
                        o = 2048 + SBO[kc]
                        last = mm(PSf[:, o:o + w], tri[:, :], x[:, SBO[kc]:SBO[kc] + w], start=True, stop=(kc == TT - 1))
                        for k2 in range(kc + 1, TT):
                            w2 = SEQ - P * k2
                            last = mm(PSf[:, o + P * (k2 - kc):o + P * (k2 - kc) + w2], ones[:, :],
                                      x[:, SBO[k2]:SBO[k2] + w2], start=False, stop=(k2 == TT - 1))
                    last.then_inc(r_done, 1)
                    if h + 1 < SBH:
                        scores(h + 1)
                    pe.wait_ge(w_ok, 4 * h + 4)
                    if h >= 2 and h % 2 == 0:
                        pe.wait_ge(sbo_out, h // 2)
                    r = 64 * (h % 2)
                    for kc in range(TT):
                        w = SEQ - P * kc
                        last = mm(PS[r:r + 64, 3, P * kc:SEQ], vT[:, kc, SBD * h:SBD * h + SBD],
                                  x[:, SBO[kc]:SBO[kc] + w], start=(kc == 0), stop=(kc == TT - 1))
                    last.then_inc(sbo_done, 1)

            def q_rows(b, first=False):
                pe.wait_ge(qcol_ok, b.at(1, 1))
                if not first:
                    pe.wait_ge(k_used, b.at(8, 4))
                for j in range(4):
                    last = mm(PS[:, 4, P * j:P * j + P], qcol[:, j:j + 1].to_broadcast((P, P)), ident[:, :], start=True, stop=True)
                last.then_inc(bq_done, 1)

            def key_sums(b):
                pe.wait_ge(bcs_ok, b.at(1, 1))
                mm(PS[:, 7, 64:320], tri[:, :], sp_s.rearrange("p h g -> p (h g)"), start=True, stop=False)
                mm(PS[:, 7, 64:320], ones[:, :], cs.rearrange("p h g -> p (h g)"), start=False, stop=True).then_inc(br_done, 1)

            def v_group(b, g):
                if g == 0:
                    pe.wait_ge(bw_ok, b.at(1, 1))
                pe.wait_ge(v_in[g % 2], b.at(256, 64 * (3 + g // 2)))
                for jj in range(4):
                    last = mm(PS[32 * jj:32 * jj + 32, 6, :], wsb[:, g, :], vring[:, g % 2, jj, :],
                              start=(g == 0), stop=(g == KGROUPS - 1))
                last.then_inc(v_used, 1)

            def head_columns(b):
                pe.wait_ge(bom_ok, b.at(1, 1))
                for j in range(4):
                    last = mm(PS[:, 7, bass.ds(b.at(2, 16 * j), 2)], om[:, P * j:P * j + P], sel[:, 2 * j:2 * j + 2], start=True, stop=True)
                last.then_inc(bf_done, 1)

            def block(b, panels, k, v, v2):
                s1, s2 = Idx(b.c - 1, b.i, b.per), Idx(b.c - 2, b.i, b.per)
                if k:
                    q_rows(b, first=not v)
                for p in range(4):
                    if p:
                        fs = [(lambda g=2 * p - 2 + m: v_group(s1, g)) if v else None for m in range(2)]
                    else:
                        fs = [(lambda g=6 + m: v_group(s2, g)) if v2 else None for m in range(2)]
                    panels[p](fs)
                    if p == 0 and v:
                        key_sums(s1)
                    if p == 1 and v2:
                        head_columns(s2)

            def mem_prompt(l):
                for h in range(4 + 1):
                    if h < 4:
                        pe.wait_ge(applied, APPLIED[l][1] - 3 + h)
                        if h == 0:
                            wait_tr(pe, pl.tr)
                        if h >= 2:
                            pe.wait_ge(po_out, 4 * l + h - 1)
                        for t in range(TT):
                            last = mm(PS[:, 2 * (h % 2) + t // 2, 256 * (t % 2):256 * (t % 2) + 256],
                                      zT[:, 8 + h, P * t:P * t + P], memKT[:, h, :], start=True, stop=True)
                        last.then_inc(sc_done, 1)
                    if h >= 1:
                        a = h - 1
                        pe.wait_ge(pn_ok, 4 * l + a + 1)
                        for mt in range(MT):
                            tr_unit([(P * t, pb[a % 2][:, t, P * mt:P * mt + P]) for t in range(TT)])
                        for mt in range(MT):
                            pe.wait_ge(tr_out[mt], pl.tr // 2)
                            last = mm(PS[:, 2 * (a % 2), :], memV[:, mt, P * a:P * a + P], pT[a % 2][:, mt, :],
                                      start=(mt == 0), stop=(mt == MT - 1))
                        last.then_inc(po_done, 1)

            def mem_samples(l):
                pe.wait_ge(rstd_ok, pl.norm)
                for b in range(NB):
                    if b >= 2:
                        pe.wait_ge(qb_read, 8 * l + b - 1)
                    for h in range(4):
                        last = mm(PS[:, NORM_BANK + b % 2, P * h:P * h + P], zT[:, 8 + h, SEQ + b:SEQ + b + 1].to_broadcast((P, P)),
                                  ident[:, :], start=True, stop=True)
                    last.then_inc(qb_done, 1)
                n0 = 4 + NB * KGROUPS if l else 0
                pe.wait_ge(k_used, n0 + 4)
                tr_unit([(P * mt, sm[:, mt].rearrange("p b h -> p (b h)")) for mt in range(MT)])
                pe.wait_ge(smn_ok, l + 1)
                tr_unit([(32 * mt, s32[:, P * mt:P * mt + P]) for mt in range(MT)])
                pe.wait_ge(tr_out[1], pl.tr // 2)
                for g in range(4):
                    n = n0 + g
                    pe.wait_ge(v_in[g % 2], 64 * (n // 2 + 1))
                    for bb in range(2):
                        b = 2 * g + bb
                        for h in range(4):
                            for mt in range(MT):
                                last = mm(PS[:, NORM_BANK, 8 * h + b:8 * h + b + 1], vring[:, g % 2, 2 * bb + mt, P * h:P * h + P],
                                          ps[:, mt, 4 * b + h:4 * b + h + 1], start=(mt == 0), stop=(mt == MT - 1))
                    last.then_inc(v_used, 1)
                pe.wait_ge(so_out, l + 1)

            def up_panel(l, f, cols, between=(None, None)):
                g0 = up_groups(l, cols)
                w, c = wring[:, f.c % 2], w_ready(l, UP0 + f.c)
                pe.wait_ge(w_in[f.c % 2], c if f.i is None else f.i * (16 * f.per) + c)
                for m in range(2):
                    pe.wait_ge(dense_free[m], f.at(1, g0 // 2))
                    dense_group(w, m, 8, hT, 0, True, True, cols).then_inc(dense_done, 1)
                    if between[m]:
                        between[m]()

            def down_panel(l, u, cols, i=None, between=(None, None)):
                m, kc, s = u // 3, u % 3, u % 2
                g0 = up_groups(l, cols) + 2 * NF
                w = wring[:, s]
                pe.wait_ge(w_in[s], w_ready(l, DOWN0 + u) if i is None else i * 48 + w_ready(l, DOWN0 + u))
                for par in range(2):
                    if kc == 0:
                        pe.wait_ge(dense_free[par], i * 2 + (g0 // 2 + m) if i is not None else g0 // 2 + m)
                    last = dense_group(w, par, 8 if kc < 2 else 6, big, 8 * kc, kc == 0, kc == 2, cols)
                    if kc == 2:
                        last.then_inc(dense_done, 1)
                    elif par:
                        last.then_inc(part_done, 1)
                    if between[par]:
                        between[par]()

            def tail(l, cols):
                for p in range(4):
                    fm_panel(l, 12 + p, mix, cols)
                norm_sums(KD, cols[1])
                pe.wait_ge(applied, APPLIED[l][2])
                with pe.Fori(0, NF // 2) as i:
                    for s in range(2):
                        up_panel(l, Idx(s, i, 2), cols)
                pl.group += 2 * NF
                pe.wait_ge(dense_free[1], pl.group // 2)
                conv_rows()
                with pe.Fori(0, 2) as i:
                    for u in range(6):
                        down_panel(l, u, cols, i)
                pl.group += 8

            def samples_rows(g, src, panel):
                nk = src.shape[1]
                for j in range((nk + 7) // 8):
                    w = panel(j)
                    for k in range(8 * j, min(nk, 8 * j + 8)):
                        last = mm(PS[32 * (k % 4):32 * (k % 4) + 32, 2 * (g % 2), 0:PCOL], src[:, k, :], w[:, k - 8 * j, :],
                                  start=(k < 4), stop=(k >= nk - 4))
                    last.then_inc(s_read, 1)

            def samples_sum(g, halves):
                pe.wait_ge(s_rows_ok, g.at(1, 1))
                for c, out in enumerate(halves):
                    last = mm(out, rowsS[:, g.c % 2, P * c:P * c + P], selb[:, :], start=True, stop=True)
                last.then_inc(s_sum_done, 1)

            def samples_tail():
                def panel(n, i=None):
                    pe.wait_ge(s_in[n % SLOTS], s_ready(n) if i is None else i * 32 + s_ready(n))
                    return sring[n % SLOTS]

                tile = lambda k: PS[:, 1, NB * k:NB * k + NB]
                for g in range(4):
                    samples_rows(g, mixS, lambda j: panel(g))
                    if g:
                        samples_sum(Idx(g - 1), [tile(2 * g - 2), tile(2 * g - 1)])
                samples_sum(Idx(3), [tile(6), tile(7)])
                norm_sums(KD, NB)
                pe.wait_ge(applied, APPLIED[1][3])

                def up(f, first=False):
                    samples_rows(f.c, hS, lambda j: panel(SUP + f.c, f.i))
                    if not first:
                        up_sum(Idx(f.c - 1, f.i, f.per))

                def up_sum(f):
                    samples_sum(Idx(4 + f.c, f.i, f.per),
                                [PS[:, 3, bass.ds(f.at(NB, 256 * c), NB)] for c in range(2)])

                up(Idx(0), first=True)
                up(Idx(1))
                with pe.Fori(0, 3) as i:
                    for s in range(SLOTS):
                        up(Idx(2 + s, i, SLOTS))
                for f in range(20, NF):
                    up(Idx(f))
                up_sum(Idx(NF - 1))
                pe.wait_ge(s_act_ok, 1)
                for m in range(4):
                    samples_rows(SDOWN + m, actS, lambda j: panel(SDOWN + 3 * m + j))
                    if m == 0:
                        pe.wait_ge(s_tails_ok, 1)
                        conv_rows()
                    else:
                        samples_sum(Idx(SDOWN + m - 1), [tile(2 * m - 2), tile(2 * m - 1)])
                samples_sum(Idx(SDOWN + 3), [tile(6), tile(7)])

            def conv_rows():
                for q in range(6):
                    tr_unit([(P * a, tails[:, 4 * q + a, :]) for a in range(4) if 4 * q + a < NF])

            pe.wait_ge(const_ok, 5)
            pe.wait_ge(row_in, 12 * 16)
            tr_unit([(0, rows1), (NC1, rows2[0]), (NC1 + NCC, rows2[1])])
            for l in range(2):
                tr_unit([(16 * f, prows[l][:, P * f:P * f + P]) for f in range(NF)])
            pe.wait_ge(x_in, 32)
            tr_unit([(NB * k, xs[:, P * k:P * k + P]) for k in range(KD)])
            for k in range(KD):
                tr_unit([(P * t, xtok[:, t, P * k:P * k + P]) for t in range(TT)])
            pe.wait_ge(mem_in, 16)
            for k in range(0, KD, 2):
                tr_unit([(256 * a + P * t, memtok[:, t, P * (k + a):P * (k + a) + P]) for a in range(2) for t in range(2)])
            norm_sums(KD, NMEM)

            for l in range(2):
                norm_sums(KD)
                pe.wait_ge(memh_ok, l + 1)
                for p in range(4):
                    in_panel(l, p)
                    for t in range(MT):
                        free(t)
                        for k in range(KD):
                            last = mm(PS[:, 2 * t, 0:PCOL], memH[:, k, P * t:P * t + P], wring[:, p % 2, k, :],
                                      start=(k == 0), stop=(k == KD - 1))
                        last.then_inc(dense_done, 1)
                        pl.group += 1
                pe.wait_ge(mk_ok, l + 1)
                for a in range(2):
                    tr_unit([(256 * c + P * t, memK[:, t, P * (2 * a + c):P * (2 * a + c) + P]) for c in range(2) for t in range(2)])
                pe.wait_ge(applied, APPLIED[l][0])
                for p in range(6):
                    fm_panel(l, 4 + p, hT)
                if l == 0:
                    pe.wait_ge(gd_in, 32)
                    pe.wait_ge(rstd_ok, pl.norm)
                    for k in range(KD):
                        for c in range(2):
                            last = mm(PS[0:GR, NORM_BANK + c, 0:HALF], wgd[:, k, :], hT[:, k, HALF * c:HALF * c + HALF],
                                      start=(k == 0), stop=(k == KD - 1))
                    last.then_inc(gd_done, 1)
                for p in range(2):
                    in_panel(l, 10 + p)
                    for t in range(TT + 1):
                        n = P if t < TT else NB
                        free(pl.group % 2)
                        for k in range(KD):
                            last = mm(PS[0:n, 2 * (pl.group % 2), 0:PCOL], hT[:, k, P * t:P * t + n], wring[:, p, k, :],
                                      start=(k == 0), stop=(k == KD - 1))
                        last.then_inc(dense_done, 1)
                        pl.group += 1
                for par in range(2):
                    pe.wait_ge(dense_free[par], pl.group // 2)
                if l == 0:
                    gla()
                    for h in range(4):
                        norm_sums(1)
                else:
                    sb_prompt()
                for h in range(4):
                    norm_sums(1)
                mem_prompt(l)
                if l == 0:
                    pe.wait_ge(po_out, 4)
                    mem_samples(0)
                    tail(0, FULL)
                    continue
                pe.wait_ge(po_out, 8)
                wait_tr(pe, pl.tr)
                out = [lambda fs, p=p: fm_panel(1, 12 + p, mix, PROMPT, fs) for p in range(4)]
                block(Idx(0), out, True, False, False)
                norm_sums(KD, SEQ)
                pe.wait_ge(applied, APPLIED[1][2])
                pe.wait_ge(rstd_ok, pl.norm)
                ups = lambda f0: [lambda fs, p=p: up_panel(1, Idx(f0.c + p, f0.i, f0.per), PROMPT, fs) for p in range(4)]
                block(Idx(1), ups(Idx(0)), True, True, False)
                with pe.Fori(0, 4) as i:
                    block(Idx(2, i, 1), ups(Idx(4, i, 4)), True, True, True)
                for f in (20, 21):
                    up_panel(1, Idx(f), PROMPT)
                pl.group += 2 * NF
                pe.wait_ge(dense_free[1], pl.group // 2)
                for b in range(6, 9):
                    downs = [lambda fs, u=4 * (b - 6) + p: down_panel(1, u, PROMPT, None, fs) for p in range(4)]
                    block(Idx(b), downs, b < NB, True, True)
                pl.group += 8
                for g in (6, 7):
                    v_group(Idx(7), g)
                head_columns(Idx(7))
                for par in range(2):
                    pe.wait_ge(dense_free[par], pl.group // 2)
                for t in range(TT):
                    for q in range(2):
                        tr_unit([(P * a, xT[:, 4 * q + a, P * t:P * t + P]) for a in range(4)])
                pe.wait_ge(bs_out, 2)
                mem_samples(1)
                samples_tail()
            pe.wait_ge(s_x_ok, 2)
            for q in range(2):
                tr_unit([(P * a, xT[:, 4 * q + a, SEQ:TOK]) for a in range(4)])

        def bank(n, rows, cols):
            return PS[0:rows, TR_BANK + n % 2, 0:cols]

        def units_setup():
            yield lambda n: (cv[:, 0:NC1 + 2 * NCC], bank(n, P, NC1 + 2 * NCC))
            for l in range(2):
                yield lambda n, l=l: (prev[:, l], bank(n, P, 16 * NF).rearrange("p (f x) -> p f x", x=16))
            yield lambda n: (xT[:, :, SEQ:TOK], bank(n, P, NB * KD).rearrange("p (k b) -> p k b", b=NB))
            for k in range(KD):
                yield lambda n, k=k: (xT[:, k, 0:SEQ], bank(n, P, SEQ))
            for q in range(4):
                yield lambda n, q=q: (memR[:, 2 * q:2 * q + 2, :], bank(n, P, 512).rearrange("p (a m) -> p a m", a=2))

        def units_memk():
            for a in range(2):
                yield lambda n, a=a: (memKT[:, 2 * a:2 * a + 2, :], bank(n, P, 512).rearrange("p (a m) -> p a m", a=2))

        def units_gla():
            for j in range(2):
                yield lambda n, j=j: (keT[:, j], bank(n, P, 512).rearrange("p (t m) -> p t m", t=TT))
            for j in range(2):
                yield lambda n, j=j: (ksT[:, P * j:P * j + P], bank(n, NB, P))

        def units_sb():
            for t in range(TT):
                yield lambda n, t=t: (ktok[:, t, :], bank(n, P, 512))
            for a in range(2):
                yield lambda n, a=a: (kstok[:, 256 * a:256 * a + 256], bank(n, NB, 256))

        def units_probs(h):
            for mt in range(MT):
                yield lambda n, mt=mt: (pT[h % 2][:, mt, :], bank(n, P, SEQ))

        def units_tail():
            for q in range(6):
                w = 512 if q < 5 else 256
                yield lambda n, q=q, w=w: (tailr[:, 512 * q:512 * q + w], bank(n, 2 + NB, w))

        def units_y():
            for t in range(TT):
                for q in range(2):
                    yield lambda n, t=t, q=q: (ytok[:, t, 512 * q:512 * q + 512], bank(n, P, 512))

        def units_ys():
            for q in range(2):
                yield lambda n, q=q: (ystok[:, 512 * q:512 * q + 512], bank(n, NB, 512))

        s_mx = lambda p: st[:, 8 * p:8 * p + 4]
        s_sum = lambda p: st[:, 16 + 8 * p:20 + 8 * p]
        s_kn = st[:, 32:40]
        s_smx, s_ssum = st[0:32, 48:49], st[0:32, 49:50]
        MSC = float(P) ** -0.5
        one = ones[:, 0:1]

        def norm_sources(l, what, cols=FULL):
            if what == "mem":
                return [memR[:, k, :] for k in range(KD)], D, None, None, NMEM
            if what == "mix":
                return [xT[:, k, :] for k in range(KD)], D, [c_mix(l, k) for k in range(KD)], [hT[:, k, :] for k in range(KD)], TOK
            if what == "ffn":
                return ([tile_cols(xT, k, cols) for k in range(KD)], D, [c_ffn(l, k) for k in range(KD)],
                        [hS[:, k, 0:NB] if cols == SAMPLES else tile_cols(hT, k, cols) for k in range(KD)], cols[1])
            if what == "gla":
                return [mix[:, l, :]], GDV, [c_on], [mix[:, l, :]], TOK
            return [zT[:, 8 + what, :]], P, [c_qn(l)], [zT[:, 8 + what, :]], TOK

        @block.scalar
        def _(act):
            pl = Place()
            steps = Steps(act, act_step)
            fn = nc.scalar.activation

            def units(which):
                for u in which:
                    if pl.tr % 2 == 0:
                        act.wait_ge(tr_done, pl.tr + 1)
                        dst, src = u(pl.tr)
                        fn(dst, src, ACT.Copy).then_inc(tr_out[0], 1)
                    pl.tr += 1

            def norm(l, what, ready=None, cols=FULL):
                srcs, n, _, _, w = norm_sources(l, what, cols)
                for k, src in enumerate(srcs):
                    if ready:
                        ready(k)
                    if pl.sq >= 2:
                        act.wait_ge(sq_used, pl.sq - 1)
                    fn(sq[:, pl.sq % 2, 0:w], src, ACT.Square).then_inc(sq_ok, 1)
                    pl.sq += 1
                act.wait_ge(sq_used, pl.sq)
                if pl.norm >= 2:
                    act.wait_ge(applied, pl.applied[-2])
                r = rstd[:, pl.norm % 2, 0:w]
                steps.link(fn(r.rearrange("p (c n) -> p c n", c=2), PS[:, NORM_BANK:NORM_BANK + 2, 0:w // 2], ACT.Ln,
                              scale=1.0 / n, bias=eps[:, 0:1]))
                fn(r, r, ACT.Exp, scale=-0.5).then_inc(rstd_ok, 1)
                pl.norm += 1
                pl.applied.append(pl.applied[-1] + len(srcs))

            pl.applied = [0]

            def gla():
                act.wait_ge(gd_done, 1)
                fn(gdT[:, :].rearrange("p (c n) -> p c n", c=2), PS[0:GR, NORM_BANK:NORM_BANK + 2, 0:HALF], ACT.Copy).then_inc(gd_ok, 1)
                for j in range(2):
                    act.wait_ge(gu_read, j + 1)
                    steps.link(fn(la[:, j], lb[:, j], ACT.Abs))
                    steps.link(fn(la[:, j], la[:, j], ACT.Exp, scale=-1.0))
                    fn(la[:, j], la[:, j], ACT.Ln, bias=one).then_inc(ln_ok, 1)
                act.wait_ge(lb_ok, 1)
                fn(eb, lb, ACT.Exp, scale=1.0 / 16).then_inc(eb_ok, 1)
                fn(la, lb, ACT.Exp, scale=-1.0 / 16).then_inc(eb_ok, 1)
                act.wait_ge(ked_ok, 1)
                fn(ke[:, :, 0:SEQ], ke[:, :, 0:SEQ], ACT.Exp, scale=1.0 / 16).then_inc(kee_ok, 1)
                for h in range(4):
                    act.wait_ge(att_done, h + 1)
                    fn(att[:, h], PS[:, h, :].rearrange("p (t n) -> p t n", t=TT), ACT.Copy).then_inc(att_out, 1)
                units(units_gla())
                act.wait_ge(qk_ok, 1)
                fn(scr[:, 0:4 * TOK].rearrange("p (h n) -> p h n", h=4), zT[:, 4:8, :], ACT.Silu).then_inc(eg_ok, 1)
                for h in range(4):
                    act.wait_ge(o_done, h + 1)
                    steps.link(fn(mix[:, h, 0:SEQ], PS[:, h, :], ACT.Copy))
                act.wait_ge(os_done, 1)
                for a in range(2):
                    steps.link(fn(mix[:, a:4:2, SEQ:TOK], PS[:, NORM_BANK + a, 0:16].rearrange("p (j b) -> p j b", j=2), ACT.Copy))
                for h in range(4):
                    norm(h, "gla")

            def softplus_prompt(h):
                act.wait_ge(z_read, h + 1)
                if h >= 2:
                    act.wait_ge(sbo_done, h - 1)
                x = sbt[h % 2]
                steps.link(fn(x, sbz[h % 2], ACT.Abs))
                steps.link(fn(x, x, ACT.Exp, scale=-1.0))
                fn(x, x, ACT.Ln, bias=one).then_inc(zl_ok, 1)

            def sb_prompt():
                softplus_prompt(0)
                for h in range(SBH):
                    act.wait_ge(zr_ok, h + 1)
                    fn(sbt[h % 2], sbz[h % 2], ACT.Exp).then_inc(wr_ok, 1)
                    if h + 1 < SBH:
                        softplus_prompt(h + 1)
                    if h % 2:
                        act.wait_ge(sbo_done, h + 1)
                        fn(mix[:, h // 2, 0:SEQ], PS[:, 3, :], ACT.Copy).then_inc(sbo_out, 1)

            def q_column(b, first=False):
                if not first:
                    act.wait_ge(bq_done, b.at(1, 0))
                fn(qcol[:, :], zT[:, 0:4, b.one(SEQ)].rearrange("p j a -> p (j a)"), ACT.Copy).then_inc(qcol_ok, 1)

            def softplus(b):
                act.wait_ge(bz_ok, b.at(1, 1))
                steps.link(fn(lg, zb, ACT.Abs))
                steps.link(fn(lg, lg, ACT.Exp, scale=-1.0))
                fn(lg, lg, ACT.Ln, bias=one).then_inc(bl_ok, 1)

            def weights(b):
                act.wait_ge(bzr_ok, b.at(1, 1))
                fn(wsb.rearrange("p g (a h) -> p h (g a)", h=SBH), zb, ACT.Exp).then_inc(bw_ok, 1)

            def rows(b):
                act.wait_ge(v_used, b.at(8, 4 + KGROUPS))
                fn(om, PS[:, 6, :], ACT.Copy).then_inc(bom_ok, 1)

            def block(b, panels, k, v, v2):
                s1, s2 = Idx(b.c - 1, b.i, b.per), Idx(b.c - 2, b.i, b.per)
                if v:
                    softplus(s1)
                for p in range(4):
                    panels[p]()
                    if p == 0:
                        if v2:
                            rows(s2)
                        if v:
                            weights(s1)
                    if p == 1 and k == 2:
                        q_column(Idx(b.c + 1, b.i, b.per))

            def up_evac(l, f, p, cols):
                g0, w = up_groups(l, cols), cols[1]
                act.wait_ge(dense_done, f.at(2, g0 + 1))
                fn(as_pair(ext[p][:, 2:2 + w], cols), pair(0, cols), ACT.Copy).then_inc(ga_ok, 1)
                fn(as_pair(acc[p][:, 0:w], cols), pair(0, cols), ACT.Identity, scale=c_conv(l, 2, f), bias=c_conv(l, 3, f)).then_inc(dense_free[0], 1)
                act.wait_ge(gc_ok, f.at(1, up_count(l, cols) + 1))
                fn(sg[p][:, 0:w], acc[p][:, 0:w], ACT.Silu).then_inc(ge_ok, 1)

            def x_from(n):
                return (lambda k: act.wait_ge(dense_free[k % 2], (n + k) // 2 + 1)) if n is not None else None

            def mem_samples(l):
                act.wait_ge(tr_done, pl.tr + 1)
                fn(s32[:, :], bank(pl.tr, 32, NMEM), ACT.Copy).then_inc(tr_out[0], 1)
                pl.tr += 2
                act.wait_ge(smx_ok, l + 1)
                fn(s32[:, :], s32[:, :], ACT.Exp, scale=MSC, bias=s_smx, accum_out=s_ssum).then_inc(sme_ok, 1)
                act.wait_ge(v_used, (4 + NB * KGROUPS if l else 0) + 4)
                fn(mixS[:, 4:8, 0:NB] if l else mix[:, 4:8, SEQ:TOK], PS[:, NORM_BANK, 0:32].rearrange("p (h b) -> p h b", h=4), ACT.Copy).then_inc(so_out, 1)

            def tail(l, cols):
                norm(l, "ffn", x_from(up_groups(l, cols) - 8), cols)
                with act.Fori(0, NF // 2) as i:
                    for p in range(2):
                        up_evac(l, Idx(p, i, 2), p, cols)
                units(units_tail())

            def samples_rows(g):
                act.wait_ge(s_read, s_group_panels(g.c) if g.i is None else g.at(1, 1))
                if g.i is not None or g.c >= 2:
                    act.wait_ge(s_sum_done, g.at(1, -1))
                fn(rowsS[:, g.c % 2, :], PS[:, 2 * (g.c % 2), 0:PCOL], ACT.Copy).then_inc(s_rows_ok, 1)

            def samples_tail():
                for g in range(4):
                    samples_rows(Idx(g))
                norm(1, "ffn", lambda k: act.wait_ge(s_x_ok, 1), SAMPLES)
                with act.Fori(0, NF // 2) as i:
                    for p in range(2):
                        samples_rows(Idx(4 + p, i, 2))
                act.wait_ge(s_acc_ok, 1)
                fn(sgS, accS, ACT.Silu).then_inc(s_silu_ok, 1)
                samples_rows(Idx(SDOWN))
                units(units_tail())
                for m in range(1, 4):
                    samples_rows(Idx(SDOWN + m))

            units(units_setup())
            wait_tr(act, 16)
            norm(0, "mem")
            for l in range(2):
                g0 = GROUPS * l
                half = GROUPS // 2
                norm(l, "mix", x_from(g0 - 8 if l else None))
                if l:
                    act.wait_ge(mem_st, 32)
                for p in range(4):
                    for t in range(MT):
                        act.wait_ge(dense_done, g0 + 2 * p + t + 1)
                        dst = memK if p < 2 else memV
                        fn(dst[:, t, PCOL * (p % 2):PCOL * (p % 2) + PCOL], PS[:, 2 * t, 0:PCOL], ACT.Copy).then_inc(dense_free[t], 1)
                act.wait_ge(kss_ok, l + 1)
                steps.link(fn(s_kn, s_kn, ACT.Ln, scale=1.0 / P, bias=eps[:, 0:1]))
                fn(s_kn, s_kn, ACT.Exp, scale=-0.5).then_inc(kr_ok, 1)
                units(units_memk())
                for j in range(12):
                    act.wait_ge(dense_done, g0 + 8 + j + 1)
                    fn(zT[:, j, :].rearrange("p (c n) -> p c n", c=2), PS[:, 2 * (j % 2):2 * (j % 2) + 2, 0:HALF], ACT.Copy).then_inc(dense_free[j % 2], 1)
                for par in range(2):
                    act.wait_ge(dense_free[par], (g0 + 20) // 2)
                if l == 0:
                    gla()
                else:
                    units(units_sb())
                    sb_prompt()
                    q_column(Idx(0), first=True)
                for h in range(4):
                    norm(l, h)
                for h in range(4 + 1):
                    if h < 4:
                        act.wait_ge(mx_ok, 4 * l + h + 1)
                        for t in range(TT):
                            last = fn(pb[h % 2][:, t, :], PS[:, 2 * (h % 2) + t // 2, 256 * (t % 2):256 * (t % 2) + 256], ACT.Exp,
                                      scale=MSC, bias=s_mx(h % 2)[:, t:t + 1], accum_out=s_sum(h % 2)[:, t:t + 1])
                        last.then_inc(pe_ok, 1)
                    if h >= 1:
                        a = h - 1
                        units(units_probs(a))
                        act.wait_ge(po_done, 4 * l + a + 1)
                        fn(mix[:, 4 + a, 0:SEQ], PS[:, 2 * (a % 2), :], ACT.Copy).then_inc(po_out, 1)
                if l == 0:
                    mem_samples(0)
                    tail(0, FULL)
                    continue
                none = [lambda: None] * 4
                block(Idx(0), none, 2, False, False)
                norm(1, "ffn", x_from(up_groups(1, PROMPT) - 8), PROMPT)
                ups = lambda f0: [lambda p=p: up_evac(1, Idx(f0.c + p, f0.i, f0.per), p % 2, PROMPT) for p in range(4)]
                block(Idx(1), ups(Idx(0)), 2, True, False)
                with act.Fori(0, 4) as i:
                    steps.enter(i, 2)
                    block(Idx(2, i, 1), ups(Idx(4, i, 4)), 2, True, True)
                    steps.leave(4)
                for f in (20, 21):
                    up_evac(1, Idx(f), f % 2, PROMPT)
                for b in range(6, 9):
                    block(Idx(b), none, 2 if b < 7 else 0, True, True)
                rows(Idx(7))
                act.wait_ge(bf_done, NB)
                o = PS[:, 7, 0:64].rearrange("p (j b c) -> p j b c", j=4, c=2)
                for c in range(2):
                    fn(mixS[64 * c:64 * c + 64, 0:4, 0:NB], o[64 * c:64 * c + 64, :, :, c], ACT.Copy).then_inc(bs_out, 1)
                units(units_y())
                mem_samples(1)
                samples_tail()
            units(units_ys())

        @block.vector
        def _(dve):
            pl = Place()
            steps = Steps(dve, dve_step)
            link = steps.link
            v = nc.vector
            stt, tt, ts = v.scalar_tensor_tensor, v.tensor_tensor, v.tensor_scalar

            def units(which):
                for u in which:
                    if pl.tr % 2 == 1:
                        dve.wait_ge(tr_done, pl.tr + 1)
                        dst, src = u(pl.tr)
                        v.tensor_copy(dst, src).then_inc(tr_out[1], 1)
                    pl.tr += 1

            def norm(l, what, cols=FULL):
                srcs, _, gains, outs, w = norm_sources(l, what, cols)
                dve.wait_ge(rstd_ok, pl.norm + 1)
                r = rstd[:, pl.norm % 2, 0:w]
                for k, src in enumerate(srcs):
                    if gains is None:
                        tt(src, src, r, ALU.mult).then_inc(applied, 1)
                    else:
                        stt(outs[k], src, gains[k], r, ALU.mult, ALU.mult).then_inc(applied, 1)
                pl.norm += 1

            def gla():
                for j in range(2):
                    dve.wait_ge(gu_done, j + 1)
                    ts(lb[:, j].rearrange("p (c n) -> p c n", c=2), PS[:, NORM_BANK:NORM_BANK + 2, 0:HALF], c_bg(j), None,
                       ALU.add).then_inc(gu_read, 1)
                    dve.wait_ge(gu_read, j + 1)
                    dve.wait_ge(ln_ok, j + 1)
                    link(stt(la[:, j], lb[:, j], 0.0, la[:, j], ALU.min, ALU.subtract))
                    v.tensor_tensor_scan(lb[:, j, 0:SEQ], keep[:, :], la[:, j, 0:SEQ], 0.0, ALU.mult, ALU.add)
                    link(v.tensor_copy(lb[:, j, SEQ:TOK], la[:, j, SEQ:TOK]))
                ch = lambda a: a[:, :, 0:SEQ].rearrange("p j (n c) -> p j n c", c=CH)
                v.tensor_copy(st[:, 0:1], lb[:, 0, 0:1]).then_inc(lb_ok, 1)
                tt(ch(ke), ch(lb)[:, :, :, CH - 1:CH].to_broadcast((P, 2, NCH, CH)), ch(lb), ALU.subtract).then_inc(ked_ok, 1)
                dve.wait_ge(kee_ok, 1)
                tt(ke[:, :, 0:SEQ], ke[:, :, 0:SEQ], zT[:, 2:4, 0:SEQ], ALU.mult).then_inc(ke_ok, 1)
                dve.wait_ge(ke_ok, 1)
                dve.wait_ge(eb_ok, 2)
                tt(zT[:, 2:4, 0:SEQ], zT[:, 2:4, 0:SEQ], la[:, :, 0:SEQ], ALU.mult)
                ts(zT[:, 0:2, SEQ:TOK], zT[:, 0:2, SEQ:TOK], GDK ** -0.5, None, ALU.mult)
                stt(zT[:, 0:2, 0:SEQ], zT[:, 0:2, 0:SEQ], GDK ** -0.5, eb[:, :, 0:SEQ], ALU.mult, ALU.mult).then_inc(qk_ok, 1)
                units(units_gla())
                wait_tr(dve, pl.tr)
                for b in range(NB):
                    last = ts(kdiag[:, b, :], ksT, ident[0:NB, b:b + 1], None, ALU.mult)
                last.then_inc(kdiag_ok, 1)
                dve.wait_ge(kv_done, 1)
                dve.wait_ge(ss_in, 64)
                for n in range(NCH):
                    kv = PS[:, n % 4, 256 * (n // 4):256 * (n // 4) + 256].rearrange("p (j v) -> p j v", j=2)
                    if n == 0:
                        link(v.tensor_copy(S[:, 0], kv))
                        continue
                    for j in range(2):
                        last = stt(S[:, n, j, :], S[:, n - 1, j, :], eb[:, j, CH * n + CH - 1:CH * n + CH], kv[:, j, :], ALU.mult, ALU.add)
                        if n < NCH - 1:
                            c = steps.mark(last)
                    if n < NCH - 1:
                        steps.wait(c)
                last.then_inc(s_ok, 1)
                dve.wait_ge(outer_done, 1)
                for b in range(NB):
                    for j in range(2):
                        last = stt(SS[:, b, j, :], SS[:, b, j, :], eb[:, j, SEQ + b:SEQ + b + 1],
                                   PS[:, b // 2, 256 * (b % 2) + P * j:256 * (b % 2) + P * j + P], ALU.mult, ALU.add)
                last.then_inc(ss_ok, 1)
                eg = scr[:, 0:4 * TOK].rearrange("p (h n) -> p h n", h=4)
                dve.wait_ge(eg_ok, 1)
                for h in range(4):
                    norm(h, "gla")
                    dve.wait_ge(applied, APPLIED[0][0] + h + 1)
                    link(tt(mix[:, h, :], mix[:, h, :], eg[:, h, :], ALU.mult))

            def prompt_z(h):
                dve.wait_ge(z_done, h + 1)
                if h >= 2:
                    dve.wait_ge(wr_ok, h - 1)
                ts(sbz[h % 2], PS[:, 0:3, :].rearrange("p a b -> p (a b)")[:, 0:SBW], SBD ** -0.5, sbb[:, h:h + 1], ALU.mult, ALU.add).then_inc(z_read, 1)
                dve.wait_ge(z_read, h + 1)
                dve.wait_ge(zl_ok, h + 1)
                stt(sbt[h % 2], sbz[h % 2], 0.0, sbt[h % 2], ALU.max, ALU.add).then_inc(spr_ok, 1)

            def sb_prompt():
                prompt_z(0)
                for h in range(SBH):
                    dve.wait_ge(r_done, h + 1)
                    tt(sbz[h % 2], sbz[h % 2], PS[:, 4:7, :].rearrange("p a b -> p (a b)")[:, 0:SBW], ALU.subtract).then_inc(zr_ok, 1)
                    if h + 1 < SBH:
                        prompt_z(h + 1)

            slots = {}

            def k_group(b, g):
                if g == 0:
                    dve.wait_ge(bq_done, b.at(1, 1))
                dve.wait_ge(k_in[g % 2], b.at(256, 64 * (3 + g // 2)))
                made = []
                for c in range(2):
                    if g:
                        if c == 0:
                            steps.wait(slots["reduced"])
                        else:
                            dve.wait_ge(k_used, b.at(8, 4 + g))
                    made.append(steps.mark(tt(prod[:, 2 * c:2 * c + 2, :], kring[:, g % 2, 2 * c:2 * c + 2, :],
                                              PS[:, 4:5, :].to_broadcast((P, 2, 512)), ALU.mult)))
                for c in range(2):
                    steps.wait(made[c])
                    o = 4 * g + 2 * c
                    last = v.tensor_reduce(zs[:, :, o:o + 2].rearrange("p h g -> p g h"),
                                           prod[:, 2 * c:2 * c + 2, :].rearrange("p a (h d) -> p a h d", h=SBH), AX.X, ALU.add)
                    if c == 0:
                        slots["reduced"] = steps.mark(last)
                    else:
                        last.then_inc(k_used, 1)

            flat = lambda a: a.rearrange("p h g -> p (h g)")

            def softplus(b):
                dve.wait_ge(k_used, b.at(8, 4 + KGROUPS))
                stt(zb, zs, SBD ** -0.5, sbb[:, :].rearrange("p (h a) -> p h a", a=1).to_broadcast((P, SBH, PAGES)),
                    ALU.mult, ALU.add).then_inc(bz_ok, 1)
                dve.wait_ge(bz_ok, b.at(1, 1))
                dve.wait_ge(bl_ok, b.at(1, 1))
                link(stt(sp_s, zb, 0.0, lg, ALU.max, ALU.add))
                link(v.tensor_tensor_scan(flat(cs), flat(keepp[:, :, :]), flat(sp_s), 0.0, ALU.mult, ALU.add))
                tt(cs, cs, sp_s, ALU.subtract).then_inc(bcs_ok, 1)

            def exponent(b):
                dve.wait_ge(br_done, b.at(1, 1))
                tt(flat(zb), flat(zb), PS[:, 7, 64:320], ALU.subtract).then_inc(bzr_ok, 1)

            def block(b, panels, k, v):
                s1 = Idx(b.c - 1, b.i, b.per)
                if v:
                    softplus(s1)
                for p in range(4):
                    if k:
                        k_group(b, 2 * p)
                        k_group(b, 2 * p + 1)
                    panels[p]()
                    if p == 0 and v:
                        exponent(s1)

            def add_group(g, k, cols):
                dve.wait_ge(dense_done, g + 1)
                x = as_pair(tile_cols(xT, k, cols), cols)
                tt(x, x, pair(k % 2, cols), ALU.add).then_inc(dense_free[k % 2], 1)

            def add_to_residual(g, cols):
                for k in range(KD):
                    add_group(g + k, k, cols)

            def conv_all(l, t):
                c = NC1 + l * NCC + t * NF
                return cv[:, c:c + NF].rearrange("p (f a) -> p f a", a=1).to_broadcast((P, NF, NB))

            def ffn_start(l, cols):
                if cols != SAMPLES:
                    for p in range(2):
                        v.memset(ext[p][:, 0:2], 0.0)
                if cols == PROMPT:
                    return
                tmp = scr[:, 3200:3200 + NF * NB].rearrange("p (f b) -> p f b", b=NB)
                taps = [conv_all(l, t) for t in range(2)]
                pv = prev[:, l].rearrange("p f (b t) -> p f b t", t=2)
                link(tt(tmp, pv[:, :, :, 0], taps[0], ALU.mult))
                link(tt(pre[:, :, :], pv[:, :, :, 1], taps[1], ALU.mult))
                link(tt(pre[:, :, :], pre[:, :, :], tmp, ALU.add))

            def up_evac(l, f, p, cols):
                g0, w = up_groups(l, cols), cols[1]
                done = f.at(1, up_count(l, cols) + 1)
                dve.wait_ge(ga_ok, done)
                dve.wait_ge(dense_free[0], f.at(1, g0 // 2 + 1))
                a = acc[p][:, 0:w]
                own = pre[:, f.one(), :].rearrange("p a b -> p (a b)")
                link(stt(a[:, 0:SEQ], ext[p][:, 1:1 + SEQ], c_conv(l, 1, f), a[:, 0:SEQ], ALU.mult, ALU.add))
                if w == TOK:
                    tt(a[:, SEQ:TOK], a[:, SEQ:TOK], own, ALU.add)
                v.tensor_copy(tails[:, f.one(), 0:w - SEQ + 2].rearrange("p a b -> p (a b)"), ext[p][:, SEQ:2 + w])
                stt(a[:, 0:SEQ], ext[p][:, 0:SEQ], c_conv(l, 0, f), a[:, 0:SEQ], ALU.mult, ALU.add).then_inc(gc_ok, 1)
                dve.wait_ge(ge_ok, done)
                dve.wait_ge(dense_done, f.at(2, g0 + 2))
                tt(as_pair(big[:, f.one(), cols[0]:cols[0] + w].rearrange("p a n -> p (a n)"), cols), as_pair(sg[p][:, 0:w], cols),
                   pair(1, cols), ALU.mult).then_inc(dense_free[1], 1)

            def mem_samples(l):
                n0 = 4 + NB * KGROUPS if l else 0
                for b in range(NB):
                    n = n0 + b // 2
                    dve.wait_ge(qb_done, NB * l + b + 1)
                    dve.wait_ge(k_in[n % 2], 64 * (n // 2 + 1))
                    if b >= 2:
                        dve.wait_ge(k_used, n0 + b // 2) if b % 2 == 0 else steps.wait(slots["sum"])
                    pr = prod[:, 2 * (b % 2):2 * (b % 2) + 2, :]
                    tt(pr, kring[:, n % 2, 2 * (b % 2):2 * (b % 2) + 2, :],
                       PS[:, NORM_BANK + b % 2:NORM_BANK + b % 2 + 1, :].to_broadcast((P, 2, 512)), ALU.mult).then_inc(qb_read, 1)
                    dve.wait_ge(qb_read, NB * l + b + 1)
                    last = v.tensor_reduce(sm[:, :, b, :], pr.rearrange("p m (h d) -> p m h d", h=4), AX.X, ALU.add)
                    if b % 2:
                        last.then_inc(k_used, 1)
                    else:
                        slots["sum"] = steps.mark(last)
                pl.tr += 1
                dve.wait_ge(tr_out[0], pl.tr // 2 + 1)
                link(v.tensor_reduce(s_smx, s32[:, :], AX.X, ALU.max))
                ts(s_smx, s_smx, -MSC, None, ALU.mult).then_inc(smx_ok, 1)
                dve.wait_ge(sme_ok, l + 1)
                link(v.reciprocal(s_ssum, s_ssum))
                ts(s32[:, :], s32[:, :], s_ssum, None, ALU.mult).then_inc(smn_ok, 1)
                dve.wait_ge(tr_done, pl.tr + 1)
                v.tensor_copy(ps[:, :, :], bank(pl.tr, P, 64).rearrange("p (m c) -> p m c", m=MT)).then_inc(tr_out[1], 1)
                pl.tr += 1

            def tail(l, cols):
                add_to_residual(up_groups(l, cols) - 8, cols)
                norm(l, "ffn", cols)
                ffn_start(l, cols)
                with dve.Fori(0, NF // 2) as i:
                    steps.enter(i, 2)
                    for p in range(2):
                        up_evac(l, Idx(p, i, 2), p, cols)
                    steps.leave(NF // 2)
                units(units_tail())
                add_to_residual(up_groups(l, cols) + 2 * NF, cols)

            def samples_add(groups):
                dve.wait_ge(s_sum_done, groups)
                x = xT[:, :, SEQ:TOK]
                tt(x, x, PS[:, 1, 0:KD * NB].rearrange("p (k b) -> p k b", b=NB), ALU.add).then_inc(s_x_ok, 1)

            def samples_tail():
                ffn_start(1, SAMPLES)
                link(tt(pre[:, :, :], pre[:, :, :], conv_all(1, 3), ALU.add))
                samples_add(4)
                norm(1, "ffn", SAMPLES)
                dve.wait_ge(s_sum_done, 4 + NF)
                gates, vals = (PS[:, 3, 256 * c:256 * c + NF * NB].rearrange("p (f b) -> p f b", b=NB) for c in range(2))
                link(tt(accS, gates, conv_all(1, 2), ALU.mult))
                tt(accS, accS, pre[:, :, :], ALU.add).then_inc(s_acc_ok, 1)
                v.tensor_copy(tails[:, :, 2:2 + NB], gates).then_inc(s_tails_ok, 1)
                dve.wait_ge(s_silu_ok, 1)
                tt(actS[:, :, 0:NB], sgS, vals, ALU.mult).then_inc(s_act_ok, 1)
                units(units_tail())
                samples_add(S_GROUPS)

            units(units_setup())
            wait_tr(dve, 16)
            norm(0, "mem")
            for l in range(2):
                g0 = GROUPS * l
                dve.wait_ge(applied, 8)
                for k in range(KD):
                    last = ts(memH[:, k, :], memR[:, k, :], c_mem(l, k), None, ALU.mult)
                last.then_inc(memh_ok, 1)
                if l:
                    dve.wait_ge(tail_st, 48)
                norm(l, "mix")
                for par in range(2):
                    dve.wait_ge(dense_free[par], g0 // 2 + 4)
                kk = memK[:, :, :].rearrange("p t (h d) -> p (t h) d", d=P)
                dve.wait_ge(bc_in, 32)
                link(tt(prod[:, 0:2, :], memK[:, :, :], memK[:, :, :], ALU.mult))
                v.tensor_reduce(s_kn, prod[:, 0:2, :].rearrange("p t (h d) -> p (t h) d", d=P), AX.X, ALU.add).then_inc(kss_ok, 1)
                dve.wait_ge(kr_ok, l + 1)
                link(tt(kk, kk, s_kn.rearrange("p (a b) -> p a b", b=1).to_broadcast((P, 8, P)), ALU.mult))
                tt(kk, kk, knorm[:, l:l + 1, :].to_broadcast((P, 8, P)), ALU.mult).then_inc(mk_ok, 1)
                units(units_memk())
                for q in range(10):
                    p, t = q // 5, q % 5
                    n = P if t < TT else NB
                    dve.wait_ge(dense_done, g0 + 20 + q + 1)
                    dst = vT[:, t, PCOL * p:PCOL * p + PCOL] if t < TT else vS[:, PCOL * p:PCOL * p + PCOL]
                    v.tensor_copy(dst, PS[0:n, 2 * (q % 2), 0:PCOL]).then_inc(dense_free[q % 2], 1)
                if l == 0:
                    gla()
                else:
                    units(units_sb())
                    sb_prompt()
                for h in range(4):
                    norm(l, h)
                for h in range(4 + 1):
                    if h < 4:
                        dve.wait_ge(sc_done, 4 * l + h + 1)
                        m = s_mx(h % 2)
                        link(v.tensor_reduce(m, PS[:, 2 * (h % 2):2 * (h % 2) + 2, :].rearrange("p a (b m) -> p (a b) m", b=2), AX.X, ALU.max))
                        ts(m, m, -MSC, None, ALU.mult).then_inc(mx_ok, 1)
                    if h >= 1:
                        a = h - 1
                        dve.wait_ge(pe_ok, 4 * l + a + 1)
                        link(v.reciprocal(s_sum(a % 2), s_sum(a % 2)))
                        for t in range(TT):
                            last = ts(pb[a % 2][:, t, :], pb[a % 2][:, t, :], s_sum(a % 2)[:, t:t + 1], None, ALU.mult)
                        last.then_inc(pn_ok, 1)
                        units(units_probs(a))
                if l == 0:
                    mem_samples(0)
                    tail(0, FULL)
                    continue
                outs = [lambda p=p: [add_group(up_groups(1, PROMPT) - 8 + 2 * p + a, 2 * p + a, PROMPT) for a in range(2)] for p in range(4)]
                block(Idx(0), outs, True, False)
                dve.wait_ge(kt_st, 64)
                v.memset(padded, 0.0)
                norm(1, "ffn", PROMPT)
                ffn_start(1, PROMPT)
                ups = lambda f0: [lambda p=p: up_evac(1, Idx(f0.c + p, f0.i, f0.per), p % 2, PROMPT) for p in range(4)]
                block(Idx(1), ups(Idx(0)), True, True)
                with dve.Fori(0, 4) as i:
                    steps.enter(i, 3 * KGROUPS + 2 + 4)
                    block(Idx(2, i, 1), ups(Idx(4, i, 4)), True, True)
                    steps.leave(4)
                for f in (20, 21):
                    up_evac(1, Idx(f), f % 2, PROMPT)

                def down_evac(u):
                    if u % 3 == 2:
                        for a in range(2):
                            k = 2 * (u // 3) + a
                            add_group(up_groups(1, PROMPT) + 2 * NF + k, k, PROMPT)

                for b in range(6, 9):
                    block(Idx(b), [lambda u=4 * (b - 6) + p: down_evac(u) for p in range(4)], b < NB, True)
                units(units_y())
                mem_samples(1)
                samples_tail()
            units(units_ys())


INS = ["x_prompt", "x_sample", "state_gla", "cache_sb_k", "cache_sb_v", "cache_mem_k", "cache_mem_v", "state_ffn_conv",
       "page_table", "mem_prompt", "norm_mix", "w_in_gla", "w_gate_up", "b_gate", "gla_out_norm", "w_in_sb", "sb_bias",
       "mem_norm", "w_mem_kv", "mem_q_norm", "mem_k_norm", "w_out", "norm_ffn", "w_ffn_up", "ffn_conv_w", "ffn_conv_b",
       "w_ffn_down"]
OUTS = [("y_p", (1, 512, 1024)), ("y_s", (8, 1, 1024)), ("gla_p", (1, 1, 4, 64, 128)), ("gla_s", (1, 8, 4, 64, 128)),
        ("sb_kp", (1, 1, 512, 8, 64)), ("sb_vp", (1, 1, 512, 8, 64)), ("sb_ks", (1, 8, 1, 8, 64)), ("sb_vs", (1, 8, 1, 8, 64)),
        ("mem_k", (2, 1, 256, 4, 128)), ("mem_v", (2, 1, 256, 4, 128)), ("conv_p", (2, 1, 2, 2816)), ("conv_s", (2, 8, 2, 2816))]


def kernel(**inputs):
    import concourse.bacc as bacc
    from concourse.bass_utils import run_bass_kernel_spmd

    nc = bacc.Bacc("TRN2", target_bir_lowering=False, num_devices=1)
    arrays, I, O = {}, {}, {}
    for name in INS:
        a = np.ascontiguousarray(inputs[name])
        arrays[name] = a
        I[name] = nc.dram_tensor(name, a.shape, mybir.dt.from_np(a.dtype), kind="ExternalInput").ap()
    for name, shape in OUTS:
        O[name] = nc.dram_tensor(name, shape, F32, kind="ExternalOutput").ap()
    build(nc, I, O)
    r = run_bass_kernel_spmd(nc, [arrays], core_ids=[0])
    return tuple(r.results[0][name] for name, _ in OUTS)
```

```python
import numpy as np
import concourse.bass as bass
from concourse import mybir
from contextlib import ExitStack

F32 = mybir.dt.float32
I32 = mybir.dt.int32
ACT = mybir.ActivationFunctionType
ALU = mybir.AluOpType
AX = mybir.AxisListType

P = 128
D = 1024
KD = D // P
SEQ, NB = 512, 8
TOK = SEQ + NB
HALF = TOK // 2
TT = SEQ // P
GR = 16
CH = 64
NCH = SEQ // CH
GDK, GDV = 64, 128
NMEM, MT = 256, 2
MW = 512
SBH, SBD = 8, 64
PAGES, PAGE = 32, 128
DFF = 2816
NF = DFF // P
PCOL = 256
EPS = 1e-6
TR_BANK, NORM_BANK = 4, 6
KGROUPS = PAGES // 4


class Steps:

    def __init__(self, eng, sem):
        self.eng, self.sem, self.n, self.extra = eng, sem, 0, 0

    def mark(self, ins):
        self.n += 1
        ins.then_inc(self.sem, 1)
        return self.n

    def wait(self, n):
        self.eng.wait_ge(self.sem, n + self.extra)

    def link(self, ins):
        self.wait(self.mark(ins))

    def enter(self, i, per):
        self.start, self.per, self.extra = self.n, per, i * per

    def leave(self, count):
        assert self.n - self.start == self.per, (self.n - self.start, self.per)
        self.n = self.start + self.per * count
        self.extra = 0


class Idx:

    def __init__(self, c, i=None, per=0):
        self.c, self.i, self.per = c, i, per

    def at(self, mult=1, add=0):
        n = self.c * mult + add
        return n if self.i is None else self.i * (self.per * mult) + n

    def one(self, add=0):
        return bass.ds(self.at(1, add), 1)


class Place:

    def __init__(self):
        self.panel = self.group = self.tr = self.norm = self.sq = 0


def build(nc, I, O):
    ctx = ExitStack()
    with ctx:
        def sb(name, shape, dt=F32):
            return ctx.enter_context(nc.sbuf_tensor(name, shape, dt))

        def sem(name):
            return ctx.enter_context(nc.semaphore(name))

        xT = sb("xT", [P, KD, TOK])
        with ExitStack() as early:
            def first(name, shape):
                return early.enter_context(nc.sbuf_tensor(name, shape, F32))

            hT = first("hT", [P, KD, TOK])
            vT = first("vT", [P, TT, 512])
            memR = first("memR", [P, KD, NMEM])
            memK = first("memK", [P, MT, 512])
            memKT = first("memKT", [P, 4, NMEM])
            memV = first("memV", [P, MT, 512])
        F32R = mybir.dt.float32r
        h_hi = sb("h_hi", [P, KD, TOK], F32R)
        h_lo = sb("h_lo", [P, KD, TOK], F32R)
        w_parts = sb("w_parts", [P, 2, 2, 4, P], F32R)
        after = sb("after", [P, 960])
        big = sb("big", [P, NF, TOK])
        zT = big[:, 0:12, :]
        mix = big[:, 12:20, :]
        zs0 = big[:, 21, 0:SBH * PAGES].rearrange("p (h g) -> p h g", h=SBH)
        vS = big[0:NB, 20, 0:512]
        vTf = vT[:, :, :].rearrange("p t n -> p (t n)")
        padded = vTf[:, 0:(2 * KD + NF) * 32]
        mixS, hS, actS = (padded[:, 32 * a:32 * b].rearrange("p (k c) -> p k c", c=32)
                          for a, b in ((0, KD), (KD, 2 * KD), (2 * KD, 2 * KD + NF)))
        accS = vTf[:, 1216:1216 + NF * NB].rearrange("p (f b) -> p f b", b=NB)
        sgS = vTf[:, 1392:1392 + NF * NB].rearrange("p (f b) -> p f b", b=NB)
        wring = sb("wring", [P, 2, 8, PCOL])
        kring = sb("kring", [P, 2, 4, 512])
        vring = sb("vring", [P, 2, 4, 512])
        prod = sb("prod", [P, 4, 512])
        memR1 = vring[:, 1, :, :].rearrange("p a (b c) -> p (a b) c", b=2)
        rowsS = prod[:, 0:2, 0:PCOL]
        om2 = prod[:, 0:2, :]
        memH = prod[:, :, :].rearrange("p a (b c) -> p (a b) c", b=2)
        scr = sb("scr", [P, 5200])
        rstd = sb("rstd", [P, 2, TOK])
        sq = sb("sq", [P, 2, TOK])
        ident = sb("ident", [P, P])
        ones = sb("ones", [P, P])
        tri = sb("tri", [P, P])
        keep = sb("keep", [P, SEQ])
        sel = sb("sel", [P, SBH])
        selm = sb("selm", [P, 4, 2, 4])
        selb = sb("selb", [P, NB])
        keepp = sb("keepp", [P, SBH, PAGES])
        cv = sb("cv", [P, 232])
        prev = sb("prev", [P, 2, NF, 2 * NB])
        pre = sb("pre", [P, NF, NB])
        tails = sb("tails", [P, NF, 2 + NB])
        eps = sb("eps", [P, 1])
        sbb = sb("sbb", [P, SBH])
        knorm = sb("knorm", [P, 2, P])
        wgd = sb("wgd", [P, KD, GR])
        wgu = sb("wgu", [GR, 256])
        gdT = sb("gdT", [GR, TOK])
        pt = sb("pt", [1, NB * PAGES], I32)
        st = sb("st", [P, 160])
        s32 = sb("s32", [32, NMEM])
        ps = sb("ps", [P, MT, 32])
        om = sq[:, 0, 0:512]
        qcol = sb("qcol", [P, 4])
        PS = ctx.enter_context(nc.psum_tensor("PS", [P, 8, 512], F32))

        c_mix = lambda l, k: cv[:, 8 * l + k:8 * l + k + 1]
        c_ffn = lambda l, k: cv[:, 16 + 8 * l + k:17 + 8 * l + k]
        c_mem = lambda l, k: cv[:, 32 + 8 * l + k:33 + 8 * l + k]
        c_bg = lambda j: cv[:, 48 + j:49 + j]
        c_on = cv[:, 50:51]
        c_qn = lambda l: cv[:, 51 + l:52 + l]
        NC1 = 53
        NCC = 4 * NF

        def c_conv(l, t, f):
            return cv[:, f.one(NC1 + l * NCC + t * NF)]

        gla_rstd = [rstd[:, 0, :], rstd[:, 1, :], scr[:, 4160:4680], scr[:, 4680:5200]]

        memtok = scr[:, 0:2048].rearrange("p (t n) -> p t n", t=2)
        xs = scr[0:NB, 2048:3072]
        rows1 = scr[0:NC1, 3072:3200]
        rows2 = [scr[0:NCC, 3200 + 128 * l:3328 + 128 * l] for l in range(2)]
        xtok = hT[:, :, :].rearrange("p a b -> p (a b)")[:, 0:4096].rearrange("p (t n) -> p t n", t=4)
        bigf = big[:, :, :].rearrange("p a b -> p (a b)")
        prows = [bigf[0:2 * NB, DFF * l:DFF * (l + 1)] for l in range(2)]
        la = scr[:, 0:1040].rearrange("p (j n) -> p j n", j=2)
        lb = scr[:, 1040:2080].rearrange("p (j n) -> p j n", j=2)
        eb = scr[:, 2080:3120].rearrange("p (j n) -> p j n", j=2)
        ke = scr[:, 3120:4160].rearrange("p (j n) -> p j n", j=2)
        hTf = hT[:, :, :].rearrange("p a b -> p (a b)")
        keT = hTf[:, 0:1024].rearrange("p (j t n) -> p j t n", j=2, t=4)
        att = hTf[:, 1024:3072].rearrange("p (h t n) -> p h t n", h=4, t=4)
        ksT = hTf[0:NB, 3072:3328]
        krf = kring[:, :, :, :].rearrange("p a b c -> p (a b c)")
        S = krf[:, 0:2048].rearrange("p (n j v) -> p n j v", n=8, j=2)
        SS = krf[:, 2048:4096].rearrange("p (b j v) -> p b j v", b=8, j=2)
        kdiag = vring[0:NB, 0, :, :].rearrange("p a b -> p (a b)").rearrange("p (b n) -> p b n", b=8)
        ktok = hTf[:, 0:2048].rearrange("p (t n) -> p t n", t=4)
        kstok = hTf[0:NB, 2048:2560]
        tailr = hTf[0:2 + NB, 0:DFF]
        ytok = bigf[:, 0:4096].rearrange("p (t n) -> p t n", t=4)
        ystok = bigf[0:NB, 4096:5120]
        SBO = {0: 0, 1: 512, 3: 896, 2: 1024}
        SBW = 1280
        sbt = [scr[:, 2560 * p:2560 * p + SBW] for p in range(2)]
        sbz = [scr[:, 2560 * p + SBW:2560 * p + 2 * SBW] for p in range(2)]
        def s5(k):
            return scr[:, 3400 + 256 * k:3656 + 256 * k]
        zs, zb, lg, cs = (s5(k).rearrange("p (h g) -> p h g", h=SBH) for k in range(4))
        sp_s = s5(4).rearrange("p (h g) -> p h g", h=SBH)
        wsb = s5(5).rearrange("p (g c) -> p g c", c=32)
        pb = [scr[:, 1024 * p:1024 * p + 1024].rearrange("p (t m) -> p t m", t=4) for p in range(2)]
        pT = [scr[:, 2048 + 1024 * p:3072 + 1024 * p].rearrange("p (m n) -> p m n", m=2) for p in range(2)]
        sm = scr[:, 5000:5064].rearrange("p (m b h) -> p m b h", m=2, b=NB)
        htmp = [scr[:, 520 * k:520 * k + 520] for k in range(6)]
        ext = [scr[:, 522 * p:522 * p + 522] for p in range(2)]
        acc = [scr[:, 1044 + 520 * p:1564 + 520 * p] for p in range(2)]
        sg = [scr[:, 2084 + 520 * p:2604 + 520 * p] for p in range(2)]

        x_in, mem_in, row_in, bc_in = sem("x_in"), sem("mem_in"), sem("row_in"), sem("bc_in")
        gd_in, pt_in, ss_in = sem("gd_in"), sem("pt_in"), sem("ss_in")
        w_in = [sem("w_in0"), sem("w_in1")]
        part_done = sem("part_done")
        s_in = [sem(f"s_in{n}") for n in range(6)]
        k_in = [sem("k_in0"), sem("k_in1")]
        v_in = [sem("v_in0"), sem("v_in1")]
        k_used, v_used = sem("k_used"), sem("v_used")
        const_ok = sem("const_ok")
        dense_done = sem("dense_done")
        dense_free = [sem("dense_free0"), sem("dense_free1")]
        tr_done = sem("tr_done")
        tr_out = [sem("tr_out_act"), sem("tr_out_dve")]
        sq_ok, sq_used, rstd_ok, applied = (sem(n) for n in ("sq_ok", "sq_used", "rstd_ok", "norm_applied"))
        act_step, dve_step, pool_step = sem("act_step"), sem("dve_step"), sem("pool_step")
        memh_ok = sem("memh_ok")
        kss_ok, kr_ok, mk_ok = sem("kss_ok"), sem("kr_ok"), sem("mk_ok")
        gd_done, gd_ok, gu_done, gu_read = (sem(n) for n in ("gd_done", "gd_ok", "gu_done", "gu_read"))
        ln_ok, lb_ok, eb_ok, ked_ok, kee_ok, qk_ok, ke_ok = (sem(n) for n in ("ln_ok", "lb_ok", "eb_ok", "ked_ok", "kee_ok", "qk_ok", "ke_ok"))
        att_done, att_out, att_ok = sem("att_done"), sem("att_out"), sem("att_ok")
        kv_done, s_ok, kdiag_ok, outer_done, ss_ok = (sem(n) for n in ("kv_done", "s_ok", "kdiag_ok", "outer_done", "ss_ok"))
        o_done, os_done, o_ok = sem("o_done"), sem("os_done"), sem("o_ok")
        eg_ok, gla_ok = sem("eg_ok"), sem("gla_ok")
        sc_done, mx_ok, pe_ok, pn_ok, po_done, po_out = (sem(n) for n in ("sc_done", "mx_ok", "pexp_ok", "pn_ok", "po_done", "po_out"))
        qb_done, qb_read, sm_ok, smx_ok, sme_ok, smn_ok, so_done, so_out = (
            sem(n) for n in ("qb_done", "qb_read", "sm_ok", "smx_ok", "sme_ok", "smn_ok", "so_done", "so_out"))
        z_done, z_read, zl_ok, spr_ok, sp_ok, r_done, zr_ok, wr_ok, w_ok, sbo_done, sbo_out = (
            sem(n) for n in ("z_done", "z_read", "zl_ok", "spr_ok", "sp_ok", "r_done", "zr_ok", "wr_ok", "w_ok", "sbo_done", "sbo_out"))
        bq_done, bk_done, bz_ok, bl_ok, bcs_ok, br_done, bzr_ok, bw_ok, bo_done, bom_ok, bf_done, qcol_ok = (
            sem(n) for n in ("bq_done", "bk_done", "bz_ok", "bl_ok", "bcs_ok", "br_done", "bzr_ok", "bw_ok", "bo_done", "bom_ok", "bf_done", "qcol_ok"))
        bs_out = sem("bs_out")
        s_read, s_rows_ok, s_sum_done, s_x_ok, s_tails_ok, s_acc_ok, s_silu_ok, s_act_ok = (
            sem(n) for n in ("s_read", "s_rows_ok", "s_sum_done", "s_x_ok", "s_tails_ok", "s_acc_ok", "s_silu_ok", "s_act_ok"))
        rln_ok, mo_ok = sem("rln_ok"), sem("mo_ok")
        whi_ok, wlo_ok, half_done, htmp_ok, hhi_ok, memr_moved = (
            sem(n) for n in ("whi_ok", "wlo_ok", "half_done", "htmp_ok", "hhi_ok", "memr_moved"))
        ga_ok, ge_ok, gc_ok, act_ok, pre_ok = (sem(n) for n in ("ga_ok", "ge_ok", "gc_ok", "act_ok", "pre_ok"))
        state_st, mem_st, kt_st, tail_st, y_st = (sem(n) for n in ("state_st", "mem_st", "kt_st", "tail_st", "y_st"))

        GIN = {0: [0, 256, 1024, 1280, 1552, 1808], 1: [0, 256, 512, 768, 1536, 1792]}
        GV = {0: [512, 768], 1: [1024, 1280]}
        MEM = 8
        MEM_K = (0, 4 + KGROUPS)
        MEM_V = (0, 4)

        def k_before(b):
            return Idx(4) if b.i is None and b.c == 0 else Idx(MEM + KGROUPS * b.c, b.i, KGROUPS * b.per)

        GROUPS = 90
        w_main = {0: I["w_in_gla"], 1: I["w_in_sb"]}

        def kw(ap2):
            return ap2.rearrange("(k p) n -> p k n", p=P)

        FULL, PROMPT, SAMPLES = (0, TOK), (0, SEQ), (SEQ, NB)

        def parts(cols):
            c0, w = cols
            return [(0, c0, w)] if w == NB else [(c, c0 + w // 2 * c, w // 2) for c in range(2)]

        def pair(par, cols):
            w = cols[1]
            return PS[:, 2 * par, 0:NB] if w == NB else PS[:, 2 * par:2 * par + 2, 0:w // 2]

        def as_pair(ap, cols):
            return ap if cols[1] == NB else ap.rearrange("p (c n) -> p c n", c=2)

        def tile_cols(t, k, cols):
            return t[:, k, cols[0]:cols[0] + cols[1]]

        def up_count(l, cols):
            return NF * (l + (1 if cols == SAMPLES else 0))

        def up_groups(l, cols):
            return GROUPS * l + 38 + (60 if cols == SAMPLES else 0)

        UP0, DOWN0, PANELS = 16, 16 + NF, 16 + NF + 12

        def w_ready(l, n):
            ups = min(max(0, (n - UP0) // 2 + 1), NF // 2)
            return 16 * (l * (PANELS // 2 + NF // 2) + n // 2 + 1 + ups)

        sring = [wring[:, 0], wring[:, 1]] + [t[:, s].rearrange("p a (b n) -> p (a b) n", b=2) for t in (kring, vring) for s in range(2)]
        SUP, SDOWN, SLOTS = 4, 4 + NF, 6

        def s_ready(n):
            return 16 * sum(2 if SUP <= m < SDOWN else 1 for m in range(n % SLOTS, n + 1, SLOTS))

        S_GROUPS = 4 + NF + 4

        def s_group_panels(g):
            return g + 1 if g < SDOWN else SDOWN + 3 * (g - SDOWN + 1)

        def wait_panel(eng, n):
            l, n = n // PANELS, n % PANELS
            if n < 10:
                c = 2 * n + 2
            elif n < 12:
                c = 20 + 5 * (n - 9)
            elif n < UP0:
                c = 30 + 2 * (n - 11)
            elif n < DOWN0:
                eng.wait_ge(wlo_ok, 4 * (NF * l + n - UP0 + 1))
                return
            elif (n - DOWN0) % 3 < 2:
                u = n - DOWN0
                eng.wait_ge(part_done, 8 * l + 2 * (u // 3) + u % 3 + 1)
                return
            else:
                c = 82 + 2 * ((n - DOWN0) // 3 + 1)
            eng.wait_ge(dense_done, GROUPS * l + c)

        def v_norms(l):
            return (5, 6, 7, 8) if l == 0 else (1, 3, 5, 7)

        APPLIED = [[16, 24, 32], [40, 44, 52, 60]]
        TRN = {"setup": 16, "ktok": 16 + 22 + 2 + 6, "y_p": 64, "tail": [16 + 22, 70], "y_s": 72}

        def wait_tr(eng, n):
            eng.wait_ge(tr_out[0], n // 2)
            eng.wait_ge(tr_out[1], n // 2)

        block = ctx.enter_context(nc.Block())

        @block.sync
        def _(sp):
            pl = Place()

            def panel(src):
                n, s = pl.panel, pl.panel % 2
                if n >= 2:
                    wait_panel(sp, n - 2)
                sp.dma_start(wring[:, s, 0:src.shape[1], 0:src.shape[2]], src).then_inc(w_in[s], 16)
                pl.panel += 1

            sp.dma_start(xtok, I["x_prompt"][0].rearrange("(t p) n -> p t n", p=P)).then_inc(x_in, 16)
            sp.dma_start(xs, I["x_sample"].rearrange("b s n -> (b s) n")).then_inc(x_in, 16)
            sp.dma_start(memtok, I["mem_prompt"][0].rearrange("(t p) n -> p t n", p=P)).then_inc(mem_in, 16)
            nr = 0
            for name, o, n in (("norm_mix", 0, 16), ("norm_ffn", 16, 16), ("mem_norm", 32, 16), ("b_gate", 48, 2),
                               ("gla_out_norm", 50, 1), ("mem_q_norm", 51, 2)):
                sp.dma_start(rows1[o:o + n, :], I[name].rearrange("l (k p) -> (l k) p", p=P)).then_inc(row_in, 16)
                nr += 1
            for l in range(2):
                sp.dma_start(rows2[l][0:3 * NF, :], I["ffn_conv_w"][l].rearrange("t (f p) -> (t f) p", p=P)).then_inc(row_in, 16)
                sp.dma_start(rows2[l][3 * NF:4 * NF, :], I["ffn_conv_b"][l].rearrange("(f p) -> f p", p=P)).then_inc(row_in, 16)
                sp.dma_start(prows[l], I["state_ffn_conv"][l].rearrange("b t f -> (b t) f")).then_inc(row_in, 16)
            sp.dma_start(knorm[:, :, :], I["mem_k_norm"].rearrange("(a l) d -> a l d", a=1).to_broadcast((P, 2, P))).then_inc(bc_in, 16)
            sp.dma_start(sbb[:, :], I["sb_bias"].to_broadcast((P, SBH))).then_inc(bc_in, 16)
            sp.dma_start(wgd[:, :, :], kw(I["w_in_gla"][0])[:, :, 1536:1536 + GR]).then_inc(gd_in, 16)
            sp.dma_start(wgu[:, :], I["w_gate_up"][0]).then_inc(gd_in, 16)
            sp.dma_start(pt[:, :], I["page_table"].rearrange("(a b) n -> a (b n)", a=1)).then_inc(pt_in, 16)
            for hh in range(2):
                for j in range(2):
                    sp.dma_start(SS[64 * hh:64 * hh + 64, :, j, :],
                                 I["state_gla"][0, :, 2 * j + hh].rearrange("b k v -> k b v")).then_inc(ss_in, 16)

            def mem_groups(l):
                kk = (kring, k_used, k_in, "cache_mem_k", MEM_K[l])
                vv = (vring, v_used, v_in, "cache_mem_v", MEM_V[l])
                for g, (ring, used, in_, cache, n0) in ((0, kk), (1, kk), (0, vv), (1, vv), (2, kk), (3, kk), (2, vv), (3, vv)):
                    n = n0 + g
                    if n >= 2:
                        sp.wait_ge(used, n - 1)
                    for bb in range(2):
                        for mt in range(2):
                            sp.dma_start(ring[:, g % 2, 2 * bb + mt, :],
                                         I[cache][l, 2 * g + bb, P * mt:P * mt + P].rearrange("m h d -> m (h d)")).then_inc(in_[g % 2], 16)

            def pages(cache, ring, in_, b, g):
                _, numbers = nc.values_load_multi_w_load_instructions(
                    pt[0:1, bass.ds(b.at(PAGES, PAGES - 4 - 4 * g), 4)], engines=[sp.engine], min_val=0, max_val=I[cache].shape[1] - 1)
                for jj in range(4):
                    page = numbers[3 - jj]
                    sp.dma_start(ring[:, g % 2, jj, :],
                                 I[cache][0, bass.ds(page, 1)].rearrange("a p h d -> (a p) (h d)")).then_inc(in_[g % 2], 16)

            def kv_pages(b, p, k, v, v2, weights=None):
                if p and v:
                    s, gs = Idx(b.c - 1, b.i, b.per), (2 * p - 2, 2 * p - 1)
                elif not p and v2:
                    s, gs = Idx(b.c - 2, b.i, b.per), (6, 7)
                else:
                    s, gs = None, ()
                for m in range(2):
                    if k:
                        sp.wait_ge(k_used, k_before(b).at(1, 2 * p + m - 1))
                        pages("cache_sb_k", kring, k_in, b, 2 * p + m)
                    if gs:
                        sp.wait_ge(v_used, s.at(8, MEM - 1 + gs[m]))
                        pages("cache_sb_v", vring, v_in, s, gs[m])
                    if weights and m == 0:
                        weights()

            for l in range(2):
                wm = kw(w_main[l][0])
                wkv = kw(I["w_mem_kv"][l])
                for p in range(4):
                    panel(wkv[:, :, PCOL * p:PCOL * p + PCOL])
                for c in GIN[l] + GV[l]:
                    panel(wm[:, :, c:c + PCOL])
                wo = kw(I["w_out"][l])
                wu = I["w_ffn_up"][l].rearrange("(k p) (c f n) -> p k c f n", p=P, c=2, n=P)
                wd = I["w_ffn_down"][l].rearrange("(k p) n -> p k n", p=P)

                def out_panel(p):
                    panel(wo[:, :, PCOL * p:PCOL * p + PCOL])

                def up_panel(s, f):
                    for c in range(2):
                        sp.dma_start(wring[:, s, :, P * c:P * c + P], wu[:, :, c, f.one(), :].rearrange("p k a n -> p k (a n)")).then_inc(w_in[s], 16)

                def down_panel(u):
                    kc = u % 3
                    nk = 8 if kc < 2 else 6
                    panel(wd[:, 8 * kc:8 * kc + nk, PCOL * (u // 3):PCOL * (u // 3) + PCOL])

                def samples_panel(n, f=None, place=None):
                    s = n % SLOTS
                    dst = sring[s]
                    if n < SUP:
                        sp.dma_start(dst, wo[:, :, PCOL * n:PCOL * n + PCOL]).then_inc(s_in[s], 16)
                    elif n < SDOWN:
                        for c in range(2):
                            sp.dma_start(dst[:, :, P * c:P * c + P], wu[:, :, c, f.one(), :].rearrange("p k a n -> p k (a n)")).then_inc(s_in[s], 16)
                    else:
                        kc, m = (n - SDOWN) % 3, (n - SDOWN) // 3
                        nk = 8 if kc < 2 else 6
                        sp.dma_start(dst[:, 0:nk, :], wd[:, 8 * kc:8 * kc + nk, PCOL * m:PCOL * m + PCOL]).then_inc(s_in[s], 16)

                out_panel(0)
                if l == 0:
                    out_panel(1)
                    sp.wait_ge(s_ok, 1)
                    sp.wait_ge(ss_ok, 1)
                    for hh in range(2):
                        for j in range(2):
                            sp.dma_start(O["gla_p"][0, 0, 2 * j + hh], S[64 * hh:64 * hh + 64, 7, j, :]).then_inc(state_st, 16)
                            sp.dma_start(O["gla_s"][0, :, 2 * j + hh].rearrange("b k v -> k b v"),
                                         SS[64 * hh:64 * hh + 64, :, j, :]).then_inc(state_st, 16)
                    sp.wait_ge(state_st, 8 * 16)
                    sp.wait_ge(os_done, 1)
                    mem_groups(0)
                    for p in range(2, 4):
                        out_panel(p)
                    for s in range(2):
                        sp.wait_ge(dense_done, 36 + 2 * s)
                        up_panel(s, Idx(s))
                    with sp.Fori(0, NF // 2 - 1) as i:
                        for s in range(2):
                            sp.wait_ge(wlo_ok, i * 8 + (4 * s + 4))
                            up_panel(s, Idx(2 + s, i, 2))
                    pl.panel += NF
                    for u in range(12):
                        down_panel(u)
                else:
                    sp.wait_ge(pt_in, 16)
                    for p in range(4):
                        kv_pages(Idx(0), p, True, False, False)
                    sp.wait_ge(memh_ok, 2)
                    mem_groups(1)
                    for p in range(4):
                        kv_pages(Idx(1), p, True, True, False)
                        if p < 3:
                            out_panel(p + 1)
                        else:
                            sp.wait_ge(dense_done, GROUPS + 36)
                            up_panel(0, Idx(0))
                            pl.panel += 1
                    for b, i in ((2, None), (3, 4)):
                        def up_block(b, f0):
                            for p in range(4):
                                f = Idx(f0.c + p + 1, f0.i, f0.per)

                                def weights():
                                    if f.i is None and f.c == 1:
                                        sp.wait_ge(dense_done, GROUPS + 38)
                                    else:
                                        sp.wait_ge(wlo_ok, f.at(4, 4 * NF - 4))
                                    up_panel((p + 1) % 2, f)

                                kv_pages(b, p, True, True, True, weights)
                        if i is None:
                            up_block(Idx(2), Idx(0))
                        else:
                            with sp.Fori(0, 4) as j:
                                up_block(Idx(3, j, 1), Idx(4, j, 4))
                    sp.wait_ge(wlo_ok, 4 * NF + 80)
                    up_panel(1, Idx(21))
                    pl.panel += NF - 1
                    down_panel(0)
                    def early(ns):
                        for n in ns:
                            sp.wait_ge(k_used if n < 4 else v_used, MEM + NB * KGROUPS - 1 + n % 2)
                            samples_panel(n, Idx(n - SUP))

                    for b in range(7, 10):
                        for p in range(4):
                            kv_pages(Idx(b), p, b < NB, b < NB + 1, True)
                            if b == 8 and p == 0:
                                early((2, 3))
                            if b == 9 and p == 2:
                                early((4, 5))
                            u = 4 * (b - 7) + p + 1
                            if u < 12:
                                down_panel(u)
                    for n in range(2):
                        wait_panel(sp, 2 * PANELS - 2 + n)
                        samples_panel(n)
                    with sp.Fori(0, 3) as i:
                        for s in range(SLOTS):
                            sp.wait_ge(s_read, i * SLOTS + (s + 1))
                            samples_panel(SLOTS + s, Idx(2 + s, i, SLOTS))
                    for n in range(24, SDOWN + 12):
                        sp.wait_ge(s_read, n - SLOTS + 1)
                        samples_panel(n, Idx(n - SUP))
            sp.wait_ge(state_st, 8 * 16)

        @block.gpsimd
        def _(pool):
            steps = Steps(pool, pool_step)
            nc.gpsimd.memset(ident[:, :], 0.0).then_inc(pool_step, 1)
            nc.gpsimd.memset(ones[:, :], 1.0).then_inc(pool_step, 1)
            nc.gpsimd.memset(tri[:, :], 1.0).then_inc(pool_step, 1)
            nc.gpsimd.memset(keep[:, :], 1.0).then_inc(pool_step, 1)
            nc.gpsimd.memset(keepp[:, :, :], 1.0).then_inc(pool_step, 1)
            nc.gpsimd.memset(eps[:, :], EPS).then_inc(pool_step, 1)
            nc.gpsimd.memset(sel[:, :], 0.0).then_inc(pool_step, 1)
            nc.gpsimd.memset(selb[:, :], 0.0).then_inc(pool_step, 1)
            nc.gpsimd.memset(selm[:, :, :, :], 0.0).then_inc(pool_step, 1)
            steps.n = 9
            pool.wait_ge(pool_step, 9)
            af = nc.gpsimd.affine_select
            af(out=ident[:, :], in_=ident[:, :], compare_op=ALU.not_equal, fill=1.0, base=0, pattern=[[-1, P]], channel_multiplier=1).then_inc(const_ok, 1)
            af(out=tri[:, :], in_=tri[:, :], compare_op=ALU.is_ge, fill=0.0, base=0, pattern=[[-1, P]], channel_multiplier=1).then_inc(const_ok, 1)
            af(out=keep[:, :], in_=keep[:, :], compare_op=ALU.not_equal, fill=0.0, base=0, pattern=[[0, NCH], [1, CH]], channel_multiplier=0).then_inc(const_ok, 1)
            af(out=keepp[:, :, :], in_=keepp[:, :, :], compare_op=ALU.not_equal, fill=0.0, base=0, pattern=[[0, SBH], [1, PAGES]], channel_multiplier=0).then_inc(const_ok, 1)

            for j in range(4):
                steps.link(af(out=sel[:, :], in_=sel[:, :], compare_op=ALU.not_equal, fill=1.0, base=-(32 + 8) * j, pattern=[[-1, SBH]],
                              channel_multiplier=1))
                steps.link(af(out=selb[:, :], in_=selb[:, :], compare_op=ALU.not_equal, fill=1.0, base=-32 * j, pattern=[[-1, NB]],
                              channel_multiplier=1))
            steps.link(af(out=selm[:, :, :, :], in_=selm[:, :, :, :], compare_op=ALU.not_equal, fill=1.0, base=0,
                          pattern=[[-1, 4], [-16, 2], [-36, 4]], channel_multiplier=1))
            nc.gpsimd.memset(st[:, 100:101], 0.0).then_inc(const_ok, 1)

            def low_parts(l, f):
                for m in range(2):
                    for q in range(2):
                        pool.wait_ge(whi_ok, f.at(4, 4 * NF * l + 2 * m + q + 1))
                        nc.gpsimd.tensor_tensor(w_parts[:, q, 1], wring[:, f.c % 2, 4 * q:4 * q + 4, P * m:P * m + P],
                                                w_parts[:, q, 0], ALU.subtract).then_inc(wlo_ok, 1)

            for l in range(2):
                pool.wait_ge(mk_ok, l + 1)
                pool.dma_start(O["mem_k"][l, 0].rearrange("(t p) h d -> p t (h d)", p=P), memK[:, :, :]).then_inc(mem_st, 16)
                pool.dma_start(O["mem_v"][l, 0].rearrange("(t p) h d -> p t (h d)", p=P), memV[:, :, :]).then_inc(mem_st, 16)
                if l == 0:
                    for h in range(4):
                        pool.wait_ge(att_out, h + 1)
                        steps.link(af(out=att[:, h], in_=att[:, h], compare_op=ALU.is_ge, fill=0.0, base=0,
                                      pattern=[[0, TT], [1, P]], channel_multiplier=-1))
                        af(out=att[:, h].rearrange("p t (c n) -> p t c n", c=2), in_=att[:, h].rearrange("p t (c n) -> p t c n", c=2),
                           compare_op=ALU.is_ge, fill=0.0, base=0, pattern=[[0, TT], [-CH, 2], [0, CH]], channel_multiplier=1).then_inc(att_ok, 1)
                    pool.wait_ge(v_used, 4)
                    nc.gpsimd.tensor_copy(memR1, memR[:, :, :]).then_inc(memr_moved, 1)
                else:
                    def earlier_keys(h, ready, done):
                        pool.wait_ge(ready, h + 1)
                        for kc in range(TT):
                            blk = sbt[h % 2][:, SBO[kc]:SBO[kc] + P]
                            af(out=blk, in_=blk, compare_op=ALU.is_gt, fill=0.0, base=0, pattern=[[1, P]],
                               channel_multiplier=-1).then_inc(done, 1)

                    for h in range(2):
                        earlier_keys(h, spr_ok, sp_ok)
                    for h in range(SBH):
                        earlier_keys(h, wr_ok, w_ok)
                        if h + 2 < SBH:
                            earlier_keys(h + 2, spr_ok, sp_ok)
                    wait_tr(pool, TRN["ktok"])
                    pool.wait_ge(dense_free[0], (GROUPS + 30) // 2)
                    pool.wait_ge(dense_free[1], (GROUPS + 30) // 2)
                    flat = lambda ap: ap.rearrange("t h d -> t (h d)")
                    pool.dma_start(flat(O["sb_kp"][0, 0]).rearrange("(t p) n -> p t n", p=P), ktok).then_inc(kt_st, 16)
                    pool.dma_start(flat(O["sb_vp"][0, 0]).rearrange("(t p) n -> p t n", p=P), vT[:, :, :]).then_inc(kt_st, 16)
                    pool.dma_start(O["sb_ks"][0].rearrange("b s h d -> (b s) (h d)"), kstok).then_inc(kt_st, 16)
                    pool.dma_start(O["sb_vs"][0].rearrange("b s h d -> (b s) (h d)"), vS).then_inc(kt_st, 16)
                with pool.Fori(0, NF // 2) as i:
                    for s in range(2):
                        low_parts(l, Idx(s, i, 2))
                if l:
                    wait_tr(pool, TRN["y_p"])
                    pool.dma_start(O["y_p"][0].rearrange("(t p) n -> p t n", p=P), ytok).then_inc(y_st, 16)
                wait_tr(pool, TRN["tail"][l])
                pool.dma_start(O["conv_p"][l, 0], tailr[0:2, :]).then_inc(tail_st, 16)
                pool.dma_start(O["conv_s"][l, :, 1, :], tailr[2:2 + NB, :]).then_inc(tail_st, 16)
                pool.dma_start(O["conv_s"][l, :, 0, :], I["state_ffn_conv"][l, :, 1, :]).then_inc(tail_st, 16)
            wait_tr(pool, TRN["y_s"])
            pool.dma_start(O["y_s"].rearrange("b s n -> (b s) n"), ystok).then_inc(y_st, 16)
            pool.wait_ge(mem_st, 64)
            pool.wait_ge(kt_st, 64)
            pool.wait_ge(tail_st, 96)
            pool.wait_ge(y_st, 32)

        @block.tensor
        def _(pe):
            pl = Place()
            mm, tp = nc.tensor.matmul, nc.tensor.transpose

            def tr_unit(parts):
                n = pl.tr
                if n >= 2:
                    pe.wait_ge(tr_out[n % 2], n // 2)
                for c, src in parts:
                    k, m = src.shape[0], src.shape[1]
                    last = tp(PS[0:m, TR_BANK + n % 2, c:c + k], src, ident[0:k, 0:k])
                last.then_inc(tr_done, 1)
                pl.tr += 1

            def norm_sums(nk, width=TOK, h=0, bank=NORM_BANK):
                if h:
                    pe.wait_ge(rln_ok, h)
                elif pl.norm:
                    pe.wait_ge(rstd_ok, pl.norm)
                w = width // 2
                for k in range(nk):
                    pe.wait_ge(sq_ok, pl.sq + 1)
                    for c in range(2):
                        last = mm(PS[:, bank + c, 0:w], ones[:, :], sq[:, pl.sq % 2, w * c:w * c + w],
                                  start=(k == 0), stop=(k == nk - 1))
                    last.then_inc(sq_used, 1)
                    pl.sq += 1
                pl.norm += 1

            def dense_group(w, par, nk, src, k0, first, last_, cols):
                for k in range(nk):
                    for c, o, n in parts(cols):
                        last = mm(PS[:, 2 * par + c, 0:n], w[:, k, P * par:P * par + P], src[:, k0 + k, o:o + n],
                                  start=(first and k == 0), stop=(last_ and k == nk - 1))
                return last

            def free(par):
                if pl.group >= 2:
                    pe.wait_ge(dense_free[par], pl.group // 2)

            def in_panel(l, n):
                pe.wait_ge(w_in[n % 2], w_ready(l, n))

            def fm_panel(l, n, src, cols=FULL, between=(None, None)):
                w = wring[:, n % 2]
                in_panel(l, n)
                for m in range(2):
                    free(m)
                    dense_group(w, m, 8, src, 0, True, True, cols).then_inc(dense_done, 1)
                    pl.group += 1
                    if between[m]:
                        between[m]()

            def gates(j):
                if j:
                    pe.wait_ge(gu_read, 1)
                else:
                    pe.wait_ge(gd_ok, 1)
                for c in range(2):
                    last = mm(PS[:, NORM_BANK + c, 0:HALF], wgu[:, P * j:P * j + P], gdT[:, HALF * c:HALF * c + HALF],
                              start=True, stop=True)
                last.then_inc(gu_done, 1)

            def gla():
                pe.wait_ge(qk_ok, 1)
                for h in range(4):
                    j, r = h // 2, 64 * (h % 2)
                    for t in range(TT):
                        last = mm(PS[:, h, P * t:P * t + P], zT[r:r + 64, 2 + j, P * t:P * t + P],
                                  zT[r:r + 64, j, P * t:P * t + P], start=True, stop=True)
                    last.then_inc(att_done, 1)
                for j in range(2):
                    tr_unit([(P * t, ke[:, j, P * t:P * t + P]) for t in range(TT)])
                for j in range(2):
                    tr_unit([(0, zT[:, 2 + j, SEQ:TOK])])
                pe.wait_ge(att_out, 4)
                wait_tr(pe, pl.tr)
                for n in range(NCH):
                    t, r = n // 2, 64 * (n % 2)
                    for h in range(4):
                        j, o = h // 2, 64 * (h % 2)
                        c = 256 * (n // 4) + P * j
                        last = mm(PS[o:o + 64, n % 4, c:c + P], keT[r:r + 64, j, t, o:o + 64],
                                  vT[r:r + 64, t, P * h:P * h + P], start=True, stop=True)
                last.then_inc(kv_done, 1)
                pe.wait_ge(s_ok, 1)
                pe.wait_ge(kdiag_ok, 1)
                for b in range(NB):
                    for h in range(4):
                        j, o = h // 2, 64 * (h % 2)
                        c = 256 * (b % 2) + P * j
                        last = mm(PS[o:o + 64, b // 2, c:c + P], kdiag[:, b, 64 * h:64 * h + 64],
                                  vS[:, P * h:P * h + P], start=True, stop=True)
                last.then_inc(outer_done, 1)
                pe.wait_ge(ss_ok, 1)
                for h in range(4):
                    j, r = h // 2, 64 * (h % 2)
                    pe.wait_ge(att_ok, h + 1)
                    for t in range(TT):
                        last = mm(PS[:, h, P * t:P * t + P], vT[:, t, P * h:P * h + P], att[:, h, t, :], start=True, stop=False)
                        for n in (2 * t, 2 * t + 1):
                            if n:
                                last = mm(PS[:, h, CH * n:CH * n + CH], S[r:r + 64, n - 1, j, :],
                                          zT[r:r + 64, j, CH * n:CH * n + CH], start=False, stop=(n == 2 * t + 1))
                    last.then_inc(o_done, 1)
                for h in range(4):
                    j, r = h // 2, 64 * (h % 2)
                    for b in range(NB):
                        last = mm(PS[:, NORM_BANK + h % 2, NB * j + b:NB * j + b + 1], SS[r:r + 64, b, j, :],
                                  zT[r:r + 64, j, SEQ + b:SEQ + b + 1], start=True, stop=True)
                last.then_inc(os_done, 1)

            PSf = PS[:, :, :].rearrange("p a b -> p (a b)")

            def sb_prompt():
                for t in range(TT):
                    tr_unit([(P * j, zT[:, 4 + j, P * t:P * t + P]) for j in range(4)])
                for a in range(2):
                    tr_unit([(P * c, zT[:, 4 + 2 * a + c, SEQ:TOK]) for c in range(2)])

                def scores(h):
                    j, r = h // 2, 64 * (h % 2)
                    if h:
                        pe.wait_ge(z_read, h)
                    for kc in range(TT):
                        w = SEQ - P * kc
                        last = mm(PSf[:, SBO[kc]:SBO[kc] + w], zT[r:r + 64, 4 + j, P * kc:P * kc + P],
                                  zT[r:r + 64, j, P * kc:SEQ], start=True, stop=True)
                    last.then_inc(z_done, 1)

                scores(0)
                scores(1)
                q_rows(Idx(0))
                wait_tr(pe, pl.tr)
                for h in range(SBH):
                    x = sbt[h % 2]
                    pe.wait_ge(sp_ok, 4 * h + 4)
                    if h:
                        pe.wait_ge(zr_ok, h)
                    for kc in range(TT):
                        w = SEQ - P * kc
                        o = 2048 + SBO[kc]
                        last = mm(PSf[:, o:o + w], tri[:, :], x[:, SBO[kc]:SBO[kc] + w], start=True, stop=(kc == TT - 1))
                        for k2 in range(kc + 1, TT):
                            w2 = SEQ - P * k2
                            last = mm(PSf[:, o + P * (k2 - kc):o + P * (k2 - kc) + w2], ones[:, :],
                                      x[:, SBO[k2]:SBO[k2] + w2], start=False, stop=(k2 == TT - 1))
                    last.then_inc(r_done, 1)
                    if h + 2 < SBH:
                        scores(h + 2)
                    pe.wait_ge(w_ok, 4 * h + 4)
                    if h >= 2 and h % 2 == 0:
                        pe.wait_ge(sbo_out, h // 2)
                    r = 64 * (h % 2)
                    for kc in range(TT):
                        w = SEQ - P * kc
                        last = mm(PS[r:r + 64, 3, P * kc:SEQ], vT[:, kc, SBD * h:SBD * h + SBD],
                                  x[:, SBO[kc]:SBO[kc] + w], start=(kc == 0), stop=(kc == TT - 1))
                    last.then_inc(sbo_done, 1)

            def q_rows(b):
                pe.wait_ge(qcol_ok, b.at(1, 1))
                bank = 4
                if b.c:
                    pe.wait_ge(k_used, b.at(8, MEM))
                else:
                    bank = 7
                    pe.wait_ge(rstd_ok, pl.norm)
                for j in range(4):
                    last = mm(PS[:, bank, P * j:P * j + P], qcol[:, j:j + 1].to_broadcast((P, P)), ident[:, :], start=True, stop=True)
                last.then_inc(bq_done, 1)

            def key_sums(b):
                pe.wait_ge(bcs_ok, b.at(1, 1))
                mm(PS[:, 7, 64:320], tri[:, :], sp_s.rearrange("p h g -> p (h g)"), start=True, stop=False)
                mm(PS[:, 7, 64:320], ones[:, :], cs.rearrange("p h g -> p (h g)"), start=False, stop=True).then_inc(br_done, 1)

            def v_group(b, g):
                if g == 0:
                    pe.wait_ge(bw_ok, b.at(1, 1))
                pe.wait_ge(v_in[g % 2], b.at(256, 64 * (MEM // 2 + 1 + g // 2)))
                for jj in range(4):
                    last = mm(PS[32 * jj:32 * jj + 32, 6, :], wsb[:, g, :], vring[:, g % 2, jj, :],
                              start=(g == 0), stop=(g == KGROUPS - 1))
                last.then_inc(v_used, 1)

            def head_columns(b):
                pe.wait_ge(bom_ok, b.at(1, 1))
                for j in range(4):
                    last = mm(PS[:, 7, bass.ds(b.at(2, 16 * j), 2)], om[:, P * j:P * j + P], sel[:, 2 * j:2 * j + 2], start=True, stop=True)
                last.then_inc(bf_done, 1)

            def block(b, panels, k, v, v2):
                s1, s2 = Idx(b.c - 1, b.i, b.per), Idx(b.c - 2, b.i, b.per)
                if k:
                    q_rows(b)
                for p in range(4):
                    if p:
                        fs = [(lambda g=2 * p - 2 + m: v_group(s1, g)) if v else None for m in range(2)]
                    else:
                        fs = [(lambda g=6 + m: v_group(s2, g)) if v2 else None for m in range(2)]
                    panels[p](fs)
                    if p == 0 and v:
                        key_sums(s1)
                    if p == 1 and v2:
                        head_columns(s2)

            def mem_prompt(l):
                pe.wait_ge(rstd_ok, pl.norm)
                if l:
                    pe.wait_ge(k_used, MEM_K[1])
                for h in range(4 + 1):
                    if h < 4:
                        pe.wait_ge(applied, APPLIED[l][0] + 1 + h)
                        if h == 0:
                            wait_tr(pe, pl.tr)
                        if h >= 2:
                            pe.wait_ge(po_out, 4 * l + h - 1)
                        for t in range(TT):
                            last = mm(PS[:, 2 * (h % 2) + t // 2, 256 * (t % 2):256 * (t % 2) + 256],
                                      zT[:, 8 + h, P * t:P * t + P], memKT[:, h, :], start=True, stop=True)
                        last.then_inc(sc_done, 1)
                        if h == 0:
                            pe.wait_ge(applied, APPLIED[l][0] + 4)
                        mem_queries(l, (2 * h, 2 * h + 1))
                    if h >= 1:
                        a = h - 1
                        pe.wait_ge(pn_ok, 4 * l + a + 1)
                        for mt in range(MT):
                            tr_unit([(P * t, pb[a % 2][:, t, P * mt:P * mt + P]) for t in range(TT)])
                        for mt in range(MT):
                            pe.wait_ge(tr_out[mt], pl.tr // 2)
                            last = mm(PS[:, 2 * (a % 2), :], memV[:, mt, P * a:P * a + P], pT[a % 2][:, mt, :],
                                      start=(mt == 0), stop=(mt == MT - 1))
                        last.then_inc(po_done, 1)

            def mem_queries(l, bs):
                for b in bs:
                    if b >= 2:
                        pe.wait_ge(qb_read, 8 * l + b - 1)
                    for h in range(4):
                        last = mm(PS[:, NORM_BANK + b % 2, P * h:P * h + P], zT[:, 8 + h, SEQ + b:SEQ + b + 1].to_broadcast((P, P)),
                                  ident[:, :], start=True, stop=True)
                    last.then_inc(qb_done, 1)

            def mem_samples(l):
                n0 = MEM_V[l]
                pe.wait_ge(k_used, MEM_K[l] + 4)
                tr_unit([(P * mt, sm[:, mt].rearrange("p b h -> p (b h)")) for mt in range(MT)])
                pe.wait_ge(smn_ok, l + 1)
                tr_unit([(32 * mt, s32[:, P * mt:P * mt + P]) for mt in range(MT)])
                pe.wait_ge(tr_out[1], pl.tr // 2)
                for g in range(4):
                    n = n0 + g
                    pe.wait_ge(v_in[g % 2], 64 * (n // 2 + 1))
                    for mt in range(MT):
                        for bb in range(2):
                            j = 2 * (g % 2) + bb
                            last = mm(PS[32 * j:32 * j + 32, NORM_BANK + g // 2, :], ps[:, mt, :], vring[:, g % 2, 2 * bb + mt, :],
                                      start=(mt == 0), stop=(mt == MT - 1))
                    last.then_inc(v_used, 1)
                pe.wait_ge(mo_ok, 2 * l + 2)
                for h in range(4):
                    for half in range(2):
                        c = NB * h + 4 * half
                        last = mm(PS[:, 0, c:c + 4], om2[:, half, P * h:P * h + P], selm[:, h, half, :], start=True, stop=True)
                last.then_inc(so_done, 1)
                pe.wait_ge(so_out, l + 1)

            def up_panel(l, f, cols, between=(None, None), first=False):
                g0 = up_groups(l, cols)
                for m in range(2):
                    pe.wait_ge(dense_free[m], f.at(1, g0 // 2))
                    for q in range(2):
                        pe.wait_ge(wlo_ok, f.at(4, 4 * NF * l + 2 * m + q + 1))
                        for k in range(4):
                            if first and m == 0:
                                pe.wait_ge(applied, APPLIED[l][2] - KD + 4 * q + k + 1)
                            for a, hs in ((0, (h_hi, h_lo)), (1, (h_hi,))):
                                for c, o, n in parts(cols):
                                    for h in hs:
                                        last = mm(PS[:, 2 * m + c, 0:n], w_parts[:, q, a, k, :], h[:, 4 * q + k, o:o + n],
                                                  start=(q == 0 and k == 0 and a == 0 and h is h_hi), stop=(q == 1 and k == 3 and a == 1))
                        last.then_inc(dense_done if q else half_done, 1)
                    if between[m]:
                        between[m]()

            def down_panel(l, u, cols, i=None, between=(None, None)):
                m, kc, s = u // 3, u % 3, u % 2
                g0 = up_groups(l, cols) + 2 * NF
                w = wring[:, s]
                pe.wait_ge(w_in[s], w_ready(l, DOWN0 + u) if i is None else i * 48 + w_ready(l, DOWN0 + u))
                for par in range(2):
                    if kc == 0:
                        pe.wait_ge(dense_free[par], i * 2 + (g0 // 2 + m) if i is not None else g0 // 2 + m)
                    last = dense_group(w, par, 8 if kc < 2 else 6, big, 8 * kc, kc == 0, kc == 2, cols)
                    if kc == 2:
                        last.then_inc(dense_done, 1)
                    elif par:
                        last.then_inc(part_done, 1)
                    if between[par]:
                        between[par]()

            def tail(l, cols):
                for p in range(4):
                    fm_panel(l, 12 + p, mix, cols)
                norm_sums(KD, cols[1])
                for f in range(2):
                    up_panel(l, Idx(f), cols, first=(f == 0))
                with pe.Fori(0, NF // 2 - 1) as i:
                    for s in range(2):
                        up_panel(l, Idx(2 + s, i, 2), cols)
                pl.group += 2 * NF
                pe.wait_ge(dense_free[1], pl.group // 2)
                conv_rows()
                with pe.Fori(0, 2) as i:
                    for u in range(6):
                        down_panel(l, u, cols, i)
                pl.group += 8

            def samples_rows(g, src, panel):
                nk = src.shape[1]
                for j in range((nk + 7) // 8):
                    w = panel(j)
                    for k in range(8 * j, min(nk, 8 * j + 8)):
                        last = mm(PS[32 * (k % 4):32 * (k % 4) + 32, 2 * (g % 2), 0:PCOL], src[:, k, :], w[:, k - 8 * j, :],
                                  start=(k < 4), stop=(k >= nk - 4))
                    last.then_inc(s_read, 1)

            def samples_sum(g, halves):
                pe.wait_ge(s_rows_ok, g.at(1, 1))
                for c, out in enumerate(halves):
                    last = mm(out, rowsS[:, g.c % 2, P * c:P * c + P], selb[:, :], start=True, stop=True)
                last.then_inc(s_sum_done, 1)

            def samples_tail():
                def panel(n, i=None):
                    pe.wait_ge(s_in[n % SLOTS], s_ready(n) if i is None else i * 32 + s_ready(n))
                    return sring[n % SLOTS]

                tile = lambda k: PS[:, 1, NB * k:NB * k + NB]
                for g in range(4):
                    samples_rows(g, mixS, lambda j: panel(g))
                    if g:
                        samples_sum(Idx(g - 1), [tile(2 * g - 2), tile(2 * g - 1)])
                samples_sum(Idx(3), [tile(6), tile(7)])
                norm_sums(KD, NB)
                pe.wait_ge(applied, APPLIED[1][3])

                def up(f, first=False):
                    samples_rows(f.c, hS, lambda j: panel(SUP + f.c, f.i))
                    if not first:
                        up_sum(Idx(f.c - 1, f.i, f.per))

                def up_sum(f):
                    samples_sum(Idx(4 + f.c, f.i, f.per),
                                [PS[:, 3, bass.ds(f.at(NB, 256 * c), NB)] for c in range(2)])

                up(Idx(0), first=True)
                up(Idx(1))
                with pe.Fori(0, 3) as i:
                    for s in range(SLOTS):
                        up(Idx(2 + s, i, SLOTS))
                for f in range(20, NF):
                    up(Idx(f))
                up_sum(Idx(NF - 1))
                pe.wait_ge(s_act_ok, 1)
                for m in range(4):
                    samples_rows(SDOWN + m, actS, lambda j: panel(SDOWN + 3 * m + j))
                    if m == 0:
                        pe.wait_ge(s_tails_ok, 1)
                        conv_rows()
                    else:
                        samples_sum(Idx(SDOWN + m - 1), [tile(2 * m - 2), tile(2 * m - 1)])
                samples_sum(Idx(SDOWN + 3), [tile(6), tile(7)])

            def conv_rows():
                for q in range(6):
                    tr_unit([(P * a, tails[:, 4 * q + a, :]) for a in range(4) if 4 * q + a < NF])

            pe.wait_ge(const_ok, 5)
            pe.wait_ge(row_in, 12 * 16)
            tr_unit([(0, rows1), (NC1, rows2[0]), (NC1 + NCC, rows2[1])])
            for l in range(2):
                tr_unit([(16 * f, prows[l][:, P * f:P * f + P]) for f in range(NF)])
            pe.wait_ge(x_in, 32)
            tr_unit([(NB * k, xs[:, P * k:P * k + P]) for k in range(KD)])
            for k in range(KD):
                tr_unit([(P * t, xtok[:, t, P * k:P * k + P]) for t in range(TT)])
            pe.wait_ge(mem_in, 16)
            for k in range(0, KD, 2):
                tr_unit([(256 * a + P * t, memtok[:, t, P * (k + a):P * (k + a) + P]) for a in range(2) for t in range(2)])
            norm_sums(KD, NMEM)

            for l in range(2):
                norm_sums(KD)
                pe.wait_ge(memh_ok, l + 1)
                for p in range(4):
                    in_panel(l, p)
                    for t in range(MT):
                        free(t)
                        for k in range(KD):
                            last = mm(PS[:, 2 * t, 0:PCOL], memH[:, k, P * t:P * t + P], wring[:, p % 2, k, :],
                                      start=(k == 0), stop=(k == KD - 1))
                        last.then_inc(dense_done, 1)
                        pl.group += 1
                pe.wait_ge(mk_ok, l + 1)
                for a in range(2):
                    tr_unit([(256 * c + P * t, memK[:, t, P * (2 * a + c):P * (2 * a + c) + P]) for c in range(2) for t in range(2)])
                pe.wait_ge(applied, APPLIED[l][0])
                for p in range(6):
                    fm_panel(l, 4 + p, hT)
                if l == 0:
                    pe.wait_ge(gd_in, 32)
                    pe.wait_ge(rstd_ok, pl.norm)
                    for k in range(KD):
                        for c in range(2):
                            last = mm(PS[0:GR, NORM_BANK + c, 0:HALF], wgd[:, k, :], hT[:, k, HALF * c:HALF * c + HALF],
                                      start=(k == 0), stop=(k == KD - 1))
                    last.then_inc(gd_done, 1)
                for p in range(2):
                    in_panel(l, 10 + p)
                    for t in range(TT + 1):
                        n = P if t < TT else NB
                        free(pl.group % 2)
                        for k in range(KD):
                            last = mm(PS[0:n, 2 * (pl.group % 2), 0:PCOL], hT[:, k, P * t:P * t + n], wring[:, p, k, :],
                                      start=(k == 0), stop=(k == KD - 1))
                        last.then_inc(dense_done, 1)
                        pl.group += 1
                        q = 5 * p + t
                        if l == 0 and q < 2:
                            gates(q)
                        if q in v_norms(l):
                            if l == 0 and q == v_norms(0)[0]:
                                pe.wait_ge(gu_read, 2)
                            norm_sums(1)
                for par in range(2):
                    pe.wait_ge(dense_free[par], pl.group // 2)
                if l == 0:
                    gla()
                    for h in range(4):
                        norm_sums(1, h=h)
                else:
                    sb_prompt()
                    pe.wait_ge(sbo_out, 4)
                mem_prompt(l)
                pe.wait_ge(po_out, 4 * l + 4)
                mem_samples(l)
                if l == 0:
                    tail(0, FULL)
                    continue
                wait_tr(pe, pl.tr)
                out = [lambda fs, p=p: fm_panel(1, 12 + p, mix, PROMPT, fs) for p in range(4)]
                block(Idx(1), out, True, True, False)
                pe.wait_ge(dense_free[1], pl.group // 2)
                norm_sums(KD, SEQ, bank=2)
                pe.wait_ge(rstd_ok, pl.norm)
                ups = lambda f0: [lambda fs, p=p: up_panel(1, Idx(f0.c + p, f0.i, f0.per), PROMPT, fs, first=(f0.i is None and p == 0))
                                  for p in range(4)]
                block(Idx(2), ups(Idx(0)), True, True, True)
                with pe.Fori(0, 4) as i:
                    block(Idx(3, i, 1), ups(Idx(4, i, 4)), True, True, True)
                for f in (20, 21):
                    up_panel(1, Idx(f), PROMPT)
                pl.group += 2 * NF
                pe.wait_ge(dense_free[1], pl.group // 2)
                for b in range(7, 10):
                    downs = [lambda fs, u=4 * (b - 7) + p: down_panel(1, u, PROMPT, None, fs) for p in range(4)]
                    block(Idx(b), downs, b < NB, b < NB + 1, True)
                pl.group += 8
                for par in range(2):
                    pe.wait_ge(dense_free[par], pl.group // 2)
                for t in range(TT):
                    for q in range(2):
                        tr_unit([(P * a, xT[:, 4 * q + a, P * t:P * t + P]) for a in range(4)])
                pe.wait_ge(bs_out, 3)
                samples_tail()
            pe.wait_ge(s_x_ok, 2)
            for q in range(2):
                tr_unit([(P * a, xT[:, 4 * q + a, SEQ:TOK]) for a in range(4)])

        def bank(n, rows, cols):
            return PS[0:rows, TR_BANK + n % 2, 0:cols]

        def units_setup():
            yield lambda n: (cv[:, 0:NC1 + 2 * NCC], bank(n, P, NC1 + 2 * NCC))
            for l in range(2):
                yield lambda n, l=l: (prev[:, l], bank(n, P, 16 * NF).rearrange("p (f x) -> p f x", x=16))
            yield lambda n: (xT[:, :, SEQ:TOK], bank(n, P, NB * KD).rearrange("p (k b) -> p k b", b=NB))
            for k in range(KD):
                yield lambda n, k=k: (xT[:, k, 0:SEQ], bank(n, P, SEQ))
            for q in range(4):
                yield lambda n, q=q: (memR[:, 2 * q:2 * q + 2, :], bank(n, P, 512).rearrange("p (a m) -> p a m", a=2))

        def units_memk():
            for a in range(2):
                yield lambda n, a=a: (memKT[:, 2 * a:2 * a + 2, :], bank(n, P, 512).rearrange("p (a m) -> p a m", a=2))

        def units_gla():
            for j in range(2):
                yield lambda n, j=j: (keT[:, j], bank(n, P, 512).rearrange("p (t m) -> p t m", t=TT))
            for j in range(2):
                yield lambda n, j=j: (ksT[:, P * j:P * j + P], bank(n, NB, P))

        def units_sb():
            for t in range(TT):
                yield lambda n, t=t: (ktok[:, t, :], bank(n, P, 512))
            for a in range(2):
                yield lambda n, a=a: (kstok[:, 256 * a:256 * a + 256], bank(n, NB, 256))

        def units_probs(h):
            for mt in range(MT):
                yield lambda n, mt=mt: (pT[h % 2][:, mt, :], bank(n, P, SEQ))

        def units_tail():
            for q in range(6):
                w = 512 if q < 5 else 256
                yield lambda n, q=q, w=w: (tailr[:, 512 * q:512 * q + w], bank(n, 2 + NB, w))

        def units_y():
            for t in range(TT):
                for q in range(2):
                    yield lambda n, t=t, q=q: (ytok[:, t, 512 * q:512 * q + 512], bank(n, P, 512))

        def units_ys():
            for q in range(2):
                yield lambda n, q=q: (ystok[:, 512 * q:512 * q + 512], bank(n, NB, 512))

        s_mx = lambda p: st[:, 8 * p:8 * p + 4]
        s_sum = lambda p: st[:, 16 + 8 * p:20 + 8 * p]
        s_kn = st[:, 32:40]
        s_smx, s_ssum = st[0:32, 48:49], st[0:32, 49:50]
        MSC = float(P) ** -0.5
        one = ones[:, 0:1]

        def norm_sources(l, what, cols=FULL):
            if what == "mem":
                return [memR[:, k, :] for k in range(KD)], D, None, None, NMEM
            if what == "mix":
                return [xT[:, k, :] for k in range(KD)], D, [c_mix(l, k) for k in range(KD)], [hT[:, k, :] for k in range(KD)], TOK
            if what == "ffn":
                return ([tile_cols(xT, k, cols) for k in range(KD)], D, [c_ffn(l, k) for k in range(KD)],
                        [hS[:, k, 0:NB] for k in range(KD)], cols[1])
            if what == "gla":
                return [mix[:, l, :]], GDV, [c_on], [mix[:, l, :]], TOK
            return [zT[:, 8 + what, :]], P, [c_qn(l)], [zT[:, 8 + what, :]], TOK

        @block.scalar
        def _(act):
            pl = Place()
            steps = Steps(act, act_step)
            fn = nc.scalar.activation

            def units(which):
                for u in which:
                    if pl.tr % 2 == 0:
                        act.wait_ge(tr_done, pl.tr + 1)
                        dst, src = u(pl.tr)
                        fn(dst, src, ACT.Copy).then_inc(tr_out[0], 1)
                    pl.tr += 1

            def norm(l, what, ready=None, cols=FULL):
                srcs, n, _, _, w = norm_sources(l, what, cols)
                for k, src in enumerate(srcs):
                    if ready:
                        ready(k)
                    if pl.sq >= 2:
                        act.wait_ge(sq_used, pl.sq - 1)
                    fn(sq[:, pl.sq % 2, 0:w], src, ACT.Square).then_inc(sq_ok, 1)
                    pl.sq += 1
                act.wait_ge(sq_used, pl.sq)
                if pl.norm >= 2:
                    act.wait_ge(applied, pl.applied[-2])
                r = rstd[:, pl.norm % 2, 0:w]
                bank = 2 if cols == PROMPT else NORM_BANK
                steps.link(fn(r.rearrange("p (c n) -> p c n", c=2), PS[:, bank:bank + 2, 0:w // 2], ACT.Ln,
                              scale=1.0 / n, bias=eps[:, 0:1]))
                fn(r, r, ACT.Exp, scale=-0.5).then_inc(rstd_ok, 1)
                pl.norm += 1
                pl.applied.append(pl.applied[-1] + len(srcs))

            pl.applied = [0]

            def gla_norms():
                act.wait_ge(applied, pl.applied[-1])
                views = [gla_rstd[h].rearrange("p (c n) -> p c n", c=2) for h in range(4)]
                for h in range(4):
                    act.wait_ge(sq_used, pl.sq - 1)
                    fn(sq[:, pl.sq % 2, :], mix[:, h, :], ACT.Square).then_inc(sq_ok, 1)
                    pl.sq += 1
                    if h:
                        act.wait_ge(sq_used, pl.sq - 1)
                        fn(views[h - 1], PS[:, NORM_BANK:NORM_BANK + 2, 0:HALF], ACT.Ln, scale=1.0 / GDV, bias=eps[:, 0:1]).then_inc(rln_ok, 1)
                act.wait_ge(sq_used, pl.sq)
                fn(views[3], PS[:, NORM_BANK:NORM_BANK + 2, 0:HALF], ACT.Ln, scale=1.0 / GDV, bias=eps[:, 0:1]).then_inc(rln_ok, 1)
                for h in range(4):
                    act.wait_ge(rln_ok, h + 1)
                    fn(gla_rstd[h], gla_rstd[h], ACT.Exp, scale=-0.5).then_inc(rstd_ok, 1)
                    pl.norm += 1
                    pl.applied.append(pl.applied[-1] + 1)

            def split_h(l, cols):
                for k in range(KD):
                    act.wait_ge(htmp_ok, KD * l + k + 1)
                    fn(tile_cols(h_hi, k, cols), htmp[k % 6][:, 0:cols[1]], ACT.Copy).then_inc(hhi_ok, 1)

            def split_w(l, f, m):
                if m == 0:
                    c = w_ready(l, UP0 + f.c)
                    act.wait_ge(w_in[f.c % 2], c if f.i is None else f.i * (16 * f.per) + c)
                n = 2 * NF * l + m
                for q in range(2):
                    if l or f.c or f.i is not None or m:
                        if q == 0:
                            act.wait_ge(half_done, f.at(2, n))
                        else:
                            act.wait_ge(dense_done, f.at(2, up_groups(l, FULL) + m))
                    fn(w_parts[:, q, 0], wring[:, f.c % 2, 4 * q:4 * q + 4, P * m:P * m + P], ACT.Copy).then_inc(whi_ok, 1)


            def gla_decays():
                for j in range(2):
                    act.wait_ge(gu_read, j + 1)
                    steps.link(fn(la[:, j], lb[:, j], ACT.Abs))
                    steps.link(fn(la[:, j], la[:, j], ACT.Exp, scale=-1.0))
                    fn(la[:, j], la[:, j], ACT.Ln, bias=one).then_inc(ln_ok, 1)
                act.wait_ge(lb_ok, 1)
                fn(eb, lb, ACT.Exp, scale=1.0 / 16).then_inc(eb_ok, 1)
                fn(la, lb, ACT.Exp, scale=-1.0 / 16).then_inc(eb_ok, 1)
                act.wait_ge(ked_ok, 1)
                fn(ke[:, :, 0:SEQ], ke[:, :, 0:SEQ], ACT.Exp, scale=1.0 / 16).then_inc(kee_ok, 1)

            def gla():
                for h in range(4):
                    act.wait_ge(att_done, h + 1)
                    fn(att[:, h], PS[:, h, :].rearrange("p (t n) -> p t n", t=TT), ACT.Copy).then_inc(att_out, 1)
                units(units_gla())
                act.wait_ge(qk_ok, 1)
                fn(scr[:, 0:4 * TOK].rearrange("p (h n) -> p h n", h=4), zT[:, 4:8, :], ACT.Silu).then_inc(eg_ok, 1)
                for h in range(4):
                    act.wait_ge(o_done, h + 1)
                    steps.link(fn(mix[:, h, 0:SEQ], PS[:, h, :], ACT.Copy))
                act.wait_ge(os_done, 1)
                for a in range(2):
                    steps.link(fn(mix[:, a:4:2, SEQ:TOK], PS[:, NORM_BANK + a, 0:16].rearrange("p (j b) -> p j b", j=2), ACT.Copy))
                gla_norms()

            def softplus_prompt(h):
                act.wait_ge(z_read, h + 1)
                if h >= 2:
                    act.wait_ge(sbo_done, h - 1)
                x = sbt[h % 2]
                steps.link(fn(x, sbz[h % 2], ACT.Abs))
                steps.link(fn(x, x, ACT.Exp, scale=-1.0))
                fn(x, x, ACT.Ln, bias=one).then_inc(zl_ok, 1)

            def sb_prompt():
                softplus_prompt(0)
                softplus_prompt(1)
                for h in range(SBH):
                    act.wait_ge(zr_ok, h + 1)
                    fn(sbt[h % 2], sbz[h % 2], ACT.Exp).then_inc(wr_ok, 1)
                    if h + 2 < SBH:
                        softplus_prompt(h + 2)
                    if h % 2:
                        act.wait_ge(sbo_done, h + 1)
                        fn(mix[:, h // 2, 0:SEQ], PS[:, 3, :], ACT.Copy).then_inc(sbo_out, 1)

            def q_column(b, first=False):
                if not first:
                    act.wait_ge(bq_done, b.at(1, 0))
                fn(qcol[:, :], zT[:, 0:4, b.one(SEQ)].rearrange("p j a -> p (j a)"), ACT.Copy).then_inc(qcol_ok, 1)

            def softplus(b):
                act.wait_ge(bz_ok, b.at(1, 1))
                steps.link(fn(lg, zb, ACT.Abs))
                steps.link(fn(lg, lg, ACT.Exp, scale=-1.0))
                fn(lg, lg, ACT.Ln, bias=one).then_inc(bl_ok, 1)

            def weights(b):
                act.wait_ge(bzr_ok, b.at(1, 1))
                fn(wsb.rearrange("p g (a h) -> p h (g a)", h=SBH), zb, ACT.Exp).then_inc(bw_ok, 1)

            def rows(b):
                act.wait_ge(v_used, b.at(8, MEM + KGROUPS))
                fn(om, PS[:, 6, :], ACT.Copy).then_inc(bom_ok, 1)

            def block(b, panels, k, v, v2):
                s1, s2 = Idx(b.c - 1, b.i, b.per), Idx(b.c - 2, b.i, b.per)
                if v:
                    softplus(s1)
                for p in range(4):
                    panels[p]()
                    if p == 0:
                        if v2:
                            rows(s2)
                        if v:
                            weights(s1)
                    if p == 1 and k == 2:
                        q_column(Idx(b.c + 1, b.i, b.per))

            def up_evac(l, f, p, cols, more=True):
                g0, w = up_groups(l, cols), cols[1]
                split_w(l, f, 1)
                act.wait_ge(dense_done, f.at(2, g0 + 1))
                fn(as_pair(ext[p][:, 2:2 + w], cols), pair(0, cols), ACT.Copy).then_inc(ga_ok, 1)
                fn(as_pair(acc[p][:, 0:w], cols), pair(0, cols), ACT.Identity, scale=c_conv(l, 2, f), bias=c_conv(l, 3, f)).then_inc(dense_free[0], 1)
                if more:
                    split_w(l, Idx(f.c + 1, f.i, f.per), 0)
                act.wait_ge(gc_ok, f.at(1, up_count(l, cols) + 1))
                fn(sg[p][:, 0:w], acc[p][:, 0:w], ACT.Silu).then_inc(ge_ok, 1)

            def x_from(n):
                return (lambda k: act.wait_ge(dense_free[k % 2], (n + k) // 2 + 1)) if n is not None else None

            def mem_samples(l):
                act.wait_ge(tr_done, pl.tr + 1)
                fn(s32[:, :], bank(pl.tr, 32, NMEM), ACT.Copy).then_inc(tr_out[0], 1)
                pl.tr += 2
                act.wait_ge(smx_ok, l + 1)
                fn(s32[:, :], s32[:, :], ACT.Exp, scale=MSC, bias=s_smx, accum_out=s_ssum).then_inc(sme_ok, 1)
                for half in range(2):
                    act.wait_ge(v_used, 4 * l + 2 * half + 2)
                    fn(om2[:, half, :], PS[:, NORM_BANK + half, :], ACT.Copy).then_inc(mo_ok, 1)
                act.wait_ge(so_done, l + 1)
                fn(mix[:, 4:8, SEQ:TOK], PS[:, 0, 0:4 * NB].rearrange("p (h b) -> p h b", h=4), ACT.Copy).then_inc(so_out, 1)

            def tail(l, cols):
                norm(l, "ffn", x_from(up_groups(l, cols) - 8), cols)
                act.wait_ge(mem_st, 32 * (l + 1))
                split_w(l, Idx(0), 0)
                split_h(l, cols)
                with act.Fori(0, NF // 2 - 1) as i:
                    for p in range(2):
                        up_evac(l, Idx(p, i, 2), p, cols)
                for p in range(2):
                    up_evac(l, Idx(NF - 2 + p), p, cols, more=(p == 0))
                units(units_tail())

            def samples_rows(g):
                act.wait_ge(s_read, s_group_panels(g.c) if g.i is None else g.at(1, 1))
                if g.i is not None or g.c >= 2:
                    act.wait_ge(s_sum_done, g.at(1, -1))
                fn(rowsS[:, g.c % 2, :], PS[:, 2 * (g.c % 2), 0:PCOL], ACT.Copy).then_inc(s_rows_ok, 1)

            def samples_tail():
                for g in range(4):
                    samples_rows(Idx(g))
                norm(1, "ffn", lambda k: act.wait_ge(s_x_ok, 1), SAMPLES)
                with act.Fori(0, NF // 2) as i:
                    for p in range(2):
                        samples_rows(Idx(4 + p, i, 2))
                act.wait_ge(s_acc_ok, 1)
                fn(sgS, accS, ACT.Silu).then_inc(s_silu_ok, 1)
                samples_rows(Idx(SDOWN))
                units(units_tail())
                for m in range(1, 4):
                    samples_rows(Idx(SDOWN + m))

            units(units_setup())
            wait_tr(act, 16)
            norm(0, "mem")
            for l in range(2):
                g0 = GROUPS * l
                half = GROUPS // 2
                norm(l, "mix", x_from(g0 - 8 if l else None))
                if l:
                    act.wait_ge(mem_st, 32)
                for p in range(4):
                    for t in range(MT):
                        act.wait_ge(dense_done, g0 + 2 * p + t + 1)
                        dst = memK if p < 2 else memV
                        fn(dst[:, t, PCOL * (p % 2):PCOL * (p % 2) + PCOL], PS[:, 2 * t, 0:PCOL], ACT.Copy).then_inc(dense_free[t], 1)
                act.wait_ge(kss_ok, l + 1)
                steps.link(fn(s_kn, s_kn, ACT.Ln, scale=1.0 / P, bias=eps[:, 0:1]))
                fn(s_kn, s_kn, ACT.Exp, scale=-0.5).then_inc(kr_ok, 1)
                units(units_memk())
                for j in range(12):
                    act.wait_ge(dense_done, g0 + 8 + j + 1)
                    fn(zT[:, j, :].rearrange("p (c n) -> p c n", c=2), PS[:, 2 * (j % 2):2 * (j % 2) + 2, 0:HALF], ACT.Copy).then_inc(dense_free[j % 2], 1)
                for par in range(2):
                    act.wait_ge(dense_free[par], (g0 + 20) // 2)
                if l == 0:
                    act.wait_ge(gd_done, 1)
                    fn(gdT[:, :].rearrange("p (c n) -> p c n", c=2), PS[0:GR, NORM_BANK:NORM_BANK + 2, 0:HALF], ACT.Copy).then_inc(gd_ok, 1)
                    gla_decays()
                for h in range(4):
                    norm(l, h)
                if l == 0:
                    gla()
                else:
                    q_column(Idx(0), first=True)
                    units(units_sb())
                    sb_prompt()
                    q_column(Idx(1))
                for h in range(4 + 1):
                    if h < 4:
                        act.wait_ge(mx_ok, 4 * l + h + 1)
                        for t in range(TT):
                            last = fn(pb[h % 2][:, t, :], PS[:, 2 * (h % 2) + t // 2, 256 * (t % 2):256 * (t % 2) + 256], ACT.Exp,
                                      scale=MSC, bias=s_mx(h % 2)[:, t:t + 1], accum_out=s_sum(h % 2)[:, t:t + 1])
                        last.then_inc(pe_ok, 1)
                    if h >= 1:
                        a = h - 1
                        units(units_probs(a))
                        act.wait_ge(po_done, 4 * l + a + 1)
                        fn(mix[:, 4 + a, 0:SEQ], PS[:, 2 * (a % 2), :], ACT.Copy).then_inc(po_out, 1)
                mem_samples(l)
                if l == 0:
                    tail(0, FULL)
                    continue
                none = [lambda: None] * 4
                block(Idx(1), none, 2, True, False)
                norm(1, "ffn", x_from(up_groups(1, PROMPT) - 8), PROMPT)
                act.wait_ge(mem_st, 64)
                split_w(1, Idx(0), 0)
                split_h(1, PROMPT)
                ups = lambda f0: [lambda p=p: up_evac(1, Idx(f0.c + p, f0.i, f0.per), p % 2, PROMPT) for p in range(4)]
                block(Idx(2), ups(Idx(0)), 2, True, True)
                with act.Fori(0, 4) as i:
                    steps.enter(i, 2)
                    block(Idx(3, i, 1), ups(Idx(4, i, 4)), 2, True, True)
                    steps.leave(4)
                for f in (20, 21):
                    up_evac(1, Idx(f), f % 2, PROMPT, more=(f == 20))
                for b in range(7, 10):
                    block(Idx(b), none, 0, b < NB + 1, True)
                act.wait_ge(bf_done, NB)
                o = PS[:, 7, 0:64].rearrange("p (j b c) -> p j b c", j=4, c=2)
                for c in range(2):
                    fn(mixS[64 * c:64 * c + 64, 0:4, 0:NB], o[64 * c:64 * c + 64, :, :, c], ACT.Copy).then_inc(bs_out, 1)
                act.wait_ge(so_out, 2)
                fn(mixS[:, 4:8, 0:NB], mix[:, 4:8, SEQ:TOK], ACT.Copy).then_inc(bs_out, 1)
                units(units_y())
                samples_tail()
            units(units_ys())

        @block.vector
        def _(dve):
            pl = Place()
            steps = Steps(dve, dve_step)
            link = steps.link
            v = nc.vector
            stt, tt, ts = v.scalar_tensor_tensor, v.tensor_tensor, v.tensor_scalar

            def units(which):
                for u in which:
                    if pl.tr % 2 == 1:
                        dve.wait_ge(tr_done, pl.tr + 1)
                        dst, src = u(pl.tr)
                        v.tensor_copy(dst, src).then_inc(tr_out[1], 1)
                    pl.tr += 1

            def norm_split(l, cols):
                srcs, _, gains, _, w = norm_sources(l, "ffn", cols)
                dve.wait_ge(rstd_ok, pl.norm + 1)
                r = rstd[:, pl.norm % 2, 0:w]
                dve.wait_ge(mem_st, 32 * (l + 1))
                dve.wait_ge(memr_moved, 1)
                base = APPLIED[l][2] - KD

                def whole(k):
                    if k >= 6:
                        dve.wait_ge(applied, base + k - 5)
                    stt(htmp[k % 6][:, 0:w], srcs[k], gains[k], r, ALU.mult, ALU.mult).then_inc(htmp_ok, 1)

                for k in range(6):
                    whole(k)
                for k in range(KD):
                    dve.wait_ge(hhi_ok, KD * l + k + 1)
                    tt(tile_cols(h_lo, k, cols), htmp[k % 6][:, 0:w], tile_cols(h_hi, k, cols), ALU.subtract).then_inc(applied, 1)
                    if k in (1, 2):
                        whole(k + 5)
                dve.wait_ge(applied, base + KD)
                pl.norm += 1

            def norm(l, what, cols=FULL):
                srcs, _, gains, outs, w = norm_sources(l, what, cols)
                dve.wait_ge(rstd_ok, pl.norm + 1)
                r = gla_rstd[l] if what == "gla" else rstd[:, pl.norm % 2, 0:w]
                for k, src in enumerate(srcs):
                    if gains is None:
                        tt(src, src, r, ALU.mult).then_inc(applied, 1)
                    else:
                        stt(outs[k], src, gains[k], r, ALU.mult, ALU.mult).then_inc(applied, 1)
                pl.norm += 1

            ch = lambda a: a[:, :, 0:SEQ].rearrange("p j (n c) -> p j n c", c=CH)

            def gate(j):
                dve.wait_ge(gu_done, j + 1)
                ts(lb[:, j].rearrange("p (c n) -> p c n", c=2), PS[:, NORM_BANK:NORM_BANK + 2, 0:HALF], c_bg(j), None,
                   ALU.add).then_inc(gu_read, 1)

            def log_decay(j):
                dve.wait_ge(gu_read, j + 1)
                dve.wait_ge(ln_ok, j + 1)
                link(stt(la[:, j], lb[:, j], 0.0, la[:, j], ALU.min, ALU.subtract))
                v.tensor_tensor_scan(lb[:, j, 0:SEQ], keep[:, :], la[:, j, 0:SEQ], 0.0, ALU.mult, ALU.add)
                link(v.tensor_copy(lb[:, j, SEQ:TOK], la[:, j, SEQ:TOK]))
                if j:
                    v.tensor_copy(st[:, 0:1], lb[:, 0, 0:1]).then_inc(lb_ok, 1)
                    tt(ch(ke), ch(lb)[:, :, :, CH - 1:CH].to_broadcast((P, 2, NCH, CH)), ch(lb), ALU.subtract).then_inc(ked_ok, 1)

            def decayed(j):
                if j == 0:
                    dve.wait_ge(kee_ok, 1)
                    tt(ke[:, :, 0:SEQ], ke[:, :, 0:SEQ], zT[:, 2:4, 0:SEQ], ALU.mult).then_inc(ke_ok, 1)
                    return
                dve.wait_ge(ke_ok, 1)
                dve.wait_ge(eb_ok, 2)
                tt(zT[:, 2:4, 0:SEQ], zT[:, 2:4, 0:SEQ], la[:, :, 0:SEQ], ALU.mult)
                ts(zT[:, 0:2, SEQ:TOK], zT[:, 0:2, SEQ:TOK], GDK ** -0.5, None, ALU.mult)
                stt(zT[:, 0:2, 0:SEQ], zT[:, 0:2, 0:SEQ], GDK ** -0.5, eb[:, :, 0:SEQ], ALU.mult, ALU.mult).then_inc(qk_ok, 1)

            def gla():
                units(units_gla())
                wait_tr(dve, pl.tr)
                for b in range(NB):
                    last = ts(kdiag[:, b, :], ksT, ident[0:NB, b:b + 1], None, ALU.mult)
                last.then_inc(kdiag_ok, 1)
                dve.wait_ge(kv_done, 1)
                dve.wait_ge(ss_in, 64)
                for n in range(NCH):
                    kv = PS[:, n % 4, 256 * (n // 4):256 * (n // 4) + 256].rearrange("p (j v) -> p j v", j=2)
                    if n == 0:
                        link(v.tensor_copy(S[:, 0], kv))
                        continue
                    for j in range(2):
                        last = stt(S[:, n, j, :], S[:, n - 1, j, :], eb[:, j, CH * n + CH - 1:CH * n + CH], kv[:, j, :], ALU.mult, ALU.add)
                        if n < NCH - 1:
                            c = steps.mark(last)
                    if n < NCH - 1:
                        steps.wait(c)
                last.then_inc(s_ok, 1)
                dve.wait_ge(outer_done, 1)
                for b in range(NB):
                    for j in range(2):
                        last = stt(SS[:, b, j, :], SS[:, b, j, :], eb[:, j, SEQ + b:SEQ + b + 1],
                                   PS[:, b // 2, 256 * (b % 2) + P * j:256 * (b % 2) + P * j + P], ALU.mult, ALU.add)
                last.then_inc(ss_ok, 1)
                eg = scr[:, 0:4 * TOK].rearrange("p (h n) -> p h n", h=4)
                dve.wait_ge(eg_ok, 1)
                for h in range(4):
                    norm(h, "gla")
                    dve.wait_ge(applied, APPLIED[0][0] + 4 + h + 1)
                    link(tt(mix[:, h, :], mix[:, h, :], eg[:, h, :], ALU.mult))

            def prompt_z(h, between=None):
                dve.wait_ge(z_done, h + 1)
                if h >= 2:
                    dve.wait_ge(wr_ok, h - 1)
                ts(sbz[h % 2], PS[:, 0:3, :].rearrange("p a b -> p (a b)")[:, 0:SBW], SBD ** -0.5, sbb[:, h:h + 1], ALU.mult, ALU.add).then_inc(z_read, 1)
                dve.wait_ge(z_read, h + 1)
                if between:
                    between()
                dve.wait_ge(zl_ok, h + 1)
                stt(sbt[h % 2], sbz[h % 2], 0.0, sbt[h % 2], ALU.max, ALU.add).then_inc(spr_ok, 1)

            def sb_prompt():
                prompt_z(0)
                prompt_z(1)
                for h in range(SBH):
                    dve.wait_ge(r_done, h + 1)
                    tt(sbz[h % 2], sbz[h % 2], PS[:, 4:7, :].rearrange("p a b -> p (a b)")[:, 0:SBW], ALU.subtract).then_inc(zr_ok, 1)
                    k0 = lambda g=h: k_group(Idx(0), g)
                    if h + 2 < SBH:
                        prompt_z(h + 2, k0)
                    else:
                        k0()

            slots = {}

            def k_group(b, g):
                if g == 0:
                    dve.wait_ge(bq_done, b.at(1, 1))
                n = k_before(b)
                dve.wait_ge(k_in[g % 2], n.at(32, 64 * (g // 2 + 1)))
                q, z = (PS[:, 7:8, :], zs0) if b.i is None and b.c == 0 else (PS[:, 4:5, :], zs)
                made = []
                for c in range(2):
                    if g:
                        if c == 0:
                            steps.wait(slots["reduced"])
                        else:
                            dve.wait_ge(k_used, n.at(1, g))
                    made.append(steps.mark(tt(prod[:, 2 * c:2 * c + 2, :], kring[:, g % 2, 2 * c:2 * c + 2, :],
                                              q.to_broadcast((P, 2, 512)), ALU.mult)))
                for c in range(2):
                    steps.wait(made[c])
                    o = 4 * g + 2 * c
                    last = v.tensor_reduce(z[:, :, o:o + 2].rearrange("p h g -> p g h"),
                                           prod[:, 2 * c:2 * c + 2, :].rearrange("p a (h d) -> p a h d", h=SBH), AX.X, ALU.add)
                    if c == 0:
                        slots["reduced"] = steps.mark(last)
                    else:
                        last.then_inc(k_used, 1)

            flat = lambda a: a.rearrange("p h g -> p (h g)")

            def softplus(b):
                dve.wait_ge(k_used, k_before(b).at(1, KGROUPS))
                stt(zb, zs0 if b.i is None and b.c == 0 else zs, SBD ** -0.5, sbb[:, :].rearrange("p (h a) -> p h a", a=1).to_broadcast((P, SBH, PAGES)),
                    ALU.mult, ALU.add).then_inc(bz_ok, 1)
                dve.wait_ge(bz_ok, b.at(1, 1))
                dve.wait_ge(bl_ok, b.at(1, 1))
                link(stt(sp_s, zb, 0.0, lg, ALU.max, ALU.add))
                link(v.tensor_tensor_scan(flat(cs), flat(keepp[:, :, :]), flat(sp_s), 0.0, ALU.mult, ALU.add))
                tt(cs, cs, sp_s, ALU.subtract).then_inc(bcs_ok, 1)

            def exponent(b):
                dve.wait_ge(br_done, b.at(1, 1))
                tt(flat(zb), flat(zb), PS[:, 7, 64:320], ALU.subtract).then_inc(bzr_ok, 1)

            def block(b, panels, k, v):
                s1 = Idx(b.c - 1, b.i, b.per)
                if v:
                    softplus(s1)
                for p in range(4):
                    if k:
                        k_group(b, 2 * p)
                        k_group(b, 2 * p + 1)
                    panels[p]()
                    if p == 0 and v:
                        exponent(s1)

            def add_group(g, k, cols):
                dve.wait_ge(dense_done, g + 1)
                x = as_pair(tile_cols(xT, k, cols), cols)
                tt(x, x, pair(k % 2, cols), ALU.add).then_inc(dense_free[k % 2], 1)

            def add_to_residual(g, cols):
                for k in range(KD):
                    add_group(g + k, k, cols)

            def conv_all(l, t):
                c = NC1 + l * NCC + t * NF
                return cv[:, c:c + NF].rearrange("p (f a) -> p f a", a=1).to_broadcast((P, NF, NB))

            def ffn_start(l, cols):
                if cols != SAMPLES:
                    for p in range(2):
                        v.memset(ext[p][:, 0:2], 0.0)
                if cols == PROMPT:
                    return
                tmp = scr[:, 3200:3200 + NF * NB].rearrange("p (f b) -> p f b", b=NB)
                taps = [conv_all(l, t) for t in range(2)]
                pv = prev[:, l].rearrange("p f (b t) -> p f b t", t=2)
                link(tt(tmp, pv[:, :, :, 0], taps[0], ALU.mult))
                link(tt(pre[:, :, :], pv[:, :, :, 1], taps[1], ALU.mult))
                link(tt(pre[:, :, :], pre[:, :, :], tmp, ALU.add))

            def up_evac(l, f, p, cols):
                g0, w = up_groups(l, cols), cols[1]
                done = f.at(1, up_count(l, cols) + 1)
                dve.wait_ge(ga_ok, done)
                dve.wait_ge(dense_free[0], f.at(1, g0 // 2 + 1))
                a = acc[p][:, 0:w]
                own = pre[:, f.one(), :].rearrange("p a b -> p (a b)")
                link(stt(a[:, 0:SEQ], ext[p][:, 1:1 + SEQ], c_conv(l, 1, f), a[:, 0:SEQ], ALU.mult, ALU.add))
                if w == TOK:
                    tt(a[:, SEQ:TOK], a[:, SEQ:TOK], own, ALU.add)
                v.tensor_copy(tails[:, f.one(), 0:w - SEQ + 2].rearrange("p a b -> p (a b)"), ext[p][:, SEQ:2 + w])
                stt(a[:, 0:SEQ], ext[p][:, 0:SEQ], c_conv(l, 0, f), a[:, 0:SEQ], ALU.mult, ALU.add).then_inc(gc_ok, 1)
                dve.wait_ge(ge_ok, done)
                dve.wait_ge(dense_done, f.at(2, g0 + 2))
                tt(as_pair(big[:, f.one(), cols[0]:cols[0] + w].rearrange("p a n -> p (a n)"), cols), as_pair(sg[p][:, 0:w], cols),
                   pair(1, cols), ALU.mult).then_inc(dense_free[1], 1)

            def mem_scores(l, bs):
                n0 = MEM_K[l]
                for b in bs:
                    n = n0 + b // 2
                    dve.wait_ge(qb_done, NB * l + b + 1)
                    dve.wait_ge(k_in[n % 2], 64 * (n // 2 + 1))
                    if b >= 2:
                        dve.wait_ge(k_used, n0 + b // 2) if b % 2 == 0 else steps.wait(slots["sum"])
                    pr = prod[:, 2 * (b % 2):2 * (b % 2) + 2, :]
                    tt(pr, kring[:, n % 2, 2 * (b % 2):2 * (b % 2) + 2, :],
                       PS[:, NORM_BANK + b % 2:NORM_BANK + b % 2 + 1, :].to_broadcast((P, 2, 512)), ALU.mult).then_inc(qb_read, 1)
                    dve.wait_ge(qb_read, NB * l + b + 1)
                    last = v.tensor_reduce(sm[:, :, b, :], pr.rearrange("p m (h d) -> p m h d", h=4), AX.X, ALU.add)
                    if b % 2:
                        last.then_inc(k_used, 1)
                    else:
                        slots["sum"] = steps.mark(last)

            def mem_samples(l):
                pl.tr += 1
                dve.wait_ge(tr_out[0], pl.tr // 2 + 1)
                link(v.tensor_reduce(s_smx, s32[:, :], AX.X, ALU.max))
                ts(s_smx, s_smx, -MSC, None, ALU.mult).then_inc(smx_ok, 1)
                dve.wait_ge(sme_ok, l + 1)
                link(v.reciprocal(s_ssum, s_ssum))
                ts(s32[:, :], s32[:, :], s_ssum, None, ALU.mult).then_inc(smn_ok, 1)
                dve.wait_ge(tr_done, pl.tr + 1)
                v.tensor_copy(ps[:, :, :], bank(pl.tr, P, 64).rearrange("p (m c) -> p m c", m=MT)).then_inc(tr_out[1], 1)
                pl.tr += 1

            def tail(l, cols):
                add_to_residual(up_groups(l, cols) - 8, cols)
                norm_split(l, cols)
                ffn_start(l, cols)
                with dve.Fori(0, NF // 2) as i:
                    steps.enter(i, 2)
                    for p in range(2):
                        up_evac(l, Idx(p, i, 2), p, cols)
                    steps.leave(NF // 2)
                units(units_tail())
                add_to_residual(up_groups(l, cols) + 2 * NF, cols)

            def samples_add(groups):
                dve.wait_ge(s_sum_done, groups)
                x = xT[:, :, SEQ:TOK]
                tt(x, x, PS[:, 1, 0:KD * NB].rearrange("p (k b) -> p k b", b=NB), ALU.add).then_inc(s_x_ok, 1)

            def samples_tail():
                ffn_start(1, SAMPLES)
                link(tt(pre[:, :, :], pre[:, :, :], conv_all(1, 3), ALU.add))
                samples_add(4)
                norm(1, "ffn", SAMPLES)
                dve.wait_ge(s_sum_done, 4 + NF)
                gates, vals = (PS[:, 3, 256 * c:256 * c + NF * NB].rearrange("p (f b) -> p f b", b=NB) for c in range(2))
                link(tt(accS, gates, conv_all(1, 2), ALU.mult))
                tt(accS, accS, pre[:, :, :], ALU.add).then_inc(s_acc_ok, 1)
                v.tensor_copy(tails[:, :, 2:2 + NB], gates).then_inc(s_tails_ok, 1)
                dve.wait_ge(s_silu_ok, 1)
                tt(actS[:, :, 0:NB], sgS, vals, ALU.mult).then_inc(s_act_ok, 1)
                units(units_tail())
                samples_add(S_GROUPS)

            units(units_setup())
            wait_tr(dve, 16)
            norm(0, "mem")
            for l in range(2):
                g0 = GROUPS * l
                dve.wait_ge(applied, 8)
                for k in range(KD):
                    last = ts(memH[:, k, :], (memR1 if l else memR)[:, k, :], c_mem(l, k), None, ALU.mult)
                last.then_inc(memh_ok, 1)
                if l:
                    dve.wait_ge(tail_st, 48)
                norm(l, "mix")
                for par in range(2):
                    dve.wait_ge(dense_free[par], g0 // 2 + 4)
                kk = memK[:, :, :].rearrange("p t (h d) -> p (t h) d", d=P)
                dve.wait_ge(bc_in, 32)
                link(tt(prod[:, 0:2, :], memK[:, :, :], memK[:, :, :], ALU.mult))
                v.tensor_reduce(s_kn, prod[:, 0:2, :].rearrange("p t (h d) -> p (t h) d", d=P), AX.X, ALU.add).then_inc(kss_ok, 1)
                dve.wait_ge(kr_ok, l + 1)
                link(tt(kk, kk, s_kn.rearrange("p (a b) -> p a b", b=1).to_broadcast((P, 8, P)), ALU.mult))
                tt(kk, kk, knorm[:, l:l + 1, :].to_broadcast((P, 8, P)), ALU.mult).then_inc(mk_ok, 1)
                units(units_memk())
                for q in range(10):
                    p, t = q // 5, q % 5
                    n = P if t < TT else NB
                    dve.wait_ge(dense_done, g0 + 20 + q + 1)
                    dst = vT[:, t, PCOL * p:PCOL * p + PCOL] if t < TT else vS[:, PCOL * p:PCOL * p + PCOL]
                    v.tensor_copy(dst, PS[0:n, 2 * (q % 2), 0:PCOL]).then_inc(dense_free[q % 2], 1)
                    if l == 0 and q < 6:
                        (gate, log_decay, decayed)[q // 2](q % 2)
                    for h in range(4):
                        if q == v_norms(l)[h] + (1 if l == 0 else 2):
                            norm(l, h)
                if l == 0:
                    gla()
                else:
                    units(units_sb())
                    sb_prompt()
                for h in range(4 + 1):
                    if h < 4:
                        dve.wait_ge(sc_done, 4 * l + h + 1)
                        m = s_mx(h % 2)
                        link(v.tensor_reduce(m, PS[:, 2 * (h % 2):2 * (h % 2) + 2, :].rearrange("p a (b m) -> p (a b) m", b=2), AX.X, ALU.max))
                        ts(m, m, -MSC, None, ALU.mult).then_inc(mx_ok, 1)
                    if h >= 1:
                        a = h - 1
                        dve.wait_ge(pe_ok, 4 * l + a + 1)
                        link(v.reciprocal(s_sum(a % 2), s_sum(a % 2)))
                        for t in range(TT):
                            last = ts(pb[a % 2][:, t, :], pb[a % 2][:, t, :], s_sum(a % 2)[:, t:t + 1], None, ALU.mult)
                        last.then_inc(pn_ok, 1)
                        units(units_probs(a))
                    if h < 4:
                        mem_scores(l, (2 * h, 2 * h + 1))
                mem_samples(l)
                if l == 0:
                    tail(0, FULL)
                    continue
                outs = [lambda p=p: [add_group(up_groups(1, PROMPT) - 8 + 2 * p + a, 2 * p + a, PROMPT) for a in range(2)] for p in range(4)]
                block(Idx(1), outs, True, True)
                dve.wait_ge(kt_st, 64)
                norm_split(1, PROMPT)
                ffn_start(1, PROMPT)
                ups = lambda f0: [lambda p=p: up_evac(1, Idx(f0.c + p, f0.i, f0.per), p % 2, PROMPT) for p in range(4)]
                block(Idx(2), ups(Idx(0)), True, True)
                with dve.Fori(0, 4) as i:
                    steps.enter(i, 3 * KGROUPS + 2 + 4)
                    block(Idx(3, i, 1), ups(Idx(4, i, 4)), True, True)
                    steps.leave(4)
                for f in (20, 21):
                    up_evac(1, Idx(f), f % 2, PROMPT)
                v.memset(padded, 0.0)

                def down_evac(u):
                    if u % 3 == 2:
                        for a in range(2):
                            k = 2 * (u // 3) + a
                            add_group(up_groups(1, PROMPT) + 2 * NF + k, k, PROMPT)

                for b in range(7, 10):
                    block(Idx(b), [lambda u=4 * (b - 7) + p: down_evac(u) for p in range(4)], b < NB, b < NB + 1)
                units(units_y())
                samples_tail()
            units(units_ys())


INS = ["x_prompt", "x_sample", "state_gla", "cache_sb_k", "cache_sb_v", "cache_mem_k", "cache_mem_v", "state_ffn_conv",
       "page_table", "mem_prompt", "norm_mix", "w_in_gla", "w_gate_up", "b_gate", "gla_out_norm", "w_in_sb", "sb_bias",
       "mem_norm", "w_mem_kv", "mem_q_norm", "mem_k_norm", "w_out", "norm_ffn", "w_ffn_up", "ffn_conv_w", "ffn_conv_b",
       "w_ffn_down"]
OUTS = [("y_p", (1, 512, 1024)), ("y_s", (8, 1, 1024)), ("gla_p", (1, 1, 4, 64, 128)), ("gla_s", (1, 8, 4, 64, 128)),
        ("sb_kp", (1, 1, 512, 8, 64)), ("sb_vp", (1, 1, 512, 8, 64)), ("sb_ks", (1, 8, 1, 8, 64)), ("sb_vs", (1, 8, 1, 8, 64)),
        ("mem_k", (2, 1, 256, 4, 128)), ("mem_v", (2, 1, 256, 4, 128)), ("conv_p", (2, 1, 2, 2816)), ("conv_s", (2, 8, 2, 2816))]


def kernel(**inputs):
    import concourse.bacc as bacc
    from concourse.bass_utils import run_bass_kernel_spmd

    nc = bacc.Bacc("TRN2", target_bir_lowering=False, num_devices=1)
    arrays, I, O = {}, {}, {}
    for name in INS:
        a = np.ascontiguousarray(inputs[name])
        arrays[name] = a
        I[name] = nc.dram_tensor(name, a.shape, mybir.dt.from_np(a.dtype), kind="ExternalInput").ap()
    for name, shape in OUTS:
        O[name] = nc.dram_tensor(name, shape, F32, kind="ExternalOutput").ap()
    build(nc, I, O)
    r = run_bass_kernel_spmd(nc, [arrays], core_ids=[0])
    return tuple(r.results[0][name] for name, _ in OUTS)
```
